# Optimizing a Trainium2 kernel written in Bass

```python
import math
import jax
import jax.numpy as jnp
from jax import lax
import numpy as np
import jax, jax.numpy as jnp

D_MODEL = 1024
BATCH = 1
SEQ = 256
DEPTH = 1

CHUNK = 64
EPS = 1e-6
NEG_BIG = -1e30
HG_HEADS = 8
HG_DK = 128
HG_DV = 128
HG_QK = HG_HEADS * HG_DK
HG_W = HG_HEADS * HG_DV
ML_HEADS = 4
ML_DQK = 128
ML_DV = 256
ML_CONV = 4
ML_QK = ML_HEADS * ML_DQK
ML_W = ML_HEADS * ML_DV
MB_HEADS = 16
MB_P = 64
MB_GROUPS = 4
MB_N = 128
MB_CONV = 4
MB_W = MB_HEADS * MB_P
MB_CONV_DIM = MB_W + 2 * MB_GROUPS * MB_N
D_FF = 2816
FFN_CONV = 3
N_BRANCH = 3
IN_SPLITS = (HG_QK, HG_QK, HG_W, HG_W,
             2 * ML_QK, ML_W, 2 * ML_HEADS, ML_W,
             MB_W, MB_CONV_DIM, MB_HEADS,
             N_BRANCH * D_MODEL)
N_IN = sum(IN_SPLITS)


def rmsnorm(x, g):
    xf = x.astype(jnp.float32)
    y = xf * lax.rsqrt(jnp.mean(xf * xf, axis=-1, keepdims=True) + EPS)
    return (y * g.astype(jnp.float32)).astype(x.dtype)

def causal_dwconv(u, w, b):
    K = w.shape[0]
    S = u.shape[1]
    up = jnp.pad(u, ((0, 0), (K - 1, 0), (0, 0)))
    return sum(up[:, k:k + S] * w[k] for k in range(K)) + b

def to_chunks(t):
    B, S = t.shape[:2]
    t = t.astype(jnp.float32).reshape(B, S // CHUNK, CHUNK, *t.shape[2:])
    return jnp.moveaxis(t, 1, 0)

def from_chunks(t):
    t = jnp.moveaxis(t, 0, 1)
    return t.reshape(t.shape[0], -1, *t.shape[3:])

def causal_tri():
    return jnp.tril(jnp.ones((CHUNK, CHUNK), dtype=bool))

def hgrn2_scan(q, log_f, v):
    B, _, H, dk = q.shape
    dv = v.shape[-1]
    k = -jnp.expm1(log_f)
    tri = causal_tri()

    def step(state, inp):
        qc, lfc, kc, vc = inp
        b = jnp.cumsum(lfc, axis=1)
        diff = b[:, :, None] - b[:, None, :]
        decay = jnp.exp(jnp.where(tri[None, :, :, None, None], diff, NEG_BIG))
        attn = jnp.einsum('bthd,btshd->bhts', qc, decay * kc[:, None])
        o_intra = jnp.einsum('bhts,bshv->bthv', attn, vc)
        o_inter = jnp.einsum('bthd,bhdv->bthv', qc * jnp.exp(b), state)
        b_last = b[:, -1]
        k_dec = kc * jnp.exp(b_last[:, None] - b)
        state = jnp.exp(b_last)[..., None] * state + jnp.einsum('bshd,bshv->bhdv', k_dec, vc)
        return state, o_intra + o_inter

    s0 = jnp.zeros((B, H, dk, dv), jnp.float32)
    _, o = lax.scan(step, s0, (to_chunks(q), to_chunks(log_f), to_chunks(k), to_chunks(v)))
    return from_chunks(o)

def mlstm_scan(q, k, v, i_pre, log_f):
    B, _, H, dk = q.shape
    dv = v.shape[-1]
    tri = causal_tri()

    def step(carry, inp):
        C, n, m = carry
        qc, kc, vc, ic, fc = inp
        bh = jnp.moveaxis(jnp.cumsum(fc, axis=1), 1, 2)
        ih = jnp.moveaxis(ic, 1, 2)
        logD = jnp.where(tri, bh[..., :, None] - bh[..., None, :] + ih[..., None, :], NEG_BIG)
        log_inter = bh + m[..., None]
        m_t = jnp.maximum(jnp.max(logD, axis=-1), log_inter)
        s = jnp.einsum('bthd,bshd->bhts', qc, kc) * jnp.exp(logD - m_t[..., None])
        inter_w = jnp.exp(log_inter - m_t)
        inter_wt = jnp.swapaxes(inter_w, 1, 2)[..., None]
        num = jnp.einsum('bhts,bshv->bthv', s, vc) + jnp.einsum('bthd,bhdv->bthv', qc, C) * inter_wt
        den = jnp.sum(s, axis=-1) + jnp.einsum('bthd,bhd->bht', qc, n) * inter_w
        denom = jnp.maximum(jnp.abs(den), jnp.exp(-m_t))
        h = num / jnp.swapaxes(denom, 1, 2)[..., None]
        b_last = bh[..., -1]
        log_w = b_last[..., None] - bh + ih
        m_new = jnp.maximum(b_last + m, jnp.max(log_w, axis=-1))
        w = jnp.swapaxes(jnp.exp(log_w - m_new[..., None]), 1, 2)[..., None]
        dstate = jnp.exp(b_last + m - m_new)
        C = dstate[..., None, None] * C + jnp.einsum('bshd,bshv->bhdv', kc * w, vc)
        n = dstate[..., None] * n + jnp.sum(kc * w, axis=1)
        return (C, n, m_new), h

    c0 = (jnp.zeros((B, H, dk, dv), jnp.float32), jnp.zeros((B, H, dk), jnp.float32),
          jnp.zeros((B, H), jnp.float32))
    _, h = lax.scan(step, c0, (to_chunks(q), to_chunks(k), to_chunks(v), to_chunks(i_pre), to_chunks(log_f)))
    return from_chunks(h)

def ssd_scan(x, dt, A, Bm, Cm):
    B, _, H, P = x.shape
    N = Bm.shape[-1]
    hpg = H // Bm.shape[2]
    tri = causal_tri()
    A = A.astype(jnp.float32)

    def step(state, inp):
        xc, dtc, Bc, Cc = inp
        cum = jnp.moveaxis(jnp.cumsum(dtc * A, axis=1), 1, 2)
        L = jnp.exp(jnp.where(tri, cum[..., :, None] - cum[..., None, :], NEG_BIG))
        CB = jnp.repeat(jnp.einsum('btgn,bsgn->bgts', Cc, Bc), hpg, axis=1)
        xdt = xc * dtc[..., None]
        y_intra = jnp.einsum('bhts,bshp->bthp', CB * L, xdt)
        Ch = jnp.repeat(Cc, hpg, axis=2)
        y_inter = jnp.einsum('bthn,bhpn->bthp', Ch, state) * jnp.swapaxes(jnp.exp(cum), 1, 2)[..., None]
        dec = jnp.swapaxes(jnp.exp(cum[..., -1:] - cum), 1, 2)[..., None]
        Bh = jnp.repeat(Bc, hpg, axis=2)
        state = jnp.exp(cum[..., -1])[..., None, None] * state + jnp.einsum('bshn,bshp->bhpn', Bh * dec, xdt)
        return state, y_intra + y_inter

    s0 = jnp.zeros((B, H, P, N), jnp.float32)
    _, y = lax.scan(step, s0, (to_chunks(x), to_chunks(dt), to_chunks(Bm), to_chunks(Cm)))
    return from_chunks(y)

def first_inputs(seed: int = 0) -> dict:
    key = jax.random.key(seed)
    ks = jax.random.split(key, 32)
    f32 = jnp.float32

    def nrm(k, shape, scale):
        return jax.random.normal(k, shape, f32) * scale

    def gain(k, shape):
        return 1.0 + 0.05 * jax.random.normal(k, shape, f32)

    dt0 = jnp.exp(jax.random.uniform(ks[12], (DEPTH, MB_HEADS), f32, math.log(1e-3), math.log(1e-1)))
    ml_f_bias = jnp.linspace(3.0, 6.0, ML_HEADS, dtype=f32)[None] + nrm(ks[7], (DEPTH, ML_HEADS), 0.1)
    ml_i_bias = nrm(ks[8], (DEPTH, ML_HEADS), 0.1)
    return {
        "x": jax.random.normal(ks[0], (BATCH, SEQ, D_MODEL), f32),
        "norm1_g": gain(ks[1], (DEPTH, D_MODEL)),
        "w_in": nrm(ks[2], (DEPTH, D_MODEL, N_IN), D_MODEL ** -0.5),
        "hg_lb_logits": nrm(ks[3], (DEPTH, HG_QK), 0.1),
        "hg_norm_g": gain(ks[4], (DEPTH, HG_DV)),
        "ml_conv_w": nrm(ks[5], (DEPTH, ML_CONV, 2 * ML_QK), ML_CONV ** -0.5),
        "ml_conv_b": nrm(ks[6], (DEPTH, 2 * ML_QK), 0.02),
        "ml_gate_b": jnp.concatenate([ml_i_bias, ml_f_bias], axis=-1),
        "ml_norm_g": gain(ks[9], (DEPTH, ML_DV)),
        "mb_conv_w": nrm(ks[10], (DEPTH, MB_CONV, MB_CONV_DIM), MB_CONV ** -0.5),
        "mb_conv_b": nrm(ks[11], (DEPTH, MB_CONV_DIM), 0.02),
        "mb_dt_bias": dt0 + jnp.log(-jnp.expm1(-dt0)),
        "mb_a_log": jnp.log(jax.random.uniform(ks[13], (DEPTH, MB_HEADS), f32, 1.0, 16.0)),
        "mb_d": gain(ks[14], (DEPTH, MB_HEADS)),
        "mb_norm_g": gain(ks[15], (DEPTH, MB_W)),
        "w_br_hg": nrm(ks[16], (DEPTH, HG_W, D_MODEL), HG_W ** -0.5),
        "w_br_ml": nrm(ks[17], (DEPTH, ML_W, D_MODEL), ML_W ** -0.5),
        "w_br_mb": nrm(ks[18], (DEPTH, MB_W, D_MODEL), MB_W ** -0.5),
        "w_out": nrm(ks[19], (DEPTH, D_MODEL, D_MODEL), D_MODEL ** -0.5),
        "norm2_g": gain(ks[20], (DEPTH, D_MODEL)),
        "w_up": nrm(ks[21], (DEPTH, D_MODEL, 2 * D_FF), D_MODEL ** -0.5),
        "ffn_conv_w": nrm(ks[22], (DEPTH, FFN_CONV, 2 * D_FF), FFN_CONV ** -0.5),
        "ffn_conv_b": nrm(ks[23], (DEPTH, 2 * D_FF), 0.02),
        "w_down": nrm(ks[24], (DEPTH, D_FF, D_MODEL), D_FF ** -0.5),
        "final_g": gain(ks[25], (D_MODEL,)),
    }

def first_block(x, norm1_g, w_in, hg_lb_logits, hg_norm_g, ml_conv_w, ml_conv_b, ml_gate_b, ml_norm_g,
              mb_conv_w, mb_conv_b, mb_dt_bias, mb_a_log, mb_d, mb_norm_g, w_br_hg, w_br_ml, w_br_mb,
              w_out, norm2_g, w_up, ffn_conv_w, ffn_conv_b, w_down, final_g):
    B, S, _ = x.shape
    f32 = jnp.float32
    lb_p = jax.nn.softmax(hg_lb_logits.astype(f32), axis=0)
    lbs = jnp.cumsum(lb_p, axis=0) - lb_p[0]
    split_at = [int(c) for c in np.cumsum(IN_SPLITS)[:-1]]

    for l in range(DEPTH):
        h = rmsnorm(x, norm1_g[l])
        (hg_q, hg_f, hg_i, hg_g, ml_qk, ml_v, ml_if, ml_o,
         mb_z, mb_xbc, mb_dt, gate_pre) = jnp.split(h @ w_in[l], split_at, axis=-1)

        lb = lbs[l]
        log_f = jnp.log(lb + (1.0 - lb) * jax.nn.sigmoid(hg_f.astype(f32)))
        o_hg = hgrn2_scan(jax.nn.silu(hg_q).reshape(B, S, HG_HEADS, HG_DK),
                          log_f.reshape(B, S, HG_HEADS, HG_DK),
                          hg_i.reshape(B, S, HG_HEADS, HG_DV))
        y_hg = (rmsnorm(o_hg, hg_norm_g[l]).reshape(B, S, HG_W)
                * jax.nn.silu(hg_g.astype(f32))).astype(x.dtype)

        qk = jax.nn.silu(causal_dwconv(ml_qk, ml_conv_w[l], ml_conv_b[l]))
        q_m, k_m = jnp.split(qk, 2, axis=-1)
        gb = ml_gate_b[l]
        i_pre = ml_if[..., :ML_HEADS] + gb[:ML_HEADS]
        log_f_m = jax.nn.log_sigmoid((ml_if[..., ML_HEADS:] + gb[ML_HEADS:]).astype(f32))
        h_ml = mlstm_scan(q_m.reshape(B, S, ML_HEADS, ML_DQK),
                          k_m.reshape(B, S, ML_HEADS, ML_DQK) * (ML_DQK ** -0.5),
                          ml_v.reshape(B, S, ML_HEADS, ML_DV), i_pre, log_f_m)
        y_ml = (rmsnorm(h_ml, ml_norm_g[l]).reshape(B, S, ML_W)
                * jax.nn.sigmoid(ml_o.astype(f32))).astype(x.dtype)

        xbc = jax.nn.silu(causal_dwconv(mb_xbc, mb_conv_w[l], mb_conv_b[l]))
        xs, Bm, Cm = jnp.split(xbc, [MB_W, MB_W + MB_GROUPS * MB_N], axis=-1)
        xs = xs.reshape(B, S, MB_HEADS, MB_P)
        dt = jax.nn.softplus((mb_dt + mb_dt_bias[l]).astype(f32))
        A = -jnp.exp(mb_a_log[l].astype(f32))
        y_ssd = ssd_scan(xs, dt, A, Bm.reshape(B, S, MB_GROUPS, MB_N), Cm.reshape(B, S, MB_GROUPS, MB_N))
        y_ssd = y_ssd + mb_d[l].astype(f32)[:, None] * xs
        yz = (y_ssd.reshape(B, S, MB_W) * jax.nn.silu(mb_z.astype(f32))).reshape(B, S, MB_GROUPS, MB_W // MB_GROUPS)
        y_mb = rmsnorm(yz, mb_norm_g[l].reshape(MB_GROUPS, MB_W // MB_GROUPS)).reshape(B, S, MB_W).astype(x.dtype)

        gates = jax.nn.sigmoid(gate_pre).reshape(B, S, N_BRANCH, D_MODEL)
        mixed = (gates[:, :, 0] * (y_hg @ w_br_hg[l])
                 + gates[:, :, 1] * (y_ml @ w_br_ml[l])
                 + gates[:, :, 2] * (y_mb @ w_br_mb[l]))
        x = x + mixed @ w_out[l]

        u = causal_dwconv(rmsnorm(x, norm2_g[l]) @ w_up[l], ffn_conv_w[l], ffn_conv_b[l])
        u_g, u_v = jnp.split(u, 2, axis=-1)
        x = x + (jax.nn.silu(u_g) * u_v) @ w_down[l]

    return rmsnorm(x, final_g)


DEPTH_2 = 2

GRID_W = 64
CTX_LEN = 256
A_WIDTH = D_MODEL // 4
A_GROUPS = 4
A_GDIM = A_WIDTH // A_GROUPS
CHUNK_2 = 128
B_HEAD_DIM = 64
B_HEADS = (D_MODEL // 2) // B_HEAD_DIM
B_KV_HEADS = B_HEADS // 4
B_WIDTH = B_HEADS * B_HEAD_DIM
WINDOW = 128
BLOCK = 128
C_V_DIM = 64
C_QK_DIM = C_V_DIM // 2
C_HEADS = (D_MODEL // 4) // C_V_DIM
C_WIDTH = C_HEADS * C_V_DIM
Q_BLOCK = 128
MIX_WIDTH = A_WIDTH + B_WIDTH + C_WIDTH
PROJ_SIZES = (2 * A_WIDTH, B_WIDTH, B_KV_HEADS * B_HEAD_DIM, B_KV_HEADS * B_HEAD_DIM,
              C_HEADS * 2 * C_QK_DIM, C_HEADS * 2 * C_QK_DIM, C_WIDTH)
PROJ_WIDTH = sum(PROJ_SIZES)
D_FF_2 = 256 * ((8 * D_MODEL // 3 + 255) // 256)
CONV_W = 3
ROPE_BASE = 10000.0


def rms_norm(x, gain=None):
    xf = x.astype(jnp.float32)
    y = xf * lax.rsqrt(jnp.mean(xf * xf, axis=-1, keepdims=True) + EPS)
    if gain is not None:
        y = y * gain.astype(jnp.float32)
    return y.astype(x.dtype)

def modulation(cond, w_ada, b_ada):
    m = jax.nn.silu(cond) @ w_ada + b_ada
    return [t[..., None, :] for t in jnp.split(m, 6, axis=-1)]

def modulate(h, shift, scale):
    return h * (1 + scale) + shift

def split_proj(z):
    idx = np.cumsum(np.array(PROJ_SIZES))[:-1].tolist()
    return jnp.split(z, idx, axis=-1)

def axial_rope(n_tokens, head_dim):
    rows = n_tokens // GRID_W
    row = jnp.repeat(jnp.arange(rows, dtype=jnp.float32), GRID_W)
    col = jnp.tile(jnp.arange(GRID_W, dtype=jnp.float32), rows)
    n_freq = head_dim // 4
    inv_freq = ROPE_BASE ** (-jnp.arange(n_freq, dtype=jnp.float32) / n_freq)
    ang = jnp.stack([row[:, None] * inv_freq, col[:, None] * inv_freq], axis=1)
    return jnp.cos(ang), jnp.sin(ang)

def apply_rope(x, cos, sin):
    b, l, h, d = x.shape
    xr = x.reshape(b, l, h, 2, 2, d // 4).astype(jnp.float32)
    x1, x2 = xr[..., 0, :], xr[..., 1, :]
    c = cos[None, :, None]
    s = sin[None, :, None]
    out = jnp.stack([x1 * c - x2 * s, x2 * c + x1 * s], axis=-2)
    return out.reshape(b, l, h, d).astype(x.dtype)

def rope_maps(t, cos, sin):
    b, l, h, m, d = t.shape
    return apply_rope(t.reshape(b, l, h * m, d), cos, sin).reshape(b, l, h, m, d)

def chunk_gmlp(z, w_s, b_s):
    b, l, _ = z.shape
    z = jax.nn.gelu(z)
    u, v = jnp.split(z, 2, axis=-1)
    v = rms_norm(v.reshape(b, l // CHUNK_2, CHUNK_2, A_GROUPS, A_GDIM))
    mixed = jnp.einsum('gpq,bnqgc->bnpgc', w_s, v) + b_s.T[None, None, :, :, None]
    return u * mixed.reshape(b, l, A_WIDTH)

def window_attn_latent(q, k, v, k_ctx, v_ctx, sink):
    b, l, hq, d = q.shape
    hkv = k.shape[2]
    g = hq // hkv
    nb = l // BLOCK
    lc = k_ctx.shape[1]
    scale = d ** -0.5
    qb = q.reshape(b, nb, BLOCK, hkv, g, d)

    def band(t):
        tb = jnp.pad(t.reshape(b, nb, BLOCK, hkv, d), ((0, 0), (1, 1), (0, 0), (0, 0), (0, 0)))
        return jnp.concatenate([tb[:, :-2], tb[:, 1:-1], tb[:, 2:]], axis=2)

    kb, vb = band(k), band(v)
    s_win = jnp.einsum('bnqhgd,bnkhd->bnhgqk', qb, kb).astype(jnp.float32) * scale
    qpos = jnp.arange(nb)[:, None, None] * BLOCK + jnp.arange(BLOCK)[None, :, None]
    kpos = (jnp.arange(nb)[:, None, None] - 1) * BLOCK + jnp.arange(3 * BLOCK)[None, None, :]
    valid = (kpos >= 0) & (kpos < l) & (jnp.abs(qpos - kpos) <= WINDOW)
    s_win = jnp.where(valid[None, :, None, None], s_win, -jnp.inf)
    s_ctx = jnp.einsum('bnqhgd,bkhd->bnhgqk', qb, k_ctx).astype(jnp.float32) * scale
    s_sink = jnp.broadcast_to(sink.astype(jnp.float32).reshape(hkv, g)[None, None, :, :, None, None],
                              s_win.shape[:-1] + (1,))
    p = jax.nn.softmax(jnp.concatenate([s_win, s_ctx, s_sink], axis=-1), axis=-1)
    kw = 3 * BLOCK
    p_win = p[..., :kw].astype(v.dtype)
    p_ctx = p[..., kw:kw + lc].astype(v.dtype)
    o = (jnp.einsum('bnhgqk,bnkhd->bnqhgd', p_win, vb)
         + jnp.einsum('bnhgqk,bkhd->bnqhgd', p_ctx, v_ctx))
    return o.reshape(b, l, hq * d)

def sink_attn_ctx(q, k, v, sink):
    b, lc, hq, d = q.shape
    hkv = k.shape[2]
    g = hq // hkv
    qg = q.reshape(b, lc, hkv, g, d)
    s = jnp.einsum('bqhgd,bkhd->bhgqk', qg, k).astype(jnp.float32) * d ** -0.5
    s_sink = jnp.broadcast_to(sink.astype(jnp.float32).reshape(1, hkv, g, 1, 1), (b, hkv, g, lc, 1))
    p = jax.nn.softmax(jnp.concatenate([s, s_sink], axis=-1), axis=-1)[..., :lc]
    o = jnp.einsum('bhgqk,bkhd->bqhgd', p.astype(v.dtype), v)
    return o.reshape(b, lc, hq * d)

def diff_lambda(lam_params, lam_init):
    lp = lam_params.astype(jnp.float32)
    return jnp.exp(jnp.sum(lp[0] * lp[1])) - jnp.exp(jnp.sum(lp[2] * lp[3])) + lam_init

def diff_attn_block(q, k, v, lam):
    s = jnp.einsum('bqhmd,bkhmd->bhmqk', q, k).astype(jnp.float32) * q.shape[-1] ** -0.5
    p = jax.nn.softmax(s, axis=-1)
    pd = p[:, :, 0] - lam * p[:, :, 1]
    return jnp.einsum('bhqk,bkhd->bqhd', pd.astype(v.dtype), v)

def diff_attn_latent(q, k, v, k_ctx, v_ctx, lam):
    b, l, h, _, dq = q.shape
    k_all = jnp.concatenate([k, k_ctx], axis=1)
    v_all = jnp.concatenate([v, v_ctx], axis=1)
    qb = jnp.moveaxis(q.reshape(b, l // Q_BLOCK, Q_BLOCK, h, 2, dq), 1, 0)
    o = lax.map(lambda qblk: diff_attn_block(qblk, k_all, v_all, lam), qb)
    return jnp.moveaxis(o, 0, 1).reshape(b, l, h, -1)

def conv_ffn(h, w_up, conv_w, conv_b, w_down):
    a = h @ w_up
    a = lax.conv_general_dilated(a, conv_w, window_strides=(1,), padding=((CONV_W // 2, CONV_W // 2),),
                                 dimension_numbers=('NWC', 'WIO', 'NWC'),
                                 feature_group_count=a.shape[-1]) + conv_b
    gate, val = jnp.split(a, 2, axis=-1)
    return (jax.nn.silu(gate) * val) @ w_down

def second_inputs(seed: int = 0) -> dict:
    key = jax.random.key(seed)
    ks = jax.random.split(key, 24)
    nrm = jax.random.normal
    f32 = jnp.float32
    L = DEPTH_2
    D = D_MODEL
    return {
        'x': nrm(ks[0], (BATCH, SEQ, D), f32),
        'c': nrm(ks[1], (BATCH, D), f32),
        'ctx': nrm(ks[2], (BATCH, CTX_LEN, D), f32),
        'c_ctx': nrm(ks[3], (D,), f32),
        'w_ada': nrm(ks[4], (L, D, 6 * D), f32) * (0.25 * D ** -0.5),
        'b_ada': nrm(ks[5], (L, 6 * D), f32) * 0.01,
        'norm1_g': 1.0 + 0.02 * nrm(ks[6], (L, D), f32),
        'norm2_g': 1.0 + 0.02 * nrm(ks[7], (L, D), f32),
        'w_in': nrm(ks[8], (L, D, PROJ_WIDTH), f32) * D ** -0.5,
        'a_ws': nrm(ks[9], (L, A_GROUPS, CHUNK_2, CHUNK_2), f32) * CHUNK_2 ** -0.5,
        'a_bs': 1.0 + 0.02 * nrm(ks[10], (L, A_GROUPS, CHUNK_2), f32),
        'b_qnorm': 1.0 + 0.02 * nrm(ks[11], (L, B_HEAD_DIM), f32),
        'b_knorm': 1.0 + 0.02 * nrm(ks[12], (L, B_HEAD_DIM), f32),
        'b_sink': 0.5 * nrm(ks[13], (L, B_HEADS), f32),
        'c_qnorm': 1.0 + 0.02 * nrm(ks[14], (L, C_QK_DIM), f32),
        'c_knorm': 1.0 + 0.02 * nrm(ks[15], (L, C_QK_DIM), f32),
        'c_lam': 0.1 * nrm(ks[16], (L, 4, C_QK_DIM), f32),
        'c_subln': 1.0 + 0.02 * nrm(ks[17], (L, C_V_DIM), f32),
        'w_out': nrm(ks[18], (L, MIX_WIDTH, D), f32) * MIX_WIDTH ** -0.5,
        'w_up': nrm(ks[19], (L, D, 2 * D_FF_2), f32) * D ** -0.5,
        'conv_w': nrm(ks[20], (L, CONV_W, 1, 2 * D_FF_2), f32) * CONV_W ** -0.5,
        'conv_b': 0.01 * nrm(ks[21], (L, 2 * D_FF_2), f32),
        'w_down': nrm(ks[22], (L, D_FF_2, D), f32) * D_FF_2 ** -0.5,
    }

def second_block(x, c, ctx, c_ctx, w_ada, b_ada, norm1_g, norm2_g, w_in, a_ws, a_bs,
              b_qnorm, b_knorm, b_sink, c_qnorm, c_knorm, c_lam, c_subln,
              w_out, w_up, conv_w, conv_b, w_down):
    b, l, _ = x.shape
    lc = ctx.shape[1]
    cos_b, sin_b = axial_rope(l, B_HEAD_DIM)
    cos_c, sin_c = axial_rope(l, C_QK_DIM)
    for i in range(DEPTH_2):
        last = i == DEPTH_2 - 1
        lam_init = 0.8 - 0.6 * math.exp(-0.3 * i)
        sh1, sc1, g1, sh2, sc2, g2 = modulation(c, w_ada[i], b_ada[i])
        csh1, csc1, cg1, csh2, csc2, cg2 = modulation(c_ctx, w_ada[i], b_ada[i])

        h = modulate(rms_norm(x, norm1_g[i]), sh1, sc1)
        hc = modulate(rms_norm(ctx, norm1_g[i]), csh1, csc1)
        a_z, bq, bk, bv, cq, ck, cv = split_proj(h @ w_in[i])
        a_zc, bqc, bkc, bvc, cqc, ckc, cvc = split_proj(hc @ w_in[i])

        k_bc = rms_norm(bkc.reshape(b, lc, B_KV_HEADS, B_HEAD_DIM), b_knorm[i])
        v_bc = bvc.reshape(b, lc, B_KV_HEADS, B_HEAD_DIM)
        k_cc = rms_norm(ckc.reshape(b, lc, C_HEADS, 2, C_QK_DIM), c_knorm[i])
        v_cc = cvc.reshape(b, lc, C_HEADS, C_V_DIM)
        lam = diff_lambda(c_lam[i], lam_init)

        out_a = chunk_gmlp(a_z, a_ws[i], a_bs[i])
        q_b = apply_rope(rms_norm(bq.reshape(b, l, B_HEADS, B_HEAD_DIM), b_qnorm[i]), cos_b, sin_b)
        k_b = apply_rope(rms_norm(bk.reshape(b, l, B_KV_HEADS, B_HEAD_DIM), b_knorm[i]), cos_b, sin_b)
        v_b = bv.reshape(b, l, B_KV_HEADS, B_HEAD_DIM)
        out_b = window_attn_latent(q_b, k_b, v_b, k_bc, v_bc, b_sink[i])
        q_c = rope_maps(rms_norm(cq.reshape(b, l, C_HEADS, 2, C_QK_DIM), c_qnorm[i]), cos_c, sin_c)
        k_c = rope_maps(rms_norm(ck.reshape(b, l, C_HEADS, 2, C_QK_DIM), c_knorm[i]), cos_c, sin_c)
        v_c = cv.reshape(b, l, C_HEADS, C_V_DIM)
        o_c = diff_attn_latent(q_c, k_c, v_c, k_cc, v_cc, lam)
        out_c = (rms_norm(o_c, c_subln[i]) * (1 - lam_init)).reshape(b, l, C_WIDTH)

        x = x + g1 * (jnp.concatenate([out_a, out_b, out_c], axis=-1) @ w_out[i])
        x = x + g2 * conv_ffn(modulate(rms_norm(x, norm2_g[i]), sh2, sc2),
                              w_up[i], conv_w[i], conv_b[i], w_down[i])

        if not last:
            out_ac = chunk_gmlp(a_zc, a_ws[i], a_bs[i])
            q_bc = rms_norm(bqc.reshape(b, lc, B_HEADS, B_HEAD_DIM), b_qnorm[i])
            out_bc = sink_attn_ctx(q_bc, k_bc, v_bc, b_sink[i])
            q_cc = rms_norm(cqc.reshape(b, lc, C_HEADS, 2, C_QK_DIM), c_qnorm[i])
            o_cc = diff_attn_block(q_cc, k_cc, v_cc, lam)
            out_cc = (rms_norm(o_cc, c_subln[i]) * (1 - lam_init)).reshape(b, lc, C_WIDTH)
            ctx = ctx + cg1 * (jnp.concatenate([out_ac, out_bc, out_cc], axis=-1) @ w_out[i])
            ctx = ctx + cg2 * conv_ffn(modulate(rms_norm(ctx, norm2_g[i]), csh2, csc2),
                                       w_up[i], conv_w[i], conv_b[i], w_down[i])
    return x


def setup_inputs(seed=0):
    out = dict(first_inputs(seed))
    for name, value in second_inputs(seed + 1).items():
        if name != "x":
            out[name + "_2"] = value
    return out


def reference(
    x, norm1_g, w_in, hg_lb_logits, hg_norm_g, ml_conv_w, ml_conv_b, ml_gate_b, ml_norm_g,
    mb_conv_w, mb_conv_b, mb_dt_bias, mb_a_log, mb_d, mb_norm_g, w_br_hg, w_br_ml, w_br_mb,
    w_out, norm2_g, w_up, ffn_conv_w, ffn_conv_b, w_down, final_g, c_2, ctx_2, c_ctx_2, w_ada_2,
    b_ada_2, norm1_g_2, norm2_g_2, w_in_2, a_ws_2, a_bs_2, b_qnorm_2, b_knorm_2, b_sink_2,
    c_qnorm_2, c_knorm_2, c_lam_2, c_subln_2, w_out_2, w_up_2, conv_w_2, conv_b_2, w_down_2,
):
    x = first_block(
        x, norm1_g, w_in, hg_lb_logits, hg_norm_g, ml_conv_w, ml_conv_b, ml_gate_b, ml_norm_g,
        mb_conv_w, mb_conv_b, mb_dt_bias, mb_a_log, mb_d, mb_norm_g, w_br_hg, w_br_ml, w_br_mb,
        w_out, norm2_g, w_up, ffn_conv_w, ffn_conv_b, w_down, final_g,
    )
    return second_block(
        x, c_2, ctx_2, c_ctx_2, w_ada_2, b_ada_2, norm1_g_2, norm2_g_2, w_in_2, a_ws_2, a_bs_2,
        b_qnorm_2, b_knorm_2, b_sink_2, c_qnorm_2, c_knorm_2, c_lam_2, c_subln_2, w_out_2,
        w_up_2, conv_w_2, conv_b_2, w_down_2,
    )


_drawn_inputs = setup_inputs


def setup_inputs(seed=0):
    import zlib

    import numpy as np

    out = dict(_drawn_inputs(seed))
    spreads = {}
    factors = {'hg_norm_g': 3.815,
     'ml_conv_b': 8.0,
     'ml_norm_g': 4.073,
     'mb_conv_b': 4.33,
     'ffn_conv_b': 4.489,
     'b_ada_2': 4.096,
     'norm1_g_2': 8.0,
     'norm2_g_2': 8.0,
     'a_bs_2': 8.0,
     'b_qnorm_2': 8.0,
     'b_knorm_2': 8.0,
     'b_sink_2': 8.0,
     'c_qnorm_2': 8.0,
     'c_knorm_2': 8.0,
     'c_lam_2': 8.0,
     'c_subln_2': 64.0,
     'conv_b_2': 8.0}
    for name, (base, spread) in spreads.items():
        noise = np.random.default_rng([zlib.crc32(name.encode()), seed]).standard_normal(out[name].shape)
        drawn = base * np.exp(spread * noise) if base else spread * noise
        out[name] = jnp.asarray(drawn.astype(out[name].dtype))
    for name, factor in factors.items():
        out[name] = (out[name] * factor).astype(out[name].dtype)
    return out
```

```python
from contextlib import ExitStack, contextmanager

import numpy as np

import concourse.bass as bass
from concourse import mybir

F32 = mybir.dt.float32
U32 = mybir.dt.uint32
ALU = mybir.AluOpType
ACT = mybir.ActivationFunctionType
AX = mybir.AxisListType

P = 128
D = 1024
DT = D // P
S = 256
ST = S // P
EPS = 1e-6

HG_H = 8
ML_H, ML_DV = 4, 256
MB_H, MB_P, MB_G = 16, 64, 4
FF = 2816
FFT = FF // P
N_ADA = 6 * DT
RING = 3
SLOT = DT * 512
BANK = 512
LEVELS = [64, 32, 16, 8, 4, 2, 1]
LAYERS = 2


class Signal:

    def __init__(self, handle):
        self.handle, self.base, self.total = handle, 0, 0

    def one(self):
        self.total += 1
        return self.handle, 1

    def dma(self):
        self.total += 16
        return self.handle, 16

    def at(self, n):
        return self.handle, self.base + n


class Core:

    def __init__(self, nc, ctx):
        self.nc, self.ctx, self.signals = nc, ctx, {}
        self.psum = ctx.enter_context(nc.psum_tensor("acc_psum", [P, 8, BANK], F32))
        self.ring = self.sbuf("ring", [P, RING, SLOT])
        self.loaded = [self.sig(f"weights_loaded_{i}") for i in range(RING)]
        self.used = self.sig("weights_used")
        self.chunks, self.taken = [], 0

    def sbuf(self, name, shape, dt=F32):
        return self.ctx.enter_context(self.nc.sbuf_tensor(name + "_sb", shape, dt))

    def sig(self, name):
        if name not in self.signals:
            self.signals[name] = Signal(self.ctx.enter_context(self.nc.semaphore(name)))
        return self.signals[name]

    @contextmanager
    def phase(self):
        with self.nc.Block() as block:
            yield block
        for s in self.signals.values():
            s.base = s.total

    def slot(self, c, kt, n):
        return self.ring[:, c % RING, 0:kt * n].rearrange("p (k n) -> p k n", k=kt)

    def load(self, sp, c):
        if c < len(self.chunks):
            src = self.chunks[c]
            sp.dma_start(self.ring[:, c % RING, 0:src.shape[1]], src).then_inc(*self.loaded[c % RING].dma())


def linker(eng, signal):
    start = signal.total

    def link(ins):
        ins.then_inc(*signal.one())
        eng.wait_ge(*signal.at(signal.total - signal.base))
        return ins

    return link


def project(core, x, T, widths, kt, fm=True, on_act=None, on_dve=None, then_act=None, tok_tiles=None):
    nc = core.nc
    acc, free = core.sig("proj_acc_ready"), core.sig("proj_bank_free")
    mid, midfree = core.sig("proj_mid_ready"), core.sig("proj_mid_free")
    c0 = core.taken
    core.taken += len(widths)
    tiles = []
    for n, w in enumerate(widths):
        if fm:
            tiles += [(n, j, 0, 0) for j in range(w // P)]
        else:
            first, cols, toks = tok_tiles(n) if tok_tiles else [(0, w, range(ST))][0]
            if isinstance(toks, dict):
                tiles += [(n, t, *fc) for t, fc in toks.items()]
            else:
                tiles += [(n, t, first, cols) for t in toks]
    BANKS = 8

    def bank(i):
        return core.psum[:, i % BANKS, :]

    with core.phase() as block:

        @block.sync
        def _(sp):
            for n in range(len(widths)):
                sp.wait_ge(core.used.handle, c0 + n + 1)
                core.load(sp, c0 + n + RING)

        @block.tensor
        def _(pe):
            for i, (n, j, first, cols) in enumerate(tiles):
                c = c0 + n
                w = core.slot(c, kt, widths[n])
                if i == 0 or tiles[i - 1][0] != n:
                    pe.wait_ge(core.loaded[c % RING].handle, 16 * (c // RING + 1))
                if i >= BANKS:
                    pe.wait_ge(*free.at(i - BANKS + 1))
                for k in range(kt):
                    if fm:
                        mm = nc.tensor.matmul(bank(i)[:, 0:T], w[:, k, j * P:(j + 1) * P], x[:, k, 0:T],
                                              start=(k == 0), stop=(k == kt - 1))
                    else:
                        mm = nc.tensor.matmul(bank(i)[:, 0:cols], x[:, k, j * P:(j + 1) * P],
                                              w[:, k, first:first + cols], start=(k == 0), stop=(k == kt - 1))
                mm.then_inc(*acc.one())
                if i == len(tiles) - 1 or tiles[i + 1][0] != n:
                    pe.wait_ge(*acc.at(i + 1))
                    pe.sem_inc(*core.used.one())

        if on_act or then_act:
            @block.scalar
            def _(act):
                for i, (n, j, first, cols) in enumerate(tiles):
                    if on_act:
                        act.wait_ge(*acc.at(i + 1))
                        on_act(act, i, n, j, bank(i)).then_inc(*free.one())
                    else:
                        act.wait_ge(*mid.at(i + 1))
                        then_act(act, i).then_inc(*midfree.one())

        if on_dve:
            @block.vector
            def _(dve):
                link = linker(dve, core.sig("dve_chain"))
                for i, (n, j, first, cols) in enumerate(tiles):
                    dve.wait_ge(*acc.at(i + 1))
                    if then_act and i >= 2:
                        dve.wait_ge(*midfree.at(i - 1))
                    link(on_dve(dve, link, i, bank(i)))
                    dve.sem_inc(*free.one())
                    if then_act:
                        dve.sem_inc(*mid.one())


def norm_fm(core, src, ntile, m, W, gain, out, shift=None, gate=None):
    nc = core.nc
    sq_ready, sq_used, root = core.sig("norm_sq_ready"), core.sig("norm_sq_used"), core.sig("norm_root_ready")
    groups = ntile // m
    NSQ = 4
    sq = core.norm_sq
    rt = core.norm_rt[:, 0:groups * W].rearrange("p (g w) -> p g w", g=groups)
    with core.phase() as block:

        @block.scalar
        def _(act):
            for t in range(ntile):
                if t >= NSQ:
                    act.wait_ge(*sq_used.at(t - NSQ + 1))
                nc.scalar.activation(sq[:, t % NSQ, 0:W], src(t), ACT.Square).then_inc(*sq_ready.one())
            for g in range(groups):
                act.wait_ge(*sq_used.at((g + 1) * m))
                nc.scalar.activation(rt[:, g, :], core.psum[:, g, 0:W], ACT.Sqrt, scale=1.0 / (P * m),
                                     bias=core.eps[:, 0:1]).then_inc(*root.one())

        @block.tensor
        def _(pe):
            for t in range(ntile):
                pe.wait_ge(*sq_ready.at(t + 1))
                nc.tensor.matmul(core.psum[:, t // m, 0:W], core.ones[:, :], sq[:, t % NSQ, 0:W],
                                 start=(t % m == 0), stop=(t % m == m - 1)).then_inc(*sq_used.one())

        @block.vector
        def _(dve):
            link = linker(dve, core.sig("dve_chain"))
            for g in range(groups):
                dve.wait_ge(*root.at(g + 1))
                link(nc.vector.reciprocal(rt[:, g, :], rt[:, g, :]))
                for t in range(g * m, g * m + m):
                    ins = nc.vector.scalar_tensor_tensor(out(t), src(t), gain(t), rt[:, g, :], ALU.mult, ALU.mult)
                    if gate:
                        link(ins)
                        nc.vector.tensor_tensor(out(t), out(t), gate(t), ALU.mult)
                    if shift:
                        link(ins)
                        nc.vector.tensor_scalar(out(t), out(t), shift(t), None, ALU.add)


def pack_columns(items):
    at, n = {}, 0
    for name, w in items:
        at[name] = (n, w)
        n += w
    return at, n


PARS = [("norm1", DT), ("hg_norm", 1), ("ml_w", 4 * DT), ("ml_b", DT), ("ml_norm", 2), ("mb_w", 4 * 16),
        ("mb_b", 16), ("mb_norm", DT), ("norm2", DT), ("ff_w", 3 * 44), ("ff_b", 44), ("final", DT), ("mb_d", DT),
        ("gate_i", 1), ("gate_f", 1), ("dt_bias", 1), ("a_log", 1), ("w_gates", DT * 24), ("cond", 2 * DT)]
for _i in range(LAYERS):
    PARS += [(f"{n}{_i}", w) for n, w in (
        ("norm1_", DT), ("norm2_", DT), ("b_ada", N_ADA), ("cw", 132), ("cb", 44), ("a_bs", 4), ("a_ws", 512),
        ("gain_b", 128), ("gain_c", 64), ("subln", 64), ("sink", 8), ("lam", 128))]
PAR_AT, PAR_N = pack_columns(PARS)
CONS = [("ident", P), ("causal", P), ("window", 2 * BANK), ("cos_b", 2 * 64), ("sin_b", 2 * 64),
        ("cos_c", 2 * 32), ("sin_c", 2 * 32)]
CON_AT, CON_N = pack_columns(CONS)
LEV_N = (len(LEVELS) + 1) * P


def build(nc, a, out):
    with ExitStack() as ctx:
        core = Core(nc, ctx)
        sb, sig = core.sbuf, core.sig
        par = sb("par", [P, PAR_N])
        con = sb("con", [P, CON_N])
        X = sb("X", [P, DT, 2 * S])
        H = sb("H", [P, DT, 2 * S])
        core.ones = sb("ones", [P, P])
        core.eps = sb("eps", [P, 1])
        core.norm_sq = sb("norm_sq", [P, 4, 512])
        core.norm_rt = sb("norm_rt", [P, 2048])
        adaM = sb("adaM", [P, N_ADA, 2])
        cond = sb("cond", [P, DT, 2])
        small = sb("small", [P, 64])
        ARENA = 17600
        arena = sb("arena", [P, ARENA])

        def pr(name, i=0, n=1):
            o = PAR_AT[name][0] + i
            return par[:, o:o + n]

        def pv(name, a_):
            o, w = PAR_AT[name]
            return par[:, o:o + w].rearrange("p (a b) -> p a b", a=a_)

        def cn(name, i=0, n=None):
            o, w = CON_AT[name]
            return con[:, o + i:o + i + (w if n is None else n)]

        def view(o, a_, b_):
            assert o + a_ * b_ <= ARENA, (o, a_, b_)
            return arena[:, o:o + a_ * b_].rearrange("p (a b) -> p a b", a=a_)

        ident = cn("ident")
        causal = cn("causal")

        plan = []

        def add(name, idx):
            plan.extend(a[name][i] for i in idx)

        add("w_in", range(0, 8))
        add("w_in", range(8, 14))
        add("w_in", range(14, 20))
        for b, name in enumerate(("w_br_hg", "w_br_ml", "w_br_mb")):
            add("w_in", range(20 + 2 * b, 22 + 2 * b))
            add(name, range(2))
        add("w_out", range(2))
        add("w_up", range(11))
        add("w_down", range(8))
        for i in range(LAYERS):
            add("w_ada_2", range(12 * i, 12 * i + 12))
            add("w_in_2", range(4 * i, 4 * i + 4))
            add("w_out_2", range(2 * i, 2 * i + 2))
            add("w_up_2", range(11 * i, 11 * i + 11))
            add("w_down_2", range(8 * i, 8 * i + 8))
        core.chunks = plan

        in_ready = sig("inputs_ready")
        with core.phase() as block:

            @block.sync
            def _(sp):
                sp.dma_start(X[:, :, 0:S], a["x"].rearrange("(k p) t -> p k t", p=P)).then_inc(*in_ready.dma())
                sp.dma_start(par[:, :], a["par"]).then_inc(*in_ready.dma())
                sp.dma_start(con[:, :], a["con"]).then_inc(*in_ready.dma())
                for c in range(RING):
                    core.load(sp, c)
                sp.wait_ge(*in_ready.at(48))

            @block.vector
            def _(dve):
                nc.vector.memset(core.ones[:, :], 1.0)
                nc.vector.memset(core.eps[:, :], EPS)

        hybrid_block(core, a, X, H, pr, pv, cn, view, ident, causal, small)
        feed_forward(core, X, H, view, S, lambda t: pr("norm2", t), None,
                     lambda k, t: pr("ff_w", k * 44 + t), lambda t: pr("ff_b", t), 2, None)
        conditions(core, a, X, pv, cond)
        for i in range(LAYERS):
            attention_layer(core, a, i, X, H, pr, pv, cn, view, ident, small, adaM, cond)
        stored = sig("output_stored")
        with core.phase() as block:

            @block.sync
            def _(sp):
                sp.dma_start(out.rearrange("(k p) t -> p k t", p=P), X[:, :, 0:S]).then_inc(*stored.dma())
                sp.wait_ge(*stored.at(16))


def hybrid_block(core, a, X, H, pr, pv, cn, view, ident, causal, small):
    nc, sig, psum = core.nc, core.sig, core.psum
    W8 = DT * S
    y_hg, y_ml, y_mb = view(0, DT, S), view(W8, DT, S), view(2 * W8, DT, S)

    norm_fm(core, lambda t: X[:, t, 0:S], DT, DT, S, lambda t: pr("norm1", t), lambda t: H[:, t, 0:S])

    q, k, b = view(0, HG_H, S), view(W8, HG_H, S), view(2 * W8, HG_H, S)
    v = view(3 * W8, ST, D)
    g = view(4 * W8, HG_H, S)
    dec = view(5 * W8, HG_H, S)
    qe, ke = view(6 * W8, HG_H, S), view(7 * W8, HG_H, S)

    def silu_to(dst):
        return lambda act, i, n, j, ps: nc.scalar.activation(dst[:, i, :], ps[:, 0:S], ACT.Silu)

    def copy_to(dst):
        return lambda act, i, n, j, ps: nc.scalar.activation(dst[:, i, :], ps[:, 0:S], ACT.Copy)

    def tm_to(dst):
        return lambda act, i, n, j, ps: nc.scalar.activation(dst[:, j, n * 512:(n + 1) * 512], ps[:, :], ACT.Copy)

    project(core, H, S, [512] * 2, DT, on_act=silu_to(q))
    project(core, H, S, [512] * 2, DT, on_act=copy_to(k))
    project(core, H, S, [512] * 2, DT, fm=False, on_act=tm_to(v))
    project(core, H, S, [512] * 2, DT, on_act=silu_to(g))

    steps = sig("hg_gate_steps")
    flat = lambda t: t.rearrange("p a b -> p (a b)")
    with core.phase() as block:

        @block.scalar
        def _(act):
            link = linker(act, sig("act_chain"))
            link(nc.scalar.activation(flat(dec), flat(k), ACT.Abs))
            link(nc.scalar.activation(flat(dec), flat(dec), ACT.Exp, scale=-1.0))
            nc.scalar.activation(flat(qe), flat(dec), ACT.Ln, bias=1.0).then_inc(*steps.one())
            act.wait_ge(*steps.at(2))
            nc.scalar.activation(flat(k), flat(k), ACT.Sigmoid, scale=-1.0)

        @block.vector
        def _(dve):
            link = linker(dve, sig("dve_chain"))
            nc.vector.memset(flat(ke), 1.0)
            dve.wait_ge(*steps.at(1))
            link(nc.vector.scalar_tensor_tensor(flat(dec), flat(k), 0.0, flat(qe), ALU.min, ALU.subtract))
            dve.sem_inc(*steps.one())
            for h in range(HG_H):
                nc.vector.tensor_tensor_scan(b[:, h, :], ke[:, h, :], dec[:, h, :], 0.0, ALU.mult, ALU.add)

    lv = view(8 * W8, 1, LEV_N)[:, 0].bitcast(U32)
    attn, attn1 = H[:, :, S:2 * S], X[:, :, S:S + P]
    mk_ready = sig("level_masks_ready")
    diff, expd, qd, kd, prod, put, peu = (sig(n) for n in (
        "hg_diff_ready", "hg_decay_ready", "hg_q_ready", "hg_k_ready", "hg_scores_ready", "hg_scores_read",
        "hg_operands_read"))
    levels = [P] + LEVELS + [0]
    NL = len(levels)
    with core.phase() as block:

        @block.sync
        def _(sp):
            sp.dma_start(lv[:, :], a["levels"]).then_inc(*mk_ready.dma())
            sp.wait_ge(*mk_ready.at(16))

        @block.vector
        def _(dve):
            link = linker(dve, sig("dve_chain"))
            nc.vector.memset(attn, 0.0)
            link(nc.vector.memset(attn1, 0.0))
            dve.wait_ge(*mk_ready.at(16))

            def take(n):
                L = levels[n]
                for h4 in range(4):
                    dve.wait_ge(*prod.at(4 * n + h4 + 1))
                    ps = psum[:, (4 * n + h4) % 8, :]
                    pair = attn[:, 2 * h4:2 * h4 + 2, :]
                    if L == P:
                        ins = nc.vector.tensor_copy(
                            pair[:, :, P:2 * P], ps[:, 0:2 * P].rearrange("p (h t) -> p h t", h=2))
                        link(ins)
                    else:
                        o = P * (levels.index(L) - 1)
                        m = lv[:, o:o + P].unsqueeze(1).broadcast_to([P, 2, P])
                        for t in range(2):
                            ins = nc.vector.copy_predicated(
                                (attn if t == 0 else attn1)[:, 2 * h4:2 * h4 + 2, 0:P], m, ps.rearrange("p (t h c) -> p t h c", t=2, h=2)[:, t])
                            link(ins)
                    dve.sem_inc(*put.one())

            for n, L in enumerate(levels):
                if L:
                    if n:
                        dve.wait_ge(*kd.at(n))
                    nb = W8 // (2 * L)
                    bv = flat(b).rearrange("p (n e l) -> p n e l", e=2, l=L)
                    dv = flat(dec).rearrange("p (n e l) -> p n e l", e=2, l=L)
                    r = bv[:, :, 0, L - 1:L].broadcast_to([P, nb, L])
                    nc.vector.tensor_tensor(dv[:, :, 1, :], bv[:, :, 1, :], r, ALU.subtract)
                    link(nc.vector.tensor_tensor(dv[:, :, 0, :], r, bv[:, :, 0, :], ALU.subtract))
                    dve.sem_inc(*diff.one())
                    dve.wait_ge(*expd.at(n + 1))
                    if n:
                        dve.wait_ge(*peu.at(n))
                    link(nc.vector.tensor_tensor(flat(qe), flat(q), flat(dec), ALU.mult))
                    dve.sem_inc(*qd.one())
                if n:
                    take(n - 1)
            take(NL - 1)

        @block.scalar
        def _(act):
            for n in range(NL - 1):
                act.wait_ge(*diff.at(n + 1))
                nc.scalar.activation(flat(dec), flat(dec), ACT.Exp).then_inc(*expd.one())

        @block.gpsimd
        def _(pool):
            for n in range(NL - 1):
                pool.wait_ge(*expd.at(n + 1))
                pool.wait_ge(*qd.at(n + 1))
                nc.gpsimd.tensor_tensor(flat(ke), flat(k), flat(dec), ALU.mult).then_inc(*kd.one())

        @block.tensor
        def _(pe):
            for n, L in enumerate(levels):
                ko, qo = (ke, qe) if L else (k, q)
                if L:
                    pe.wait_ge(*qd.at(n + 1))
                    pe.wait_ge(*kd.at(n + 1))
                for h4 in range(4):
                    i = 4 * n + h4
                    if i >= 8:
                        pe.wait_ge(*put.at(i - 7))
                    for t in range(1 if L == P else 2):
                        for e in range(2):
                            h = 2 * h4 + e
                            o = psum[:, i % 8, (2 * t + e) * P:(2 * t + e + 1) * P]
                            ks = ko[:, h, t * P:(t + 1) * P]
                            qs = qo[:, h, P:2 * P] if L == P else qo[:, h, t * P:(t + 1) * P]
                            mm = nc.tensor.matmul(o, ks, qs, start=True, stop=True)
                    mm.then_inc(*prod.one())
                if L:
                    pe.wait_ge(*prod.at(4 * n + 4))
                    pe.sem_inc(*peu.one())

    o = dec
    oacc = sig("hg_out_ready")
    with core.phase() as block:

        @block.tensor
        def _(pe):
            for h in range(HG_H):
                ps = psum[:, h, 0:S]
                nc.tensor.matmul(ps[:, P:S], v[:, 1, h * P:(h + 1) * P], attn1[:, h, :], start=True, stop=False,
                                 skip_group_check=True)
                nc.tensor.matmul(ps, v[:, 0, h * P:(h + 1) * P], attn[:, h, :], start=False, stop=True,
                                 skip_group_check=True).then_inc(*oacc.one())

        @block.scalar
        def _(act):
            for h in range(HG_H):
                act.wait_ge(*oacc.at(h + 1))
                nc.scalar.activation(o[:, h, :], psum[:, h, 0:S], ACT.Copy)

    norm_fm(core, lambda t: o[:, t, :], HG_H, 1, S, lambda t: pr("hg_norm"), lambda t: y_hg[:, t, :],
            gate=lambda t: g[:, t, :])

    mq = view(2 * W8, 2 * ML_H, S)
    vml = view(3 * W8, ST, D)
    go = view(4 * W8, DT, S)
    tmp = view(8 * W8 - 512, 2, S)

    def conv4(w, bias, tmpb):
        def f(dve, link, i, ps):
            t = tmpb[:, i % 2, :]
            link(nc.vector.tensor_scalar(t, ps[:, 0:S], w(3, i), bias(i), ALU.mult, ALU.add))
            for d in (1, 2, 3):
                ins = nc.vector.scalar_tensor_tensor(t[:, d:S], ps[:, 0:S - d], w(3 - d, i), t[:, d:S],
                                                     ALU.mult, ALU.add)
                if d < 3:
                    link(ins)
            return ins
        return f

    project(core, H, S, [512] * 2, DT, on_dve=conv4(lambda kk, i: pr("ml_w", kk * DT + i), lambda i: pr("ml_b", i), tmp),
            then_act=lambda act, i: nc.scalar.activation(mq[:, i, :], tmp[:, i % 2, :], ACT.Silu))
    project(core, H, S, [512] * 2, DT, fm=False, on_act=tm_to(vml))
    project(core, H, S, [512] * 2, DT,
            on_act=lambda act, i, n, j, ps: nc.scalar.activation(go[:, i, :], ps[:, 0:S], ACT.Sigmoid))

    WK = 5 * W8
    gt = view(WK, 12, S)
    gs = sig("gates_steps")
    wg = pv("w_gates", DT)
    ml, mi, md = 0, 1, 2
    with core.phase() as block:

        @block.tensor
        def _(pe):
            for bank, (c, n) in enumerate(((0, 4), (4, 4), (8, 16))):
                for kk in range(DT):
                    mm = nc.tensor.matmul(psum[0:n, bank, 0:S], wg[:, kk, c:c + n], H[:, kk, 0:S],
                                          start=(kk == 0), stop=(kk == DT - 1))
                mm.then_inc(*gs.one())

        @block.scalar
        def _(act):
            link = linker(act, sig("act_chain"))
            act.wait_ge(*gs.at(3))
            link(nc.scalar.activation(gt[0:4, 0, :], psum[0:4, 0, 0:S], ACT.Identity, bias=pr("gate_i")[0:4]))
            link(nc.scalar.activation(gt[0:4, 1, :], psum[0:4, 1, 0:S], ACT.Identity, bias=pr("gate_f")[0:4]))
            link(nc.scalar.activation(gt[0:16, 2, :], psum[0:16, 2, 0:S], ACT.Identity, bias=pr("dt_bias")[0:16]))
            link(nc.scalar.activation(gt[0:4, 3, :], gt[0:4, 1, :], ACT.Abs))
            link(nc.scalar.activation(gt[0:16, 4, :], gt[0:16, 2, :], ACT.Abs))
            link(nc.scalar.activation(gt[0:4, 3, :], gt[0:4, 3, :], ACT.Exp, scale=-1.0))
            link(nc.scalar.activation(gt[0:16, 4, :], gt[0:16, 4, :], ACT.Exp, scale=-1.0))
            link(nc.scalar.activation(small[0:16, 0:1], pr("a_log")[0:16], ACT.Exp))
            link(nc.scalar.activation(gt[0:4, 3, :], gt[0:4, 3, :], ACT.Ln, bias=1.0))
            link(nc.scalar.activation(gt[0:16, 4, :], gt[0:16, 4, :], ACT.Ln, bias=1.0))
            act.sem_inc(*gs.one())

        @block.vector
        def _(dve):
            link = linker(dve, sig("dve_chain"))
            link(nc.vector.memset(gt[0:16, 5, :], 1.0))
            dve.wait_ge(*gs.at(4))
            link(nc.vector.scalar_tensor_tensor(gt[0:4, 1, :], gt[0:4, 1, :], 0.0, gt[0:4, 3, :], ALU.min, ALU.subtract))
            link(nc.vector.tensor_tensor_scan(gt[0:4, 6, :], gt[0:4, 5, :], gt[0:4, 1, :], 0.0, ALU.mult, ALU.add))
            link(nc.vector.tensor_tensor(gt[0:4, 7, :], gt[0:4, 0, :], gt[0:4, 6, :], ALU.subtract))
            link(nc.vector.tensor_tensor_scan(gt[0:4, 8, :], gt[0:4, 7, :], gt[0:4, 7, :], 0.0, ALU.max, ALU.max))
            link(nc.vector.tensor_tensor(gt[0:4, 9, :], gt[0:4, 6, :], gt[0:4, 8, :], ALU.add))
            link(nc.vector.scalar_tensor_tensor(gt[0:16, 2, :], gt[0:16, 2, :], 0.0, gt[0:16, 4, :], ALU.max, ALU.add))
            link(nc.vector.tensor_scalar(gt[0:16, 10, :], gt[0:16, 2, :], small[0:16, 0:1], -1.0, ALU.mult, ALU.mult))
            nc.vector.tensor_tensor_scan(gt[0:16, 11, :], gt[0:16, 5, :], gt[0:16, 10, :], 0.0, ALU.mult, ALU.add)

    cols = core.sbuf("gate_columns", [P, ST, 3, MB_H])
    cs = sig("columns_ready")
    with core.phase() as block:

        @block.tensor
        def _(pe):
            for t in range(ST):
                for i, (r, n) in enumerate(((7, 4), (11, 16), (2, 16))):
                    mm = nc.tensor.transpose(psum[:, 3 * t + i, 0:n], gt[0:n, r, t * P:(t + 1) * P], ident[0:n, 0:n])
                    mm.then_inc(*cs.one())

        @block.vector
        def _(dve):
            dve.wait_ge(*cs.at(6))
            for t in range(ST):
                nc.vector.tensor_copy(cols[:, t, 0, 0:4], psum[:, 3 * t, 0:4])
                nc.vector.tensor_scalar(cols[:, t, 1, :], psum[:, 3 * t + 1, 0:16], -1.0, None, ALU.mult)
                nc.vector.tensor_copy(cols[:, t, 2, :], psum[:, 3 * t + 2, 0:16])

    arg = view(WK + 12 * S, 2, 3 * P)
    wts = view(WK + 12 * S + 6 * P, 2, 3 * P)
    num = H[:, :, S:2 * S]

    def pick(h, n):
        return ident[0:n, h:h + 1].broadcast_to([n, P])

    big = [sig(n) for n in ("ml_scores_ready", "ml_arg_ready", "ml_exp_ready", "ml_weights_ready", "ml_sums_ready",
                            "ml_abs_ready", "ml_head_done")]
    sc, ag, ex, wt, sm, ab, hd = big
    scale = float(P) ** -0.5
    with core.phase() as block:

        @block.tensor
        def _(pe):
            def scores(h):
                if h >= 1:
                    pe.wait_ge(*wt.at(h))
                nc.tensor.matmul(psum[:, 0, 0:S], mq[:, ML_H + h, 0:P], mq[:, h, :], start=True, stop=True)
                nc.tensor.matmul(psum[:, 0, S:3 * P], mq[:, ML_H + h, P:S], mq[:, h, P:S], start=True, stop=True,
                                 skip_group_check=True)
                nc.tensor.matmul(psum[:, 1, 0:S], pick(h, 4), gt[0:4, 8, :], start=True, stop=True)\
                    .then_inc(*sc.one())

            scores(0)
            for h in range(ML_H):
                pe.wait_ge(*wt.at(h + 1))
                if h >= 1:
                    pe.wait_ge(*hd.at(h))
                w = wts[:, h % 2, :]
                for j in range(3):
                    v0 = vml[:, 0, h * 256 + j * P:h * 256 + (j + 1) * P] if j < 2 else core.ones[:, :]
                    v1 = vml[:, 1, h * 256 + j * P:h * 256 + (j + 1) * P] if j < 2 else core.ones[:, :]
                    nc.tensor.matmul(psum[:, 2 + j, P:S], v1, w[:, S:3 * P], start=True, stop=False,
                                     skip_group_check=True)
                    nc.tensor.matmul(psum[:, 2 + j, 0:S], v0, w[:, 0:S], start=False, stop=True,
                                     skip_group_check=True)
                nc.tensor.matmul(psum[:, 5, 0:S], pick(h, 4), gt[0:4, 9, :], start=True, stop=True)\
                    .then_inc(*sm.one())
                if h + 1 < ML_H:
                    scores(h + 1)

        @block.scalar
        def _(act):
            link = linker(act, sig("act_chain"))
            for h in range(ML_H):
                act.wait_ge(*ag.at(h + 1))
                nc.scalar.activation(arg[:, h % 2, :], arg[:, h % 2, :], ACT.Exp).then_inc(*ex.one())
                act.wait_ge(*sm.at(h + 1))
                nc.scalar.activation(core.norm_rt[:, 0:S], psum[:, 4, 0:S], ACT.Abs)
                link(nc.scalar.activation(core.norm_rt[:, S:2 * S], psum[:, 5, 0:S], ACT.Exp, scale=-1.0))
                act.sem_inc(*ab.one())

        @block.vector
        def _(dve):
            link = linker(dve, sig("dve_chain"))
            for h in range(ML_H):
                dve.wait_ge(*sc.at(h + 1))
                ar = arg[:, h % 2, :]
                mt = psum[:, 1, 0:S]
                link(nc.vector.tensor_scalar(ar[:, 0:S], mt, -1.0, cols[:, 0, 0, h:h + 1], ALU.mult, ALU.add))
                link(nc.vector.tensor_scalar(ar[:, S:3 * P], mt[:, P:S], -1.0, cols[:, 1, 0, h:h + 1], ALU.mult, ALU.add))
                link(nc.vector.tensor_scalar(ar[:, :], ar[:, :], 0.0, None, ALU.min))
                dve.sem_inc(*ag.one())
                dve.wait_ge(*ex.at(h + 1))
                dg = ar.rearrange("p (b c) -> p b c", b=3)[:, 0:3:2, :]
                link(nc.vector.tensor_tensor(dg, dg, causal.unsqueeze(1).broadcast_to([P, 2, P]), ALU.mult))
                link(nc.vector.scalar_tensor_tensor(wts[:, h % 2, :], psum[:, 0, 0:3 * P], scale, ar, ALU.mult, ALU.mult))
                dve.sem_inc(*wt.one())
                dve.wait_ge(*ab.at(h + 1))
                rt = core.norm_rt
                link(nc.vector.tensor_tensor(rt[:, 2 * S:3 * S], rt[:, 0:S], rt[:, S:2 * S], ALU.max))
                link(nc.vector.reciprocal(rt[:, 2 * S:3 * S], rt[:, 2 * S:3 * S]))
                for j in range(2):
                    ins = nc.vector.tensor_tensor(num[:, 2 * h + j, :], psum[:, 2 + j, 0:S], rt[:, 2 * S:3 * S], ALU.mult)
                    link(ins)
                dve.sem_inc(*hd.one())

    norm_fm(core, lambda t: num[:, t, :], DT, 2, S, lambda t: pr("ml_norm", t % 2), lambda t: y_ml[:, t, :],
            gate=lambda t: go[:, t, :])

    z = view(2 * W8, DT, S)
    xbc = view(3 * W8, 2 * DT, S)
    XS, BM, CM = 0, DT, DT + MB_G
    tmp2 = core.norm_rt[:, 0:2 * S].rearrange("p (a b) -> p a b", a=2)
    project(core, H, S, [512] * 2, DT, on_act=silu_to(z))
    project(core, H, S, [512] * 4, DT, on_dve=conv4(lambda kk, i: pr("mb_w", kk * 16 + i), lambda i: pr("mb_b", i), tmp2),
            then_act=lambda act, i: nc.scalar.activation(xbc[:, i, :], tmp2[:, i % 2, :], ACT.Silu))

    cbs = view(WK + 12 * S + 12 * P, MB_G, 3 * P)
    tr, trr, cb, cbr = sig("mb_x_turned"), sig("mb_x_read"), sig("mb_cb_ready"), sig("mb_cb_read")
    halves = (H[:, :, S:2 * S], X[:, :, S:2 * S])

    def xh(t, h):
        return halves[t][:, h // 2, (h % 2) * P:(h % 2 + 1) * P]

    with core.phase() as block:

        @block.tensor
        def _(pe):
            for i in range(2 * DT):
                t, j = i // DT, i % DT
                if i >= 4:
                    pe.wait_ge(*trr.at(i - 3))
                nc.tensor.transpose(psum[:, i % 4, 0:P], xbc[:, XS + j, t * P:(t + 1) * P], ident).then_inc(*tr.one())
            for gq in range(MB_G):
                ps = psum[:, 4 + gq, :]
                nc.tensor.matmul(ps[:, 0:S], xbc[:, BM + gq, 0:P], xbc[:, CM + gq, :], start=True, stop=True)
                nc.tensor.matmul(ps[:, S:3 * P], xbc[:, BM + gq, P:S], xbc[:, CM + gq, P:S], start=True, stop=True,
                                 skip_group_check=True).then_inc(*cb.one())

        @block.scalar
        def _(act):
            for gq in range(MB_G):
                act.wait_ge(*cb.at(gq + 1))
                nc.scalar.activation(cbs[:, gq, :], psum[:, 4 + gq, 0:3 * P], ACT.Copy)

        @block.vector
        def _(dve):
            link = linker(dve, sig("dve_chain"))
            for t in range(ST):
                link(nc.vector.memset(halves[t], 0.0))
            for i in range(2 * DT):
                t, j = i // DT, i % DT
                dve.wait_ge(*tr.at(i + 1))
                for e in range(2):
                    ins = nc.vector.tensor_scalar(xh(t, 2 * j + e)[:, e * 64:(e + 1) * 64], psum[:, i % 4, e * 64:(e + 1) * 64],
                                                  cols[:, t, 2, 2 * j + e:2 * j + e + 1], None, ALU.mult)
                link(ins)
                dve.sem_inc(*trr.one())

    yz, ytmp = z, core.norm_rt[:, 0:S]
    bc, ag2, ex2, wt2, ou, our = (sig(n) for n in ("mb_cum_ready", "mb_arg_ready", "mb_exp_ready", "mb_weights_ready",
                                                   "mb_pair_ready", "mb_pair_read"))
    with core.phase() as block:

        @block.tensor
        def _(pe):
            def cum(h):
                if h >= 4:
                    pe.wait_ge(*ag2.at(h - 3))
                nc.tensor.matmul(psum[:, h % 4, 0:S], pick(h, 16), gt[0:16, 11, :], start=True, stop=True)\
                    .then_inc(*bc.one())

            cum(0)
            cum(1)
            for h in range(MB_H):
                if h + 2 < MB_H:
                    cum(h + 2)
                pe.wait_ge(*wt2.at(h + 1))
                j, e = h // 2, h % 2
                if e == 0 and j >= 2:
                    pe.wait_ge(*our.at(j - 1))
                ps = psum[:, 4 + j % 2, 0:S]
                w = wts[:, h % 2, :]
                if e == 0:
                    nc.tensor.matmul(ps, xh(0, h), w[:, 0:S], start=True, stop=False, skip_group_check=True)
                mm = nc.tensor.matmul(ps[:, P:S], xh(1, h), w[:, S:3 * P], start=False, stop=False, skip_group_check=True)
                if e == 1:
                    mm = nc.tensor.matmul(ps, xh(0, h), w[:, 0:S], start=False, stop=True, skip_group_check=True)
                mm.then_inc(*ou.one())

        @block.scalar
        def _(act):
            for h in range(MB_H):
                act.wait_ge(*ag2.at(h + 1))
                nc.scalar.activation(arg[:, h % 2, :], arg[:, h % 2, :], ACT.Exp).then_inc(*ex2.one())

        @block.vector
        def _(dve):
            link = linker(dve, sig("dve_chain"))

            def exponents(h):
                dve.wait_ge(*bc.at(h + 1))
                ar, ps = arg[:, h % 2, :], psum[:, h % 4, 0:S]
                nc.vector.tensor_scalar(ar[:, 0:S], ps, cols[:, 0, 1, h:h + 1], 0.0, ALU.add, ALU.min)
                link(nc.vector.tensor_scalar(ar[:, S:3 * P], ps[:, P:S], cols[:, 1, 1, h:h + 1], 0.0, ALU.add, ALU.min))
                dve.sem_inc(*ag2.one())

            def pair(j):
                dve.wait_ge(*ou.at(2 * j + 2))
                link(nc.vector.scalar_tensor_tensor(ytmp, xbc[:, XS + j, :], pr("mb_d", j), psum[:, 4 + j % 2, 0:S],
                                                    ALU.mult, ALU.add))
                dve.sem_inc(*our.one())
                link(nc.vector.tensor_tensor(yz[:, j, :], ytmp, z[:, j, :], ALU.mult))

            exponents(0)
            for h in range(MB_H):
                if h + 1 < MB_H:
                    exponents(h + 1)
                dve.wait_ge(*ex2.at(h + 1))
                ar = arg[:, h % 2, :]
                dg = ar.rearrange("p (b c) -> p b c", b=3)[:, 0:3:2, :]
                link(nc.vector.tensor_tensor(dg, dg, causal.unsqueeze(1).broadcast_to([P, 2, P]), ALU.mult))
                if h >= 2:
                    dve.wait_ge(*ou.at(h - 1))
                link(nc.vector.tensor_tensor(wts[:, h % 2, :], cbs[:, h // 4, :], ar, ALU.mult))
                dve.sem_inc(*wt2.one())
                if h >= 3 and h % 2 == 1:
                    pair(h // 2 - 1)
            pair(MB_H // 2 - 1)

    norm_fm(core, lambda t: yz[:, t, :], DT, 2, S, lambda t: pr("mb_norm", t), lambda t: y_mb[:, t, :])

    gate, mixed = view(3 * W8, DT, S), view(4 * W8, DT, S)
    tmpm = core.norm_rt[:, 0:S]
    for bi, y in enumerate((y_hg, y_ml, y_mb)):
        project(core, H, S, [512] * 2, DT,
                on_act=lambda act, i, n, j, ps: nc.scalar.activation(gate[:, i, :], ps[:, 0:S], ACT.Sigmoid))

        def gated(dve, link, i, ps, bi=bi):
            if bi == 0:
                return nc.vector.tensor_tensor(mixed[:, i, :], ps[:, 0:S], gate[:, i, :], ALU.mult)
            link(nc.vector.tensor_tensor(tmpm, ps[:, 0:S], gate[:, i, :], ALU.mult))
            return nc.vector.tensor_tensor(mixed[:, i, :], mixed[:, i, :], tmpm, ALU.add)

        project(core, y, S, [512] * 2, DT, on_dve=gated)
    project(core, mixed, S, [512] * 2, DT,
            on_dve=lambda dve, link, i, ps: nc.vector.tensor_tensor(X[:, i, 0:S], ps[:, 0:S], X[:, i, 0:S], ALU.add))


def feed_forward(core, X, H, view, T, gain, shift, cw, cb, lead, scale, ctx_pars=None):
    nc = core.nc
    seg = T // S
    u = view(0, FFT, T)
    tmp = view(FFT * T, 4, T)
    norm_fm(core, lambda t: X[:, t, 0:T], DT, DT, T, gain, lambda t: H[:, t, 0:T],
            shift=shift) if ctx_pars is None else ctx_pars()

    def tile_of(i):
        c, j = i // 4, i % 4
        return (2 * c + j) if j < 2 else (FFT + 2 * c + j - 2)

    def conv3(dve, link, i, ps):
        ch = tile_of(i)
        t = tmp[:, i % 4, :].rearrange("p (s t) -> p s t", s=seg)
        pp = ps[:, 0:T].rearrange("p (s t) -> p s t", s=seg)
        link(nc.vector.tensor_scalar(tmp[:, i % 4, :], ps[:, 0:T], cw(lead, ch), cb(ch), ALU.mult, ALU.add))
        taps = [k for k in range(3) if k != lead]
        for n, k in enumerate(taps):
            d = lead - k
            if d > 0:
                o, s_ = t[:, :, d:S], pp[:, :, 0:S - d]
            else:
                o, s_ = t[:, :, 0:S + d], pp[:, :, -d:S]
            ins = nc.vector.scalar_tensor_tensor(o, s_, cw(k, ch), o, ALU.mult, ALU.add)
            if n == 0:
                link(ins)
        return ins

    up(core, H, T, conv3, tmp, u)
    project(core, u, T, [P] * DT, FFT,
            on_dve=(lambda dve, link, i, ps: nc.vector.tensor_tensor(X[:, i, 0:T], ps[:, 0:T], X[:, i, 0:T], ALU.add))
            if scale is None else scale)


def up(core, H, T, conv3, tmp, u):
    nc = core.nc
    acc, free = core.sig("up_acc_ready"), core.sig("up_bank_free")
    filt, sil = core.sig("up_filtered"), core.sig("up_silu_ready")
    c0 = core.taken
    NC = FFT // 2
    core.taken += NC
    with core.phase() as block:

        @block.sync
        def _(sp):
            for n in range(NC):
                sp.wait_ge(core.used.handle, c0 + n + 1)
                core.load(sp, c0 + n + RING)

        @block.tensor
        def _(pe):
            for n in range(NC):
                c = c0 + n
                w = core.slot(c, DT, 512)
                pe.wait_ge(core.loaded[c % RING].handle, 16 * (c // RING + 1))
                for j in range(4):
                    i = 4 * n + j
                    if i >= 8:
                        pe.wait_ge(*free.at(i - 7))
                    for k in range(DT):
                        mm = nc.tensor.matmul(core.psum[:, i % 8, 0:T], w[:, k, j * P:(j + 1) * P], H[:, k, 0:T],
                                              start=(k == 0), stop=(k == DT - 1))
                    mm.then_inc(*acc.one())
                pe.wait_ge(*acc.at(4 * n + 4))
                pe.sem_inc(*core.used.one())

        @block.vector
        def _(dve):
            link = linker(dve, core.sig("dve_chain"))
            for n in range(NC):
                for j in range(4):
                    i = 4 * n + j
                    dve.wait_ge(*acc.at(i + 1))
                    link(conv3(dve, link, i, core.psum[:, i % 8, :]))
                    dve.sem_inc(*free.one())
                    if j < 2:
                        dve.sem_inc(*filt.one())
                for j in range(2):
                    dve.wait_ge(*sil.at(2 * n + j + 1))
                    link(nc.vector.tensor_tensor(u[:, 2 * n + j, :], tmp[:, j, :], tmp[:, 2 + j, :], ALU.mult))

        @block.scalar
        def _(act):
            for i in range(FFT):
                act.wait_ge(*filt.at(i + 1))
                nc.scalar.activation(tmp[:, i % 2, :], tmp[:, i % 2, :], ACT.Silu).then_inc(*sil.one())


def conditions(core, a, X, pv, cond):
    nc = core.nc
    src = pv("cond", DT)
    ctx_ready = core.sig("context_ready")
    with core.phase() as block:

        @block.sync
        def _(sp):
            sp.dma_start(X[:, :, S:2 * S], a["ctx"].rearrange("(k p) t -> p k t", p=P)).then_inc(*ctx_ready.dma())
            sp.wait_ge(*ctx_ready.at(16))

        @block.scalar
        def _(act):
            nc.scalar.activation(cond[:, :, :], src, ACT.Silu)


def attention_layer(core, a, i, X, H, pr, pv, cn, view, ident, small, adaM, cond):
    nc, sig, psum = core.nc, core.sig, core.psum
    last = i == LAYERS - 1
    lam_init = 0.8 - 0.6 * float(np.exp(-0.3 * i))
    ba = pv(f"b_ada{i}", N_ADA)

    if i == 0:
        norm_fm(core, lambda t: X[:, t, 0:S], DT, DT, S, lambda t: pr("final", t), lambda t: X[:, t, 0:S])

    project(core, cond, 2, [512] * 12, DT,
            on_act=lambda act, n_, n, j, ps: nc.scalar.activation(adaM[:, n_, :], ps[:, 0:2], ACT.Identity,
                                                                  bias=ba[:, n_, 0:1]))
    gains = core.sbuf(f"mod_gains{i}", [P, 2, DT, 2])
    with core.phase() as block:

        @block.vector
        def _(dve):
            link = linker(dve, sig("dve_chain"))
            for half, (name, part) in enumerate(((f"norm1_{i}", 1), (f"norm2_{i}", 4))):
                gcol = pv(name, DT).broadcast_to([P, DT, 2])
                sc_ = adaM[:, part * DT:(part + 1) * DT, :]
                link(nc.vector.tensor_scalar(gains[:, half], sc_, 1.0, None, ALU.add))
                link(nc.vector.tensor_tensor(gains[:, half], gains[:, half], gcol, ALU.mult))

    def modulated(half, T):
        for s_ in range(T // S):
            norm_fm(core, lambda t, s_=s_: X[:, t, s_ * S:(s_ + 1) * S], DT, DT, S,
                    lambda t, s_=s_: gains[:, half, t, s_:s_ + 1],
                    lambda t, s_=s_: H[:, t, s_ * S:(s_ + 1) * S],
                    shift=lambda t, s_=s_: adaM[:, 3 * half * DT + t, s_:s_ + 1])

    modulated(0, 2 * S)

    z = view(0, 4, 2048)
    need = {0: range(4), 1: range(4), 2: range(4), 3: range(4)}
    NT = 4

    def toks(n):
        if not last:
            return 0, 512, range(4)
        if n < 2:
            return 0, 512, range(2)
        if n == 2:
            return 0, 0, {0: (0, 512), 1: (0, 512), 2: (0, 256), 3: (0, 256)}
        return 0, 512, range(4)

    def zout(act, i_, n, j, ps):
        w = 256 if (last and n == 2 and j >= 2) else 512
        f = ACT.Gelu_apprx_tanh if n == 0 else ACT.Copy
        if n == 1:
            return nc.scalar.activation(z[:, j, 512:1024].rearrange("p (h g c) -> p g h c", g=2, h=4),
                                        ps.rearrange("p (g h c) -> p g h c", g=2, h=4), f)
        return nc.scalar.activation(z[:, j, n * 512:n * 512 + w], ps[:, 0:w], f)

    project(core, H, 2 * S, [512] * 4, DT, fm=False, on_act=zout, tok_tiles=toks)

    sq = core.norm_rt
    rs = small
    r2 = core.norm_sq[:, :, :].rearrange("p a b -> p (a b)")
    st = sig("qk_steps")
    lamc = core.sbuf(f"lambda{i}", [P, 4])
    with core.phase() as block:

        @block.scalar
        def _(act):
            link = linker(act, sig("act_chain"))
            act.wait_ge(*st.at(1))
            link(nc.scalar.activation(lamc[:, 0:2], lamc[:, 0:2], ACT.Exp))
            act.sem_inc(*st.one())
            for t in range(NT):
                if t:
                    act.wait_ge(*st.at(2 + 4 * t))
                if last and t >= 2:
                    nc.scalar.activation(sq[:, 768:896], z[:, t, 1024:1152], ACT.Square)
                    link(nc.scalar.activation(sq[:, 1152:1408], z[:, t, 1536:1792], ACT.Square))
                else:
                    nc.scalar.activation(sq[:, 0:896], z[:, t, 256:1152], ACT.Square)
                    link(nc.scalar.activation(sq[:, 896:1408], z[:, t, 1280:1792], ACT.Square))
                act.sem_inc(*st.one())
                act.wait_ge(*st.at(2 + 4 * t + 2))
                lo = 12 if (last and t >= 2) else 0
                nc.scalar.activation(rs[:, lo:14], rs[:, lo:14], ACT.Sqrt, scale=1.0 / 64, bias=core.eps[:, 0:1])
                lo = 22 if (last and t >= 2) else 14
                link(nc.scalar.activation(rs[:, lo:30], rs[:, lo:30], ACT.Sqrt, scale=1.0 / 32, bias=core.eps[:, 0:1]))
                act.sem_inc(*st.one())

        @block.vector
        def _(dve):
            link = linker(dve, sig("dve_chain"))
            lp = pv(f"lam{i}", 4)
            for m in range(2):
                link(nc.vector.tensor_tensor(r2[:, 0:32], lp[:, 2 * m, :], lp[:, 2 * m + 1, :], ALU.mult))
                link(nc.vector.tensor_reduce(lamc[:, m:m + 1], r2[:, 0:32], AX.X, ALU.add))
            dve.sem_inc(*st.one())
            dve.wait_ge(*st.at(2))
            link(nc.vector.tensor_tensor(lamc[:, 2:3], lamc[:, 1:2], lamc[:, 0:1], ALU.subtract))
            link(nc.vector.tensor_scalar(lamc[:, 2:3], lamc[:, 2:3], -lam_init, None, ALU.add))
            for t in range(NT):
                short = last and t >= 2
                b0, b1 = (12, 14) if short else (0, 14)
                c0, c1 = (8, 16) if short else (0, 16)
                dve.wait_ge(*st.at(2 + 4 * t + 1))
                link(nc.vector.tensor_reduce(rs[:, b0:b1], sq[:, b0 * 64:b1 * 64].rearrange("p (g c) -> p g c", c=64), AX.X, ALU.add))
                link(nc.vector.tensor_reduce(rs[:, 14 + c0:14 + c1], sq[:, 896 + c0 * 32:896 + c1 * 32].rearrange("p (g c) -> p g c", c=32), AX.X, ALU.add))
                dve.sem_inc(*st.one())
                dve.wait_ge(*st.at(2 + 4 * t + 3))
                if short:
                    nc.vector.reciprocal(rs[:, 12:14], rs[:, 12:14])
                    link(nc.vector.reciprocal(rs[:, 22:30], rs[:, 22:30]))
                else:
                    link(nc.vector.reciprocal(rs[:, 0:30], rs[:, 0:30]))
                zb = z[:, t, 256 + b0 * 64:256 + b1 * 64]
                zc = z[:, t, 1280 + c0 * 32:1280 + c1 * 32]
                zb3, zc3 = zb.rearrange("p (g c) -> p g c", c=64), zc.rearrange("p (g c) -> p g c", c=32)
                nc.vector.tensor_tensor(zb3, zb3, rs[:, b0:b1].unsqueeze(2).broadcast_to([P, b1 - b0, 64]), ALU.mult)
                link(nc.vector.tensor_tensor(zc3, zc3, rs[:, 14 + c0:14 + c1].unsqueeze(2).broadcast_to([P, c1 - c0, 32]), ALU.mult))
                for o, n, w, gname, go in ((512, 8, 64, "gain_b", 0), (1024, 2, 64, "gain_b", 64),
                                           (1280, 8, 32, "gain_c", 0), (1536, 8, 32, "gain_c", 32)):
                    if not short or o in (1024, 1536):
                        zg = z[:, t, o:o + n * w].rearrange("p (n w) -> p n w", n=n)
                        gv = pr(f"{gname}{i}", go, w).unsqueeze(1).broadcast_to([P, n, w])
                        link(nc.vector.tensor_tensor(zg, zg, gv, ALU.mult))
                if t < 2:
                    for o, n, w, cname, sname in ((512, 10, 64, "cos_b", "sin_b"), (1280, 16, 32, "cos_c", "sin_c")):
                        f = w // 4
                        zz = z[:, t, o:o + n * w]
                        cosv = cn(cname, t * w, w).unsqueeze(1).broadcast_to([P, n, w])
                        sinv = cn(sname, t * w, w).rearrange("p (x e f) -> p x e f", x=2, e=2)
                        m1, m2 = r2[:, 0:n * w], r2[:, 640:640 + n * w]
                        z5 = zz.rearrange("p (n x e f) -> p n x e f", n=n, x=2, e=2)
                        m5 = m2.rearrange("p (n x e f) -> p n x e f", n=n, x=2, e=2)
                        nc.vector.tensor_tensor(m1.rearrange("p (n w) -> p n w", n=n), zz.rearrange("p (n w) -> p n w", n=n), cosv, ALU.mult)
                        for e in range(2):
                            ins = nc.vector.tensor_tensor(m5[:, :, :, e, :], z5[:, :, :, 1 - e, :],
                                                          sinv[:, :, e, :].unsqueeze(1).broadcast_to([P, n, 2, f]), ALU.mult)
                        link(ins)
                        link(nc.vector.tensor_tensor(zz, m1, m2, ALU.add))
                if t < NT - 1:
                    dve.sem_inc(*st.one())

    TT = view(4 * 2048, 9, 512)
    tu, tur = sig("turned"), sig("turned_read")

    def turn_src(j, t):
        if j < 4:
            return z[:, t, 512 + j * P:512 + (j + 1) * P]
        o = {4: 1024, 5: 1280, 6: 1408, 7: 1536, 8: 1664}[j]
        return z[:, t, o:o + P]

    def turn_n(j):
        return 2 if last and j in (0, 1, 2, 3, 5, 6) else 4

    cat = view(4 * 2048 + 9 * 512, 4, 1024)
    NQ = 2 if last else 4
    wsT = pv(f"a_ws{i}", 4)
    gm = sig("gmlp_ready")
    with core.phase() as block:

        @block.tensor
        def _(pe):
            for j in range(9):
                if j >= 4:
                    pe.wait_ge(*tur.at(j - 3))
                for t in range(turn_n(j)):
                    mm = nc.tensor.transpose(psum[:, j % 4, t * P:(t + 1) * P], turn_src(j, t), ident)
                mm.then_inc(*tu.one())
            for t in range(NQ):
                for g_ in range(4):
                    mm = nc.tensor.matmul(psum[:, 4 + t, g_ * 64:(g_ + 1) * 64], wsT[:, g_, :],
                                          z[:, t, 256 + g_ * 64:256 + (g_ + 1) * 64], start=True, stop=True,
                                          skip_group_check=True)
                mm.then_inc(*gm.one())

        @block.scalar
        def _(act):
            for j in range(9):
                n = turn_n(j) * P
                act.wait_ge(*tu.at(j + 1))
                nc.scalar.activation(TT[:, j, 0:n], psum[:, j % 4, 0:n], ACT.Copy).then_inc(*tur.one())

        @block.vector
        def _(dve):
            for t in range(NQ):
                dve.wait_ge(*gm.at(t + 1))
                for g_ in range(4):
                    nc.vector.scalar_tensor_tensor(cat[:, t, g_ * 64:(g_ + 1) * 64], psum[:, 4 + t, g_ * 64:(g_ + 1) * 64],
                                                   pr(f"a_bs{i}", g_), z[:, t, g_ * 64:(g_ + 1) * 64], ALU.add, ALU.mult)

    units = [("B", t, h) for t in range(NQ) for h in range(8)] + [("C", t, h) for t in range(NQ) for h in range(4)]
    E = core.norm_rt[:, :].rearrange("p (u m k) -> p u m k", u=2, m=2)
    ET = core.norm_sq
    cf = small
    scr, mxr, exr, pdr, tp, tpr, ov, ovr = (sig(n) for n in (
        "at_scores_ready", "at_max_ready", "at_exp_ready", "at_probs_ready", "at_turned", "at_turned_read",
        "at_out_ready", "at_out_read"))
    U = len(units)

    def span(u):
        return (0, 512) if units[u][1] < 2 else (S, S)

    def maps(u):
        return 1 if units[u][0] == "B" else 2

    with core.phase() as block:

        @block.tensor
        def _(pe):
            def scores(u):
                kind, t, h = units[u]
                k0, nk = span(u)
                if u >= 2:
                    pe.wait_ge(*exr.at(u - 1))
                for m in range(maps(u)):
                    if kind == "B":
                        r0, r1, jq, jk = 64 * (h // 4), 64 * (h // 4) + 64, h % 4, 4
                    else:
                        r0 = 32 * (2 * (h % 2) + m)
                        r1, jq, jk = r0 + 32, 5 + h // 2, 7 + h // 2
                    mm = nc.tensor.matmul(psum[:, 2 * (u % 2) + m, 0:nk], TT[r0:r1, jq, t * P:(t + 1) * P],
                                          TT[r0:r1, jk, k0:k0 + nk], start=True, stop=True)
                mm.then_inc(*scr.one())

            def turn(u):
                k0, nk = span(u)
                pe.wait_ge(*pdr.at(u + 1))
                if u >= 2:
                    pe.wait_ge(*tpr.at(u - 1))
                for kt in range(nk // P):
                    mm = nc.tensor.transpose(psum[:, 4 + u % 2, kt * P:(kt + 1) * P], E[:, u % 2, 0, kt * P:(kt + 1) * P], ident)
                mm.then_inc(*tp.one())

            def values(u):
                kind, t, h = units[u]
                k0, nk = span(u)
                o = 1152 + 64 * (h // 4) if kind == "B" else 1792 + 64 * h
                pe.wait_ge(*tpr.at(u + 1))
                if u >= 2:
                    pe.wait_ge(*ovr.at(u - 1))
                for kt in range(nk // P):
                    mm = nc.tensor.matmul(psum[:, 6 + u % 2, 0:64], ET[:, u % 4, kt * P:(kt + 1) * P],
                                          z[:, k0 // P + kt, o:o + 64], start=(kt == 0), stop=(kt == nk // P - 1))
                mm.then_inc(*ov.one())

            for u in range(U + 2):
                if u < U:
                    scores(u)
                if 1 <= u <= U:
                    turn(u - 1)
                if u >= 2:
                    values(u - 2)

        @block.scalar
        def _(act):
            link = linker(act, sig("act_chain"))

            def exps(u):
                kind, t, h = units[u]
                _, nk = span(u)
                c = cf[:, 16 * (u % 4):16 * (u % 4) + 16]
                act.wait_ge(*mxr.at(u + 1))
                if u >= 2:
                    act.wait_ge(*tp.at(u - 1))
                if kind == "B":
                    nc.scalar.activation(c[:, 3:4], pr(f"sink{i}", h), ACT.Exp, bias=c[:, 2:3])
                    link(nc.scalar.activation(E[:, u % 2, 0, 0:nk], E[:, u % 2, 1, 0:nk], ACT.Exp, bias=c[:, 2:3],
                                              accum_out=c[:, 4:5]))
                else:
                    nc.scalar.activation(E[:, u % 2, 0, 0:nk], psum[:, 2 * (u % 2), 0:nk], ACT.Exp, bias=c[:, 2:3],
                                         scale=32 ** -0.5, accum_out=c[:, 4:5])
                    link(nc.scalar.activation(E[:, u % 2, 1, 0:nk], psum[:, 2 * (u % 2) + 1, 0:nk], ACT.Exp,
                                              bias=c[:, 3:4], scale=32 ** -0.5, accum_out=c[:, 5:6]))
                act.sem_inc(*exr.one())

            def read_turned(u):
                _, nk = span(u)
                act.wait_ge(*tp.at(u + 1))
                if u >= 4:
                    act.wait_ge(*ov.at(u - 3))
                nc.scalar.activation(ET[:, u % 4, 0:nk], psum[:, 4 + u % 2, 0:nk], ACT.Copy).then_inc(*tpr.one())

            for u in range(U + 1):
                if u < U:
                    exps(u)
                if u >= 1:
                    read_turned(u - 1)

        @block.vector
        def _(dve):
            link = linker(dve, sig("dve_chain"))

            def maxima(u):
                kind, t, h = units[u]
                _, nk = span(u)
                c = cf[:, 16 * (u % 4):16 * (u % 4) + 16]
                dve.wait_ge(*scr.at(u + 1))
                if kind == "B":
                    if u >= 2:
                        dve.wait_ge(*exr.at(u - 1))
                    mask = cn("window", t * BANK, BANK) if t < 2 else None
                    so = E[:, u % 2, 1, 0:nk]
                    if mask is not None:
                        link(nc.vector.scalar_tensor_tensor(so, psum[:, 2 * (u % 2), 0:nk], 0.125, mask, ALU.mult, ALU.add))
                    else:
                        link(nc.vector.tensor_scalar(so, psum[:, 2 * (u % 2), 0:nk], 0.125, None, ALU.mult))
                    link(nc.vector.tensor_reduce(c[:, 0:1], so, AX.X, ALU.max))
                    link(nc.vector.tensor_scalar(c[:, 2:3], c[:, 0:1], pr(f"sink{i}", h), -1.0, ALU.max, ALU.mult))
                else:
                    for m in range(2):
                        link(nc.vector.tensor_reduce(c[:, m:m + 1], psum[:, 2 * (u % 2) + m, 0:nk], AX.X, ALU.max))
                    link(nc.vector.tensor_scalar(c[:, 2:4], c[:, 0:2], -(32 ** -0.5), None, ALU.mult))
                dve.sem_inc(*mxr.one())

            def weigh(u):
                kind, t, h = units[u]
                _, nk = span(u)
                c = cf[:, 16 * (u % 4):16 * (u % 4) + 16]
                dve.wait_ge(*exr.at(u + 1))
                if kind == "B":
                    link(nc.vector.tensor_tensor(c[:, 6:7], c[:, 3:4], c[:, 4:5], ALU.add))
                    link(nc.vector.reciprocal(c[:, 7:8], c[:, 6:7]))
                else:
                    link(nc.vector.reciprocal(c[:, 6:8], c[:, 4:6]))
                    link(nc.vector.tensor_scalar(c[:, 8:9], c[:, 7:8], lamc[:, 2:3], None, ALU.mult))
                    link(nc.vector.tensor_scalar(E[:, u % 2, 0, 0:nk], E[:, u % 2, 0, 0:nk], c[:, 6:7], None, ALU.mult))
                    link(nc.vector.scalar_tensor_tensor(E[:, u % 2, 0, 0:nk], E[:, u % 2, 1, 0:nk], c[:, 8:9],
                                                        E[:, u % 2, 0, 0:nk], ALU.mult, ALU.add))
                dve.sem_inc(*pdr.one())

            def result(u):
                kind, t, h = units[u]
                c = cf[:, 16 * (u % 4):16 * (u % 4) + 16]
                dve.wait_ge(*ov.at(u + 1))
                ps = psum[:, 6 + u % 2, 0:64]
                if kind == "B":
                    link(nc.vector.tensor_scalar(cat[:, t, 256 + 64 * h:320 + 64 * h], ps, c[:, 7:8], None, ALU.mult))
                else:
                    link(nc.vector.tensor_copy(cat[:, t, 768 + 64 * h:832 + 64 * h], ps))
                dve.sem_inc(*ovr.one())

            for u in range(U + 2):
                if u < U:
                    maxima(u)
                if 1 <= u <= U:
                    weigh(u - 1)
                if u >= 2:
                    result(u - 2)

    ns = sig("subln_steps")
    with core.phase() as block:

        @block.scalar
        def _(act):
            act.wait_ge(*ns.at(1))
            nc.scalar.activation(small[:, 0:4 * NQ], small[:, 0:4 * NQ], ACT.Sqrt, scale=1.0 / 64, bias=core.eps[:, 0:1])\
                .then_inc(*ns.one())

        @block.vector
        def _(dve):
            link = linker(dve, sig("dve_chain"))
            cc = cat[:, 0:NQ, 768:1024]
            s3 = core.norm_rt[:, 0:NQ * 256].rearrange("p (t c) -> p t c", t=NQ)
            link(nc.vector.tensor_tensor(s3, cc, cc, ALU.mult))
            link(nc.vector.tensor_reduce(small[:, 0:4 * NQ], core.norm_rt[:, 0:NQ * 256].rearrange("p (g c) -> p g c", c=64),
                                         AX.X, ALU.add))
            dve.sem_inc(*ns.one())
            dve.wait_ge(*ns.at(2))
            link(nc.vector.reciprocal(small[:, 0:4 * NQ], small[:, 0:4 * NQ]))
            link(nc.vector.tensor_scalar(small[:, 0:4 * NQ], small[:, 0:4 * NQ], 1.0 - lam_init, None, ALU.mult))
            for t in range(NQ):
                c3 = cat[:, t, 768:1024].rearrange("p (h c) -> p h c", h=4)
                link(nc.vector.tensor_tensor(c3, c3, small[:, 4 * t:4 * t + 4].unsqueeze(2).broadcast_to([P, 4, 64]), ALU.mult))
                link(nc.vector.tensor_tensor(c3, c3, pr(f"subln{i}", 0, 64).unsqueeze(1).broadcast_to([P, 4, 64]), ALU.mult))

    catT = view(0, DT, 512)
    ct, ctr = sig("cat_turned"), sig("cat_read")
    T = NQ * P
    with core.phase() as block:

        @block.tensor
        def _(pe):
            for j in range(DT):
                for t in range(NQ):
                    mm = nc.tensor.transpose(psum[:, j, t * P:(t + 1) * P], cat[:, t, j * P:(j + 1) * P], ident)
                mm.then_inc(*ct.one())

        @block.scalar
        def _(act):
            for j in range(DT):
                act.wait_ge(*ct.at(j + 1))
                nc.scalar.activation(catT[:, j, 0:T], psum[:, j, 0:T], ACT.Copy)

    def residual(part):
        def f(dve, link, n_, ps):
            for s_ in range(T // S):
                ins = nc.vector.scalar_tensor_tensor(X[:, n_, s_ * S:(s_ + 1) * S], ps[:, s_ * S:(s_ + 1) * S],
                                                     adaM[:, part * DT + n_, s_:s_ + 1], X[:, n_, s_ * S:(s_ + 1) * S],
                                                     ALU.mult, ALU.add)
                if s_ < T // S - 1:
                    link(ins)
            return ins
        return f

    project(core, catT, T, [512] * 2, DT, on_dve=residual(2))
    feed_forward(core, X, H, view, T, None, None, lambda k, t: pr(f"cw{i}", k * 44 + t), lambda t: pr(f"cb{i}", t), 1,
                 residual(5), ctx_pars=lambda: modulated(1, T))


def constants():
    con = {}
    con["ident"] = np.eye(P, dtype=np.float32)
    s, t = np.meshgrid(np.arange(P), np.arange(P), indexing="ij")
    con["causal"] = (s <= t).astype(np.float32)
    win = np.zeros((P, 2, BANK), np.float32)
    for qt in range(2):
        qpos, kpos = qt * P + np.arange(P)[:, None], np.arange(S)[None, :]
        win[:, qt, 0:S] = np.where(np.abs(qpos - kpos) <= P, 0.0, -1e30)
    con["window"] = win.reshape(P, -1)
    for name, w in (("b", 64), ("c", 32)):
        nf = w // 4
        row, col = np.repeat(np.arange(S // 64), 64), np.tile(np.arange(64), S // 64)
        inv = (np.float32(10000.0) ** (-np.arange(nf, dtype=np.float32) / np.float32(nf))).astype(np.float32)
        ang = np.stack([row[:, None].astype(np.float32) * inv, col[:, None].astype(np.float32) * inv], axis=1)
        cos, sin = np.cos(ang).astype(np.float32), np.sin(ang).astype(np.float32)
        cos2 = np.stack([cos, cos], axis=2).reshape(2, P, w)
        sin2 = np.stack([-sin, sin], axis=2).reshape(2, P, w)
        con["cos_" + name] = cos2.transpose(1, 0, 2).reshape(P, -1)
        con["sin_" + name] = sin2.transpose(1, 0, 2).reshape(P, -1)
    lev = np.zeros((P, len(LEVELS) + 1, P), np.uint32)
    for n, L in enumerate(LEVELS):
        lev[:, n] = ((s // L) % 2 == 0) & (t // L == s // L + 1)
    lev[:, -1] = s == t
    return np.concatenate([con[n] for n, _ in CONS], axis=1), lev.reshape(P, -1)


def columns(v):
    v = np.asarray(v)
    return v.reshape(-1, P).T


def chunked(w, cols=512):
    w = np.asarray(w)
    w = w.reshape(-1, w.shape[-2], w.shape[-1])
    L, K, N = w.shape
    w = w.reshape(L, K // P, P, N // cols, cols).transpose(0, 3, 2, 1, 4)
    return np.ascontiguousarray(w).reshape(L * (N // cols), P, -1)


def paired(w):
    w = np.asarray(w)
    w = w.reshape(-1, D, 2, FFT // 2, 256).transpose(0, 1, 3, 2, 4)
    return chunked(np.ascontiguousarray(w).reshape(-1, D, 2 * FF))


def lay_out(i):
    w_in = np.asarray(i["w_in"])[0]
    big = np.concatenate([w_in[:, 0:6144], w_in[:, 6152:7176], w_in[:, 7176:10248], w_in[:, 10264:]], axis=1)
    small_w = np.concatenate([w_in[:, 6144:6152], w_in[:, 10248:10264]], axis=1)
    pad = lambda v: np.concatenate([np.asarray(v).reshape(-1), np.zeros(P - np.asarray(v).size, np.float32)])[:, None]
    rows = lambda v: np.broadcast_to(np.asarray(v).reshape(1, -1), (P, np.asarray(v).size))
    taps = lambda w: np.concatenate([columns(r) for r in np.asarray(w)], axis=1)
    gb = np.asarray(i["ml_gate_b"])[0]
    p = {
        "norm1": columns(i["norm1_g"][0]), "hg_norm": columns(i["hg_norm_g"][0]), "ml_w": taps(i["ml_conv_w"][0]),
        "ml_b": columns(i["ml_conv_b"][0]), "ml_norm": columns(i["ml_norm_g"][0]), "mb_w": taps(i["mb_conv_w"][0]),
        "mb_b": columns(i["mb_conv_b"][0]), "mb_norm": columns(i["mb_norm_g"][0]), "norm2": columns(i["norm2_g"][0]),
        "ff_w": taps(i["ffn_conv_w"][0]), "ff_b": columns(i["ffn_conv_b"][0]), "final": columns(i["final_g"]),
        "mb_d": columns(np.repeat(np.asarray(i["mb_d"])[0], MB_P)),
        "gate_i": pad(gb[:ML_H]), "gate_f": pad(gb[ML_H:]), "dt_bias": pad(i["mb_dt_bias"]), "a_log": pad(i["mb_a_log"]),
        "w_gates": small_w.reshape(DT, P, 24).transpose(1, 0, 2).reshape(P, -1),
        "cond": np.stack([columns(i["c_2"][0]), columns(i["c_ctx_2"])], axis=2).reshape(P, -1),
    }
    for n in range(LAYERS):
        bq, bk = np.asarray(i["b_qnorm_2"])[n], np.asarray(i["b_knorm_2"])[n]
        cq, ck = np.asarray(i["c_qnorm_2"])[n], np.asarray(i["c_knorm_2"])[n]
        p |= {
            f"norm1_{n}": columns(i["norm1_g_2"][n]), f"norm2_{n}": columns(i["norm2_g_2"][n]),
            f"b_ada{n}": columns(i["b_ada_2"][n]), f"cw{n}": taps(i["conv_w_2"][n][:, 0]), f"cb{n}": columns(i["conv_b_2"][n]),
            f"a_bs{n}": np.asarray(i["a_bs_2"])[n].T,
            f"a_ws{n}": np.asarray(i["a_ws_2"])[n].transpose(2, 0, 1).reshape(P, -1),
            f"gain_b{n}": rows(np.concatenate([bq, bk])),
            f"gain_c{n}": rows(np.concatenate([cq, ck])),
            f"subln{n}": rows(i["c_subln_2"][n]), f"sink{n}": rows(i["b_sink_2"][n]), f"lam{n}": rows(i["c_lam_2"][n]),
        }
    con, lev = constants()
    return {
        "x": np.asarray(i["x"])[0].T, "ctx": np.asarray(i["ctx_2"])[0].T,
        "par": np.concatenate([p[n] for n, _ in PARS], axis=1), "con": con, "levels": lev,
        "w_in": chunked(big), "w_br_hg": chunked(i["w_br_hg"]), "w_br_ml": chunked(i["w_br_ml"]),
        "w_br_mb": chunked(i["w_br_mb"]), "w_out": chunked(i["w_out"]), "w_up": paired(i["w_up"]),
        "w_down": chunked(i["w_down"], P), "w_ada_2": chunked(i["w_ada_2"]), "w_in_2": chunked(i["w_in_2"]),
        "w_out_2": chunked(i["w_out_2"]), "w_up_2": paired(i["w_up_2"]), "w_down_2": chunked(i["w_down_2"], P),
    }


def kernel(**inputs):
    import concourse.bacc as bacc
    from concourse.bass_utils import run_bass_kernel_spmd

    nc = bacc.Bacc("TRN2", target_bir_lowering=False, num_devices=1)
    arrays, aps = {}, {}
    for name, v in lay_out(inputs).items():
        v = np.ascontiguousarray(v)
        arrays[f"in_{name}"] = v
        aps[name] = nc.dram_tensor(f"in_{name}", v.shape, mybir.dt.from_np(v.dtype), kind="ExternalInput").ap()
    out = nc.dram_tensor("out", (D, S), F32, kind="ExternalOutput").ap()
    build(nc, aps, out)
    r = run_bass_kernel_spmd(nc, [arrays], core_ids=[0])
    return np.ascontiguousarray(r.results[0]["out"].T).reshape(1, S, D)
```

```python
from contextlib import ExitStack, contextmanager

import numpy as np

import concourse.bass as bass
from concourse import mybir

F32 = mybir.dt.float32
U32 = mybir.dt.uint32
ALU = mybir.AluOpType
ACT = mybir.ActivationFunctionType
AX = mybir.AxisListType

P = 128
D = 1024
DT = D // P
S = 256
ST = S // P
EPS = 1e-6

HG_H = 8
ML_H, ML_DV = 4, 256
MB_H, MB_P, MB_G = 16, 64, 4
FF = 2816
FFT = FF // P
N_ADA = 6 * DT
RING = 3
SLOT = DT * 512
BANK = 512
LEVELS = [64, 32, 16, 8, 4, 2, 1]
LAYERS = 2


class Signal:

    def __init__(self, handle):
        self.handle, self.base, self.total = handle, 0, 0

    def one(self):
        self.total += 1
        return self.handle, 1

    def dma(self):
        self.total += 16
        return self.handle, 16

    def at(self, n):
        return self.handle, self.base + n


class Core:

    def __init__(self, nc, ctx):
        self.nc, self.ctx, self.signals = nc, ctx, {}
        self.psum = ctx.enter_context(nc.psum_tensor("acc_psum", [P, 8, BANK], F32))
        self.ring = self.sbuf("ring", [P, RING, SLOT])
        self.loaded = [self.sig(f"weights_loaded_{i}") for i in range(RING)]
        self.chunks, self.taken = [], 0

    def sbuf(self, name, shape, dt=F32):
        return self.ctx.enter_context(self.nc.sbuf_tensor(name + "_sb", shape, dt))

    def sig(self, name):
        if name not in self.signals:
            self.signals[name] = Signal(self.ctx.enter_context(self.nc.semaphore(name)))
        return self.signals[name]

    @contextmanager
    def phase(self):
        with self.nc.Block() as block:
            yield block
        for s in self.signals.values():
            s.base = s.total

    def slot(self, c, kt, n):
        return self.ring[:, c % RING, 0:kt * n].rearrange("p (k n) -> p k n", k=kt)

    def load(self, sp, c):
        if c < len(self.chunks):
            src = self.chunks[c]
            sp.dma_start(self.ring[:, c % RING, 0:src.shape[1]], src).then_inc(*self.loaded[c % RING].dma())


def linker(eng, signal):
    start = signal.total

    def link(ins):
        ins.then_inc(*signal.one())
        eng.wait_ge(*signal.at(signal.total - signal.base))
        return ins

    return link


class Modulation:

    def __init__(self, core, cond, bias, result, sums):
        self.core, self.cond, self.bias, self.result, self.sums = core, cond, bias, result, sums
        self.taken = 0
        self.scaled, self.summed = core.sig("mod_scaled"), core.sig("mod_summed")

    def scale(self, dve, link, n, slot):
        nc = self.core.nc
        if n >= 2:
            dve.wait_ge(*self.summed.at(n - 1))
        for k in range(DT):
            for s in range(2):
                dst, c = self.sums[:, n % 2, s, :], self.cond[:, k, s:s + 1]
                if k == 0:
                    ins = nc.vector.tensor_scalar(dst, slot[:, k, :], c, None, ALU.mult)
                else:
                    ins = nc.vector.scalar_tensor_tensor(dst, slot[:, k, :], c, dst, ALU.mult, ALU.add)
            link(ins)
        dve.sem_inc(*self.scaled.one())

    def reduce(self, pe, n, m):
        nc = self.core.nc
        pe.wait_ge(*self.scaled.at(n + 1))
        for j in range(4):
            for s in range(2):
                o = 2 * (4 * m + j) + s
                mm = nc.tensor.matmul(self.core.psum[:, 7, o:o + 1], self.sums[:, n % 2, s, j * P:(j + 1) * P],
                                      self.core.ones[:, 0:1], start=True, stop=True)
        mm.then_inc(*self.summed.one())

    def read(self, dve, n, m0):
        nc = self.core.nc
        dve.wait_ge(*self.summed.at(n))
        t0, t1 = 4 * m0, 4 * (m0 + n)
        ps = self.core.psum[:, 7, 2 * t0:2 * t1].rearrange("p (t s) -> p t s", s=2)
        nc.vector.tensor_tensor(self.result[:, t0:t1, :], ps, self.bias[:, t0:t1, :].broadcast_to([P, t1 - t0, 2]), ALU.add)


def project(core, x, T, widths, kt, fm=True, on_act=None, on_dve=None, then_act=None, tok_tiles=None, side=None):
    nc = core.nc
    acc, free = core.sig("proj_acc_ready"), core.sig("proj_bank_free")
    mid, midfree = core.sig("proj_mid_ready"), core.sig("proj_mid_free")
    c0 = core.taken
    N = len(widths)
    per = 2 if side else 1
    core.taken += per * N
    m0 = 0
    if side:
        m0 = side.taken
        side.taken += N
    tiles = []
    for n, w in enumerate(widths):
        if fm:
            tiles += [(n, j, 0, 0) for j in range(w // P)]
        else:
            first, cols, toks = tok_tiles(n) if tok_tiles else (0, w, range(ST))
            if isinstance(toks, dict):
                tiles += [(n, t, *fc) for t, fc in toks.items()]
            else:
                tiles += [(n, t, first, cols) for t in toks]
    last_of = {n: i for i, (n, *_) in enumerate(tiles)}
    BANKS = 7 if side else 8

    def bank(i):
        return core.psum[:, i % BANKS, :]

    with core.phase() as block:

        @block.sync
        def _(sp):
            for n in range(N):
                sp.wait_ge(*acc.at(last_of[n] + 1))
                core.load(sp, c0 + per * n + RING)
                if side:
                    sp.wait_ge(*side.scaled.at(n + 1))
                    core.load(sp, c0 + per * n + 1 + RING)

        @block.tensor
        def _(pe):
            for i, (n, j, first, cols) in enumerate(tiles):
                c = c0 + per * n
                w = core.slot(c, kt, widths[n])
                if i == 0 or tiles[i - 1][0] != n:
                    pe.wait_ge(core.loaded[c % RING].handle, 16 * (c // RING + 1))
                if i >= BANKS:
                    pe.wait_ge(*free.at(i - BANKS + 1))
                for k in range(kt):
                    if fm:
                        mm = nc.tensor.matmul(bank(i)[:, 0:T], w[:, k, j * P:(j + 1) * P], x[:, k, 0:T],
                                              start=(k == 0), stop=(k == kt - 1))
                    else:
                        mm = nc.tensor.matmul(bank(i)[:, 0:cols], x[:, k, j * P:(j + 1) * P],
                                              w[:, k, first:first + cols], start=(k == 0), stop=(k == kt - 1))
                mm.then_inc(*acc.one())
                if side and i == last_of[n] and n:
                    side.reduce(pe, n - 1, m0 + n - 1)
            if side:
                side.reduce(pe, N - 1, m0 + N - 1)

        if on_act or then_act:
            @block.scalar
            def _(act):
                for i, (n, j, first, cols) in enumerate(tiles):
                    if on_act:
                        act.wait_ge(*acc.at(i + 1))
                        on_act(act, i, n, j, bank(i)).then_inc(*free.one())
                    else:
                        act.wait_ge(*mid.at(i + 1))
                        then_act(act, i).then_inc(*midfree.one())

        if on_dve:
            @block.vector
            def _(dve):
                link = linker(dve, core.sig("dve_chain"))
                for i, (n, j, first, cols) in enumerate(tiles):
                    dve.wait_ge(*acc.at(i + 1))
                    if then_act and i >= 2:
                        dve.wait_ge(*midfree.at(i - 1))
                    link(on_dve(dve, link, i, bank(i)))
                    dve.sem_inc(*free.one())
                    if then_act:
                        dve.sem_inc(*mid.one())

        elif side:
            @block.vector
            def _(dve):
                link = linker(dve, core.sig("dve_chain"))
                for n in range(N):
                    c = c0 + per * n + 1
                    dve.wait_ge(core.loaded[c % RING].handle, 16 * (c // RING + 1))
                    side.scale(dve, link, n, core.slot(c, DT, 512))
                side.read(dve, N, m0)


def norm_fm(core, src, ntile, m, W, gain, out, shift=None, gate=None):
    nc = core.nc
    sq_ready, sq_used, root = core.sig("norm_sq_ready"), core.sig("norm_sq_used"), core.sig("norm_root_ready")
    groups = ntile // m
    NSQ = 4
    sq = core.norm_sq
    rt = core.norm_rt[:, 0:groups * W].rearrange("p (g w) -> p g w", g=groups)
    with core.phase() as block:

        @block.scalar
        def _(act):
            for t in range(ntile):
                if t >= NSQ:
                    act.wait_ge(*sq_used.at(t - NSQ + 1))
                nc.scalar.activation(sq[:, t % NSQ, 0:W], src(t), ACT.Square).then_inc(*sq_ready.one())
            for g in range(groups):
                act.wait_ge(*sq_used.at((g + 1) * m))
                nc.scalar.activation(rt[:, g, :], core.psum[:, g, 0:W], ACT.Sqrt, scale=1.0 / (P * m),
                                     bias=core.eps[:, 0:1]).then_inc(*root.one())

        @block.tensor
        def _(pe):
            for t in range(ntile):
                pe.wait_ge(*sq_ready.at(t + 1))
                nc.tensor.matmul(core.psum[:, t // m, 0:W], core.ones[:, :], sq[:, t % NSQ, 0:W],
                                 start=(t % m == 0), stop=(t % m == m - 1)).then_inc(*sq_used.one())

        @block.vector
        def _(dve):
            link = linker(dve, core.sig("dve_chain"))
            for g in range(groups):
                dve.wait_ge(*root.at(g + 1))
                link(nc.vector.reciprocal(rt[:, g, :], rt[:, g, :]))
                for t in range(g * m, g * m + m):
                    ins = nc.vector.scalar_tensor_tensor(out(t), src(t), gain(t), rt[:, g, :], ALU.mult, ALU.mult)
                    if gate:
                        link(ins)
                        nc.vector.tensor_tensor(out(t), out(t), gate(t), ALU.mult)
                    if shift:
                        link(ins)
                        nc.vector.tensor_scalar(out(t), out(t), shift(t), None, ALU.add)


def pack_columns(items):
    at, n = {}, 0
    for name, w in items:
        at[name] = (n, w)
        n += w
    return at, n


PARS = [("norm1", DT), ("hg_norm", 1), ("ml_w", 4 * DT), ("ml_b", DT), ("ml_norm", 2), ("mb_w", 4 * 16),
        ("mb_b", 16), ("mb_norm", DT), ("norm2", DT), ("ff_w", 3 * 44), ("ff_b", 44), ("final", DT), ("mb_d", DT),
        ("gate_i", 1), ("gate_f", 1), ("dt_bias", 1), ("a_log", 1), ("w_gates", DT * 24), ("cond", 2 * DT)]
for _i in range(LAYERS):
    PARS += [(f"{n}{_i}", w) for n, w in (
        ("norm1_", DT), ("norm2_", DT), ("b_ada", N_ADA), ("cw", 132), ("cb", 44), ("a_bs", 4), ("a_ws", 512),
        ("gain_b", 128), ("gain_c", 64), ("subln", 64), ("sink", 8), ("lam", 128))]
PAR_AT, PAR_N = pack_columns(PARS)
CONS = [("ident", P), ("causal", P), ("window", 2 * BANK), ("cos_b", 2 * 64), ("sin_b", 2 * 64),
        ("cos_c", 2 * 32), ("sin_c", 2 * 32)]
CON_AT, CON_N = pack_columns(CONS)
LEV_N = (len(LEVELS) + 1) * P


def build(nc, a, out):
    with ExitStack() as ctx:
        core = Core(nc, ctx)
        sb, sig = core.sbuf, core.sig
        par = sb("par", [P, PAR_N])
        con = sb("con", [P, CON_N])
        X = sb("X", [P, DT, 2 * S])
        H = sb("H", [P, DT, 2 * S])
        core.ones = sb("ones", [P, P])
        core.eps = sb("eps", [P, 1])
        core.norm_sq = sb("norm_sq", [P, 4, 512])
        core.norm_rt = sb("norm_rt", [P, 2048])
        adaM = [sb(f"modulation{i}", [P, N_ADA, 2]) for i in range(LAYERS)]
        cond = sb("cond", [P, DT, 2])
        mod_sums = sb("mod_sums", [P, 2, 2, 512])
        small = sb("small", [P, 64])
        ARENA = 17600
        arena = sb("arena", [P, ARENA])

        def pr(name, i=0, n=1):
            o = PAR_AT[name][0] + i
            return par[:, o:o + n]

        def pv(name, a_):
            o, w = PAR_AT[name]
            return par[:, o:o + w].rearrange("p (a b) -> p a b", a=a_)

        def cn(name, i=0, n=None):
            o, w = CON_AT[name]
            return con[:, o + i:o + i + (w if n is None else n)]

        def view(o, a_, b_):
            assert o + a_ * b_ <= ARENA, (o, a_, b_)
            return arena[:, o:o + a_ * b_].rearrange("p (a b) -> p a b", a=a_)

        ident = cn("ident")
        causal = cn("causal")

        plan = []

        def add(name, idx, layer=None):
            for n in idx:
                plan.append(a[name][n])
                if layer is not None:
                    plan.append(a["w_ada_2"][12 * layer + counts[layer]])
                    counts[layer] += 1

        counts = [0, 0]
        add("w_in", range(0, 8), 0)
        add("w_in", range(8, 10))
        add("w_in", range(10, 14), 0)
        add("w_in", range(14, 16), 1)
        add("w_in", range(16, 20))
        for b, name in enumerate(("w_br_hg", "w_br_ml", "w_br_mb")):
            add("w_in", range(20 + 2 * b, 22 + 2 * b), 1)
            add(name, range(2))
        add("w_out", range(2))
        add("w_up", range(11))
        add("w_down", range(8))
        for i in range(LAYERS):
            add("w_in_2", range(4 * i, 4 * i + 4), 1 if i == 0 else None)
            add("w_out_2", range(2 * i, 2 * i + 2))
            add("w_up_2", range(11 * i, 11 * i + 11))
            add("w_down_2", range(8 * i, 8 * i + 8))
        core.chunks = plan

        in_ready = sig("inputs_ready")
        with core.phase() as block:

            @block.sync
            def _(sp):
                sp.dma_start(X[:, :, 0:S], a["x"].rearrange("(k p) t -> p k t", p=P)).then_inc(*in_ready.dma())
                sp.dma_start(par[:, :], a["par"]).then_inc(*in_ready.dma())
                sp.dma_start(con[:, :], a["con"]).then_inc(*in_ready.dma())
                for c in range(RING):
                    core.load(sp, c)
                sp.wait_ge(*in_ready.at(48))

            @block.vector
            def _(dve):
                nc.vector.memset(core.ones[:, :], 1.0)
                nc.vector.memset(core.eps[:, :], EPS)

            @block.scalar
            def _(act):
                act.wait_ge(*in_ready.at(48))
                nc.scalar.activation(cond[:, :, :], pv("cond", DT), ACT.Silu)

        mods = [Modulation(core, cond, pv(f"b_ada{i}", N_ADA), adaM[i], mod_sums) for i in range(LAYERS)]
        hybrid_block(core, a, X, H, pr, pv, cn, view, ident, causal, small, mods)
        feed_forward(core, X, H, view, S, lambda t: pr("norm2", t), None,
                     lambda k, t: pr("ff_w", k * 44 + t), lambda t: pr("ff_b", t), 2, None)
        load_context(core, a, X)
        for i in range(LAYERS):
            attention_layer(core, a, i, X, H, pr, pv, cn, view, ident, small, adaM[i], mods[1] if i == 0 else None)
        stored = sig("output_stored")
        with core.phase() as block:

            @block.sync
            def _(sp):
                sp.dma_start(out.rearrange("(k p) t -> p k t", p=P), X[:, :, 0:S]).then_inc(*stored.dma())
                sp.wait_ge(*stored.at(16))


def hybrid_block(core, a, X, H, pr, pv, cn, view, ident, causal, small, mods):
    nc, sig, psum = core.nc, core.sig, core.psum
    W8 = DT * S
    y_hg, y_ml, y_mb = view(0, DT, S), view(W8, DT, S), view(2 * W8, DT, S)

    norm_fm(core, lambda t: X[:, t, 0:S], DT, DT, S, lambda t: pr("norm1", t), lambda t: H[:, t, 0:S])

    q, k, b = view(0, HG_H, S), view(W8, HG_H, S), view(2 * W8, HG_H, S)
    v = view(3 * W8, ST, D)
    g = view(4 * W8, HG_H, S)
    dec = view(5 * W8, HG_H, S)
    qe, ke = view(6 * W8, HG_H, S), view(7 * W8, HG_H, S)

    def silu_to(dst):
        return lambda act, i, n, j, ps: nc.scalar.activation(dst[:, i, :], ps[:, 0:S], ACT.Silu)

    def copy_to(dst):
        return lambda act, i, n, j, ps: nc.scalar.activation(dst[:, i, :], ps[:, 0:S], ACT.Copy)

    def tm_to(dst):
        return lambda act, i, n, j, ps: nc.scalar.activation(dst[:, j, n * 512:(n + 1) * 512], ps[:, :], ACT.Copy)

    project(core, H, S, [512] * 2, DT, on_act=silu_to(q), side=mods[0])
    project(core, H, S, [512] * 2, DT, on_act=copy_to(k), side=mods[0])
    project(core, H, S, [512] * 2, DT, fm=False, on_act=tm_to(v), side=mods[0])
    project(core, H, S, [512] * 2, DT, on_act=silu_to(g), side=mods[0])

    steps = sig("hg_gate_steps")
    flat = lambda t: t.rearrange("p a b -> p (a b)")
    with core.phase() as block:

        @block.scalar
        def _(act):
            link = linker(act, sig("act_chain"))
            link(nc.scalar.activation(flat(dec), flat(k), ACT.Abs))
            link(nc.scalar.activation(flat(dec), flat(dec), ACT.Exp, scale=-1.0))
            nc.scalar.activation(flat(qe), flat(dec), ACT.Ln, bias=1.0).then_inc(*steps.one())
            act.wait_ge(*steps.at(2))
            nc.scalar.activation(flat(k), flat(k), ACT.Sigmoid, scale=-1.0)

        @block.vector
        def _(dve):
            link = linker(dve, sig("dve_chain"))
            nc.vector.memset(flat(ke), 1.0)
            dve.wait_ge(*steps.at(1))
            link(nc.vector.scalar_tensor_tensor(flat(dec), flat(k), 0.0, flat(qe), ALU.min, ALU.subtract))
            dve.sem_inc(*steps.one())
            for h in range(HG_H):
                nc.vector.tensor_tensor_scan(b[:, h, :], ke[:, h, :], dec[:, h, :], 0.0, ALU.mult, ALU.add)

    lv = view(8 * W8, 1, LEV_N)[:, 0].bitcast(U32)
    attn, attn1 = H[:, :, S:2 * S], X[:, :, S:S + P]
    mk_ready = sig("level_masks_ready")
    diff, expd, qd, kd, prod, put, peu = (sig(n) for n in (
        "hg_diff_ready", "hg_decay_ready", "hg_q_ready", "hg_k_ready", "hg_scores_ready", "hg_scores_read",
        "hg_operands_read"))
    levels = [P] + LEVELS + [0]
    decs = (flat(dec), core.norm_rt[:, :])
    qes = (flat(qe), core.norm_sq[:, :, :].rearrange("p a b -> p (a b)"))
    NL = len(levels)
    with core.phase() as block:

        @block.sync
        def _(sp):
            sp.dma_start(lv[:, :], a["levels"]).then_inc(*mk_ready.dma())
            sp.wait_ge(*mk_ready.at(16))

        @block.vector
        def _(dve):
            link = linker(dve, sig("dve_chain"))
            nc.vector.memset(attn, 0.0)
            link(nc.vector.memset(attn1, 0.0))
            dve.wait_ge(*mk_ready.at(16))

            def take(n):
                L = levels[n]
                for h4 in range(4):
                    dve.wait_ge(*prod.at(4 * n + h4 + 1))
                    ps = psum[:, (4 * n + h4) % 8, :]
                    pair = attn[:, 2 * h4:2 * h4 + 2, :]
                    if L == P:
                        ins = nc.vector.tensor_copy(
                            pair[:, :, P:2 * P], ps[:, 0:2 * P].rearrange("p (h t) -> p h t", h=2))
                        link(ins)
                    else:
                        o = P * (levels.index(L) - 1)
                        m = lv[:, o:o + P].unsqueeze(1).broadcast_to([P, 2, P])
                        for t in range(2):
                            ins = nc.vector.copy_predicated(
                                (attn if t == 0 else attn1)[:, 2 * h4:2 * h4 + 2, 0:P], m, ps.rearrange("p (t h c) -> p t h c", t=2, h=2)[:, t])
                            link(ins)
                    dve.sem_inc(*put.one())

            def difference(n):
                L = levels[n]
                if n >= 2:
                    dve.wait_ge(*kd.at(n - 1))
                nb = W8 // (2 * L)
                bv = flat(b).rearrange("p (n e l) -> p n e l", e=2, l=L)
                dv = decs[n % 2].rearrange("p (n e l) -> p n e l", e=2, l=L)
                r = bv[:, :, 0, L - 1:L].broadcast_to([P, nb, L])
                nc.vector.tensor_tensor(dv[:, :, 1, :], bv[:, :, 1, :], r, ALU.subtract)
                link(nc.vector.tensor_tensor(dv[:, :, 0, :], r, bv[:, :, 0, :], ALU.subtract))
                dve.sem_inc(*diff.one())

            difference(0)
            for n in range(NL - 1):
                if n + 1 < NL - 1:
                    difference(n + 1)
                dve.wait_ge(*expd.at(n + 1))
                if n >= 2:
                    dve.wait_ge(*peu.at(n - 1))
                link(nc.vector.tensor_tensor(qes[n % 2], flat(q), decs[n % 2], ALU.mult))
                dve.sem_inc(*qd.one())
                if n:
                    take(n - 1)
            take(NL - 2)
            take(NL - 1)

        @block.scalar
        def _(act):
            for n in range(NL - 1):
                act.wait_ge(*diff.at(n + 1))
                nc.scalar.activation(decs[n % 2], decs[n % 2], ACT.Exp).then_inc(*expd.one())

        @block.gpsimd
        def _(pool):
            for n in range(NL - 1):
                pool.wait_ge(*expd.at(n + 1))
                if n:
                    pool.wait_ge(*peu.at(n))
                nc.gpsimd.tensor_tensor(flat(ke), flat(k), decs[n % 2], ALU.mult).then_inc(*kd.one())

        @block.tensor
        def _(pe):
            for n, L in enumerate(levels):
                ko = ke if L else k
                qo = qes[n % 2].rearrange("p (h t) -> p h t", h=HG_H) if L else q
                if L:
                    pe.wait_ge(*qd.at(n + 1))
                    pe.wait_ge(*kd.at(n + 1))
                for h4 in range(4):
                    i = 4 * n + h4
                    if i >= 8:
                        pe.wait_ge(*put.at(i - 7))
                    for t in range(1 if L == P else 2):
                        for e in range(2):
                            h = 2 * h4 + e
                            o = psum[:, i % 8, (2 * t + e) * P:(2 * t + e + 1) * P]
                            ks = ko[:, h, t * P:(t + 1) * P]
                            qs = qo[:, h, P:2 * P] if L == P else qo[:, h, t * P:(t + 1) * P]
                            mm = nc.tensor.matmul(o, ks, qs, start=True, stop=True)
                    mm.then_inc(*prod.one())
                if L:
                    pe.wait_ge(*prod.at(4 * n + 4))
                    pe.sem_inc(*peu.one())

    o = dec
    oacc = sig("hg_out_ready")
    with core.phase() as block:

        @block.tensor
        def _(pe):
            for h in range(HG_H):
                ps = psum[:, h, 0:S]
                nc.tensor.matmul(ps[:, P:S], v[:, 1, h * P:(h + 1) * P], attn1[:, h, :], start=True, stop=False,
                                 skip_group_check=True)
                nc.tensor.matmul(ps, v[:, 0, h * P:(h + 1) * P], attn[:, h, :], start=False, stop=True,
                                 skip_group_check=True).then_inc(*oacc.one())

        @block.scalar
        def _(act):
            for h in range(HG_H):
                act.wait_ge(*oacc.at(h + 1))
                nc.scalar.activation(o[:, h, :], psum[:, h, 0:S], ACT.Copy)

    norm_fm(core, lambda t: o[:, t, :], HG_H, 1, S, lambda t: pr("hg_norm"), lambda t: y_hg[:, t, :],
            gate=lambda t: g[:, t, :])

    mq = view(2 * W8, 2 * ML_H, S)
    vml = view(3 * W8, ST, D)
    go = view(4 * W8, DT, S)
    tmp = view(8 * W8 - 512, 2, S)

    def conv4(w, bias, tmpb):
        def f(dve, link, i, ps):
            t = tmpb[:, i % 2, :]
            link(nc.vector.tensor_scalar(t, ps[:, 0:S], w(3, i), bias(i), ALU.mult, ALU.add))
            for d in (1, 2, 3):
                ins = nc.vector.scalar_tensor_tensor(t[:, d:S], ps[:, 0:S - d], w(3 - d, i), t[:, d:S],
                                                     ALU.mult, ALU.add)
                if d < 3:
                    link(ins)
            return ins
        return f

    project(core, H, S, [512] * 2, DT, on_dve=conv4(lambda kk, i: pr("ml_w", kk * DT + i), lambda i: pr("ml_b", i), tmp),
            then_act=lambda act, i: nc.scalar.activation(mq[:, i, :], tmp[:, i % 2, :], ACT.Silu))
    project(core, H, S, [512] * 2, DT, fm=False, on_act=tm_to(vml), side=mods[0])
    project(core, H, S, [512] * 2, DT,
            on_act=lambda act, i, n, j, ps: nc.scalar.activation(go[:, i, :], ps[:, 0:S], ACT.Sigmoid), side=mods[0])

    WK = 5 * W8
    gt = view(WK, 12, S)
    gs = sig("gates_steps")
    wg = pv("w_gates", DT)
    ml, mi, md = 0, 1, 2
    with core.phase() as block:

        @block.tensor
        def _(pe):
            for bank, (c, n) in enumerate(((0, 4), (4, 4), (8, 16))):
                for kk in range(DT):
                    mm = nc.tensor.matmul(psum[0:n, bank, 0:S], wg[:, kk, c:c + n], H[:, kk, 0:S],
                                          start=(kk == 0), stop=(kk == DT - 1))
                mm.then_inc(*gs.one())

        @block.scalar
        def _(act):
            link = linker(act, sig("act_chain"))
            act.wait_ge(*gs.at(3))
            link(nc.scalar.activation(gt[0:4, 0, :], psum[0:4, 0, 0:S], ACT.Identity, bias=pr("gate_i")[0:4]))
            link(nc.scalar.activation(gt[0:4, 1, :], psum[0:4, 1, 0:S], ACT.Identity, bias=pr("gate_f")[0:4]))
            link(nc.scalar.activation(gt[0:16, 2, :], psum[0:16, 2, 0:S], ACT.Identity, bias=pr("dt_bias")[0:16]))
            link(nc.scalar.activation(gt[0:4, 3, :], gt[0:4, 1, :], ACT.Abs))
            link(nc.scalar.activation(gt[0:16, 4, :], gt[0:16, 2, :], ACT.Abs))
            link(nc.scalar.activation(gt[0:4, 3, :], gt[0:4, 3, :], ACT.Exp, scale=-1.0))
            link(nc.scalar.activation(gt[0:16, 4, :], gt[0:16, 4, :], ACT.Exp, scale=-1.0))
            link(nc.scalar.activation(small[0:16, 0:1], pr("a_log")[0:16], ACT.Exp))
            link(nc.scalar.activation(gt[0:4, 3, :], gt[0:4, 3, :], ACT.Ln, bias=1.0))
            link(nc.scalar.activation(gt[0:16, 4, :], gt[0:16, 4, :], ACT.Ln, bias=1.0))
            act.sem_inc(*gs.one())

        @block.vector
        def _(dve):
            link = linker(dve, sig("dve_chain"))
            link(nc.vector.memset(gt[0:16, 5, :], 1.0))
            dve.wait_ge(*gs.at(4))
            link(nc.vector.scalar_tensor_tensor(gt[0:4, 1, :], gt[0:4, 1, :], 0.0, gt[0:4, 3, :], ALU.min, ALU.subtract))
            link(nc.vector.tensor_tensor_scan(gt[0:4, 6, :], gt[0:4, 5, :], gt[0:4, 1, :], 0.0, ALU.mult, ALU.add))
            link(nc.vector.tensor_tensor(gt[0:4, 7, :], gt[0:4, 0, :], gt[0:4, 6, :], ALU.subtract))
            link(nc.vector.tensor_tensor_scan(gt[0:4, 8, :], gt[0:4, 7, :], gt[0:4, 7, :], 0.0, ALU.max, ALU.max))
            link(nc.vector.tensor_tensor(gt[0:4, 9, :], gt[0:4, 6, :], gt[0:4, 8, :], ALU.add))
            link(nc.vector.scalar_tensor_tensor(gt[0:16, 2, :], gt[0:16, 2, :], 0.0, gt[0:16, 4, :], ALU.max, ALU.add))
            link(nc.vector.tensor_scalar(gt[0:16, 10, :], gt[0:16, 2, :], small[0:16, 0:1], -1.0, ALU.mult, ALU.mult))
            nc.vector.tensor_tensor_scan(gt[0:16, 11, :], gt[0:16, 5, :], gt[0:16, 10, :], 0.0, ALU.mult, ALU.add)

    cols = core.sbuf("gate_columns", [P, ST, 3, MB_H])
    cs = sig("columns_ready")
    with core.phase() as block:

        @block.tensor
        def _(pe):
            for t in range(ST):
                for i, (r, n) in enumerate(((7, 4), (11, 16), (2, 16))):
                    mm = nc.tensor.transpose(psum[:, 3 * t + i, 0:n], gt[0:n, r, t * P:(t + 1) * P], ident[0:n, 0:n])
                    mm.then_inc(*cs.one())

        @block.vector
        def _(dve):
            dve.wait_ge(*cs.at(6))
            for t in range(ST):
                nc.vector.tensor_copy(cols[:, t, 0, 0:4], psum[:, 3 * t, 0:4])
                nc.vector.tensor_scalar(cols[:, t, 1, :], psum[:, 3 * t + 1, 0:16], -1.0, None, ALU.mult)
                nc.vector.tensor_copy(cols[:, t, 2, :], psum[:, 3 * t + 2, 0:16])

    arg = view(WK + 12 * S, 2, 3 * P)
    wts = view(WK + 12 * S + 6 * P, 2, 3 * P)
    num = H[:, :, S:2 * S]

    def pick(h, n):
        return ident[0:n, h:h + 1].broadcast_to([n, P])

    big = [sig(n) for n in ("ml_scores_ready", "ml_arg_ready", "ml_exp_ready", "ml_weights_ready", "ml_sums_ready",
                            "ml_abs_ready", "ml_head_done")]
    sc, ag, ex, wt, sm, ab, hd = big
    scale = float(P) ** -0.5
    with core.phase() as block:

        @block.tensor
        def _(pe):
            def scores(h):
                if h >= 2:
                    pe.wait_ge(*wt.at(h - 1))
                b0 = 2 * (h % 2)
                nc.tensor.matmul(psum[:, b0, 0:S], mq[:, ML_H + h, 0:P], mq[:, h, :], start=True, stop=True)
                nc.tensor.matmul(psum[:, b0, S:3 * P], mq[:, ML_H + h, P:S], mq[:, h, P:S], start=True, stop=True,
                                 skip_group_check=True)
                nc.tensor.matmul(psum[:, b0 + 1, 0:S], pick(h, 4), gt[0:4, 8, :], start=True, stop=True)\
                    .then_inc(*sc.one())

            scores(0)
            for h in range(ML_H):
                if h + 1 < ML_H:
                    scores(h + 1)
                pe.wait_ge(*wt.at(h + 1))
                if h >= 1:
                    pe.wait_ge(*hd.at(h))
                w = wts[:, h % 2, :]
                for j in range(3):
                    v0 = vml[:, 0, h * 256 + j * P:h * 256 + (j + 1) * P] if j < 2 else core.ones[:, :]
                    v1 = vml[:, 1, h * 256 + j * P:h * 256 + (j + 1) * P] if j < 2 else core.ones[:, :]
                    nc.tensor.matmul(psum[:, 4 + j, P:S], v1, w[:, S:3 * P], start=True, stop=False,
                                     skip_group_check=True)
                    nc.tensor.matmul(psum[:, 4 + j, 0:S], v0, w[:, 0:S], start=False, stop=True,
                                     skip_group_check=True)
                nc.tensor.matmul(psum[:, 7, 0:S], pick(h, 4), gt[0:4, 9, :], start=True, stop=True)\
                    .then_inc(*sm.one())

        @block.scalar
        def _(act):
            link = linker(act, sig("act_chain"))

            def bounds(h):
                act.wait_ge(*sm.at(h + 1))
                if h:
                    act.wait_ge(*hd.at(h))
                nc.scalar.activation(core.norm_rt[:, 0:S], psum[:, 6, 0:S], ACT.Abs)
                link(nc.scalar.activation(core.norm_rt[:, S:2 * S], psum[:, 7, 0:S], ACT.Exp, scale=-1.0))
                act.sem_inc(*ab.one())

            for h in range(ML_H):
                act.wait_ge(*ag.at(h + 1))
                nc.scalar.activation(arg[:, h % 2, :], arg[:, h % 2, :], ACT.Exp).then_inc(*ex.one())
                if h:
                    bounds(h - 1)
            bounds(ML_H - 1)

        @block.vector
        def _(dve):
            link = linker(dve, sig("dve_chain"))

            def exponents(h):
                dve.wait_ge(*sc.at(h + 1))
                ar = arg[:, h % 2, :]
                mt = psum[:, 2 * (h % 2) + 1, 0:S]
                nc.vector.tensor_scalar(ar[:, 0:S], mt, -1.0, cols[:, 0, 0, h:h + 1], ALU.mult, ALU.add)
                link(nc.vector.tensor_scalar(ar[:, S:3 * P], mt[:, P:S], -1.0, cols[:, 1, 0, h:h + 1], ALU.mult, ALU.add))
                link(nc.vector.tensor_scalar(ar[:, :], ar[:, :], 0.0, None, ALU.min))
                dve.sem_inc(*ag.one())

            def weights(h):
                dve.wait_ge(*ex.at(h + 1))
                ar = arg[:, h % 2, :]
                dg = ar.rearrange("p (b c) -> p b c", b=3)[:, 0:3:2, :]
                link(nc.vector.tensor_tensor(dg, dg, causal.unsqueeze(1).broadcast_to([P, 2, P]), ALU.mult))
                if h >= 2:
                    dve.wait_ge(*sm.at(h - 1))
                link(nc.vector.scalar_tensor_tensor(wts[:, h % 2, :], psum[:, 2 * (h % 2), 0:3 * P], scale, ar,
                                                    ALU.mult, ALU.mult))
                dve.sem_inc(*wt.one())

            def divide(h):
                dve.wait_ge(*ab.at(h + 1))
                rt = core.norm_rt
                link(nc.vector.tensor_tensor(rt[:, 2 * S:3 * S], rt[:, 0:S], rt[:, S:2 * S], ALU.max))
                link(nc.vector.reciprocal(rt[:, 2 * S:3 * S], rt[:, 2 * S:3 * S]))
                for j in range(2):
                    ins = nc.vector.tensor_tensor(num[:, 2 * h + j, :], psum[:, 4 + j, 0:S], rt[:, 2 * S:3 * S], ALU.mult)
                link(ins)
                dve.sem_inc(*hd.one())

            exponents(0)
            for h in range(ML_H):
                if h + 1 < ML_H:
                    exponents(h + 1)
                weights(h)
                if h:
                    divide(h - 1)
            divide(ML_H - 1)

    norm_fm(core, lambda t: num[:, t, :], DT, 2, S, lambda t: pr("ml_norm", t % 2), lambda t: y_ml[:, t, :],
            gate=lambda t: go[:, t, :])

    z = view(2 * W8, DT, S)
    xbc = view(3 * W8, 2 * DT, S)
    XS, BM, CM = 0, DT, DT + MB_G
    tmp2 = core.norm_rt[:, 0:2 * S].rearrange("p (a b) -> p a b", a=2)
    project(core, H, S, [512] * 2, DT, on_act=silu_to(z), side=mods[1])
    project(core, H, S, [512] * 4, DT, on_dve=conv4(lambda kk, i: pr("mb_w", kk * 16 + i), lambda i: pr("mb_b", i), tmp2),
            then_act=lambda act, i: nc.scalar.activation(xbc[:, i, :], tmp2[:, i % 2, :], ACT.Silu))

    cbs = view(WK + 12 * S + 12 * P, MB_G, 3 * P)
    tr, trr, cb, cbr = sig("mb_x_turned"), sig("mb_x_read"), sig("mb_cb_ready"), sig("mb_cb_read")
    halves = (H[:, :, S:2 * S], X[:, :, S:2 * S])

    def xh(t, h):
        return halves[t][:, h // 2, (h % 2) * P:(h % 2 + 1) * P]

    with core.phase() as block:

        @block.tensor
        def _(pe):
            for i in range(2 * DT):
                t, j = i // DT, i % DT
                if i >= 4:
                    pe.wait_ge(*trr.at(i - 3))
                nc.tensor.transpose(psum[:, i % 4, 0:P], xbc[:, XS + j, t * P:(t + 1) * P], ident).then_inc(*tr.one())
            for gq in range(MB_G):
                ps = psum[:, 4 + gq, :]
                nc.tensor.matmul(ps[:, 0:S], xbc[:, BM + gq, 0:P], xbc[:, CM + gq, :], start=True, stop=True)
                nc.tensor.matmul(ps[:, S:3 * P], xbc[:, BM + gq, P:S], xbc[:, CM + gq, P:S], start=True, stop=True,
                                 skip_group_check=True).then_inc(*cb.one())

        @block.scalar
        def _(act):
            for gq in range(MB_G):
                act.wait_ge(*cb.at(gq + 1))
                nc.scalar.activation(cbs[:, gq, :], psum[:, 4 + gq, 0:3 * P], ACT.Copy)

        @block.vector
        def _(dve):
            link = linker(dve, sig("dve_chain"))
            for t in range(ST):
                link(nc.vector.memset(halves[t], 0.0))
            for i in range(2 * DT):
                t, j = i // DT, i % DT
                dve.wait_ge(*tr.at(i + 1))
                for e in range(2):
                    ins = nc.vector.tensor_scalar(xh(t, 2 * j + e)[:, e * 64:(e + 1) * 64], psum[:, i % 4, e * 64:(e + 1) * 64],
                                                  cols[:, t, 2, 2 * j + e:2 * j + e + 1], None, ALU.mult)
                link(ins)
                dve.sem_inc(*trr.one())

    yz, ytmp = z, core.norm_rt[:, 0:S]
    bc, ag2, ex2, wt2, ou, our = (sig(n) for n in ("mb_cum_ready", "mb_arg_ready", "mb_exp_ready", "mb_weights_ready",
                                                   "mb_pair_ready", "mb_pair_read"))
    with core.phase() as block:

        @block.tensor
        def _(pe):
            def cum(h):
                if h >= 4:
                    pe.wait_ge(*ag2.at(h - 3))
                nc.tensor.matmul(psum[:, h % 4, 0:S], pick(h, 16), gt[0:16, 11, :], start=True, stop=True)\
                    .then_inc(*bc.one())

            cum(0)
            cum(1)
            for h in range(MB_H):
                if h + 2 < MB_H:
                    cum(h + 2)
                pe.wait_ge(*wt2.at(h + 1))
                j, e = h // 2, h % 2
                if e == 0 and j >= 2:
                    pe.wait_ge(*our.at(j - 1))
                ps = psum[:, 4 + j % 2, 0:S]
                w = wts[:, h % 2, :]
                if e == 0:
                    nc.tensor.matmul(ps, xh(0, h), w[:, 0:S], start=True, stop=False, skip_group_check=True)
                mm = nc.tensor.matmul(ps[:, P:S], xh(1, h), w[:, S:3 * P], start=False, stop=False, skip_group_check=True)
                if e == 1:
                    mm = nc.tensor.matmul(ps, xh(0, h), w[:, 0:S], start=False, stop=True, skip_group_check=True)
                mm.then_inc(*ou.one())

        @block.scalar
        def _(act):
            for h in range(MB_H):
                act.wait_ge(*ag2.at(h + 1))
                nc.scalar.activation(arg[:, h % 2, :], arg[:, h % 2, :], ACT.Exp).then_inc(*ex2.one())

        @block.vector
        def _(dve):
            link = linker(dve, sig("dve_chain"))

            def exponents(h):
                dve.wait_ge(*bc.at(h + 1))
                ar, ps = arg[:, h % 2, :], psum[:, h % 4, 0:S]
                nc.vector.tensor_scalar(ar[:, 0:S], ps, cols[:, 0, 1, h:h + 1], 0.0, ALU.add, ALU.min)
                link(nc.vector.tensor_scalar(ar[:, S:3 * P], ps[:, P:S], cols[:, 1, 1, h:h + 1], 0.0, ALU.add, ALU.min))
                dve.sem_inc(*ag2.one())

            def pair(j):
                dve.wait_ge(*ou.at(2 * j + 2))
                link(nc.vector.scalar_tensor_tensor(ytmp, xbc[:, XS + j, :], pr("mb_d", j), psum[:, 4 + j % 2, 0:S],
                                                    ALU.mult, ALU.add))
                dve.sem_inc(*our.one())
                link(nc.vector.tensor_tensor(yz[:, j, :], ytmp, z[:, j, :], ALU.mult))

            exponents(0)
            for h in range(MB_H):
                if h + 1 < MB_H:
                    exponents(h + 1)
                dve.wait_ge(*ex2.at(h + 1))
                ar = arg[:, h % 2, :]
                dg = ar.rearrange("p (b c) -> p b c", b=3)[:, 0:3:2, :]
                link(nc.vector.tensor_tensor(dg, dg, causal.unsqueeze(1).broadcast_to([P, 2, P]), ALU.mult))
                if h >= 2:
                    dve.wait_ge(*ou.at(h - 1))
                link(nc.vector.tensor_tensor(wts[:, h % 2, :], cbs[:, h // 4, :], ar, ALU.mult))
                dve.sem_inc(*wt2.one())
                if h >= 3 and h % 2 == 1:
                    pair(h // 2 - 1)
            pair(MB_H // 2 - 1)

    norm_fm(core, lambda t: yz[:, t, :], DT, 2, S, lambda t: pr("mb_norm", t), lambda t: y_mb[:, t, :])

    gate, mixed = view(3 * W8, DT, S), view(4 * W8, DT, S)
    tmpm = core.norm_rt[:, 0:S]
    for bi, y in enumerate((y_hg, y_ml, y_mb)):
        project(core, H, S, [512] * 2, DT,
                on_act=lambda act, i, n, j, ps: nc.scalar.activation(gate[:, i, :], ps[:, 0:S], ACT.Sigmoid),
                side=mods[1])

        def gated(dve, link, i, ps, bi=bi):
            if bi == 0:
                return nc.vector.tensor_tensor(mixed[:, i, :], ps[:, 0:S], gate[:, i, :], ALU.mult)
            link(nc.vector.tensor_tensor(tmpm, ps[:, 0:S], gate[:, i, :], ALU.mult))
            return nc.vector.tensor_tensor(mixed[:, i, :], mixed[:, i, :], tmpm, ALU.add)

        project(core, y, S, [512] * 2, DT, on_dve=gated)
    project(core, mixed, S, [512] * 2, DT,
            on_dve=lambda dve, link, i, ps: nc.vector.tensor_tensor(X[:, i, 0:S], ps[:, 0:S], X[:, i, 0:S], ALU.add))


def feed_forward(core, X, H, view, T, gain, shift, cw, cb, lead, scale, ctx_pars=None):
    nc = core.nc
    seg = T // S
    u = view(0, FFT, T)
    tmp = view(FFT * T, 4, T)
    norm_fm(core, lambda t: X[:, t, 0:T], DT, DT, T, gain, lambda t: H[:, t, 0:T],
            shift=shift) if ctx_pars is None else ctx_pars()

    def tile_of(i):
        c, j = i // 4, i % 4
        return (2 * c + j) if j < 2 else (FFT + 2 * c + j - 2)

    def conv3(dve, link, i, ps):
        ch = tile_of(i)
        t = tmp[:, i % 4, :].rearrange("p (s t) -> p s t", s=seg)
        pp = ps[:, 0:T].rearrange("p (s t) -> p s t", s=seg)
        link(nc.vector.tensor_scalar(tmp[:, i % 4, :], ps[:, 0:T], cw(lead, ch), cb(ch), ALU.mult, ALU.add))
        taps = [k for k in range(3) if k != lead]
        for n, k in enumerate(taps):
            d = lead - k
            if d > 0:
                o, s_ = t[:, :, d:S], pp[:, :, 0:S - d]
            else:
                o, s_ = t[:, :, 0:S + d], pp[:, :, -d:S]
            ins = nc.vector.scalar_tensor_tensor(o, s_, cw(k, ch), o, ALU.mult, ALU.add)
            if n == 0:
                link(ins)
        return ins

    up(core, H, T, conv3, tmp, u)
    project(core, u, T, [P] * DT, FFT,
            on_dve=(lambda dve, link, i, ps: nc.vector.tensor_tensor(X[:, i, 0:T], ps[:, 0:T], X[:, i, 0:T], ALU.add))
            if scale is None else scale)


def up(core, H, T, conv3, tmp, u):
    nc = core.nc
    acc, free = core.sig("up_acc_ready"), core.sig("up_bank_free")
    filt, sil = core.sig("up_filtered"), core.sig("up_silu_ready")
    c0 = core.taken
    NC = FFT // 2
    core.taken += NC
    with core.phase() as block:

        @block.sync
        def _(sp):
            for n in range(NC):
                sp.wait_ge(*acc.at(4 * n + 4))
                core.load(sp, c0 + n + RING)

        @block.tensor
        def _(pe):
            for n in range(NC):
                c = c0 + n
                w = core.slot(c, DT, 512)
                pe.wait_ge(core.loaded[c % RING].handle, 16 * (c // RING + 1))
                for j in range(4):
                    i = 4 * n + j
                    if i >= 8:
                        pe.wait_ge(*free.at(i - 7))
                    for k in range(DT):
                        mm = nc.tensor.matmul(core.psum[:, i % 8, 0:T], w[:, k, j * P:(j + 1) * P], H[:, k, 0:T],
                                              start=(k == 0), stop=(k == DT - 1))
                    mm.then_inc(*acc.one())

        @block.vector
        def _(dve):
            link = linker(dve, core.sig("dve_chain"))
            for n in range(NC):
                for j in range(4):
                    i = 4 * n + j
                    dve.wait_ge(*acc.at(i + 1))
                    link(conv3(dve, link, i, core.psum[:, i % 8, :]))
                    dve.sem_inc(*free.one())
                    if j < 2:
                        dve.sem_inc(*filt.one())
                for j in range(2):
                    dve.wait_ge(*sil.at(2 * n + j + 1))
                    link(nc.vector.tensor_tensor(u[:, 2 * n + j, :], tmp[:, j, :], tmp[:, 2 + j, :], ALU.mult))

        @block.scalar
        def _(act):
            for i in range(FFT):
                act.wait_ge(*filt.at(i + 1))
                nc.scalar.activation(tmp[:, i % 2, :], tmp[:, i % 2, :], ACT.Silu).then_inc(*sil.one())


def load_context(core, a, X):
    ctx_ready = core.sig("context_ready")
    with core.phase() as block:

        @block.sync
        def _(sp):
            sp.dma_start(X[:, :, S:2 * S], a["ctx"].rearrange("(k p) t -> p k t", p=P)).then_inc(*ctx_ready.dma())
            sp.wait_ge(*ctx_ready.at(16))


def attention_layer(core, a, i, X, H, pr, pv, cn, view, ident, small, adaM, side):
    nc, sig, psum = core.nc, core.sig, core.psum
    last = i == LAYERS - 1
    lam_init = 0.8 - 0.6 * float(np.exp(-0.3 * i))
    if i == 0:
        norm_fm(core, lambda t: X[:, t, 0:S], DT, DT, S, lambda t: pr("final", t), lambda t: X[:, t, 0:S])

    gains = core.sbuf(f"mod_gains{i}", [P, 2, DT, 2])
    with core.phase() as block:

        @block.vector
        def _(dve):
            link = linker(dve, sig("dve_chain"))
            for half, (name, part) in enumerate(((f"norm1_{i}", 1), (f"norm2_{i}", 4))):
                gcol = pv(name, DT).broadcast_to([P, DT, 2])
                sc_ = adaM[:, part * DT:(part + 1) * DT, :]
                link(nc.vector.tensor_scalar(gains[:, half], sc_, 1.0, None, ALU.add))
                link(nc.vector.tensor_tensor(gains[:, half], gains[:, half], gcol, ALU.mult))

    def modulated(half, T):
        for s_ in range(T // S):
            norm_fm(core, lambda t, s_=s_: X[:, t, s_ * S:(s_ + 1) * S], DT, DT, S,
                    lambda t, s_=s_: gains[:, half, t, s_:s_ + 1],
                    lambda t, s_=s_: H[:, t, s_ * S:(s_ + 1) * S],
                    shift=lambda t, s_=s_: adaM[:, 3 * half * DT + t, s_:s_ + 1])

    modulated(0, 2 * S)

    z = view(0, 4, 2048)
    need = {0: range(4), 1: range(4), 2: range(4), 3: range(4)}
    NT = 4

    def toks(n):
        if not last:
            return 0, 512, range(4)
        if n < 2:
            return 0, 512, range(2)
        if n == 2:
            return 0, 0, {0: (0, 512), 1: (0, 512), 2: (0, 256), 3: (0, 256)}
        return 0, 512, range(4)

    def zout(act, i_, n, j, ps):
        w = 256 if (last and n == 2 and j >= 2) else 512
        f = ACT.Gelu_apprx_tanh if n == 0 else ACT.Copy
        if n == 1:
            return nc.scalar.activation(z[:, j, 512:1024].rearrange("p (h g c) -> p g h c", g=2, h=4),
                                        ps.rearrange("p (g h c) -> p g h c", g=2, h=4), f)
        return nc.scalar.activation(z[:, j, n * 512:n * 512 + w], ps[:, 0:w], f)

    project(core, H, 2 * S, [512] * 4, DT, fm=False, on_act=zout, tok_tiles=toks, side=side)

    TT = view(4 * 2048, 16, 512)
    sqs = (core.norm_rt[:, 0:1408], view(4 * 2048, 1, 1408)[:, 0])
    rss = (small[:, 0:30], small[:, 32:62])
    r2 = core.norm_sq[:, :, :].rearrange("p a b -> p (a b)")
    lam_s, sq_r, ss_r, rt_r = (sig(n) for n in ("lambda_steps", "qk_squares_ready", "qk_sums_ready", "qk_roots_ready"))
    lamc = core.sbuf(f"lambda{i}", [P, 4])
    with core.phase() as block:

        @block.gpsimd
        def _(pool):
            nc.gpsimd.memset(TT[:, 4:6, :], 0.0)
            nc.gpsimd.memset(TT[:, 8:16, :], 0.0)

        @block.scalar
        def _(act):
            link = linker(act, sig("act_chain"))
            act.wait_ge(*lam_s.at(1))
            nc.scalar.activation(lamc[:, 0:2], lamc[:, 0:2], ACT.Exp).then_inc(*lam_s.one())

            def squares(t):
                sq = sqs[t % 2]
                if t >= 2:
                    act.wait_ge(*ss_r.at(t - 1))
                if last and t >= 2:
                    nc.scalar.activation(sq[:, 768:896], z[:, t, 1024:1152], ACT.Square)
                    link(nc.scalar.activation(sq[:, 1152:1408], z[:, t, 1536:1792], ACT.Square))
                else:
                    nc.scalar.activation(sq[:, 0:896], z[:, t, 256:1152], ACT.Square)
                    link(nc.scalar.activation(sq[:, 896:1408], z[:, t, 1280:1792], ACT.Square))
                act.sem_inc(*sq_r.one())

            squares(0)
            for t in range(NT):
                if t + 1 < NT:
                    squares(t + 1)
                act.wait_ge(*ss_r.at(t + 1))
                rs = rss[t % 2]
                lo = 12 if (last and t >= 2) else 0
                nc.scalar.activation(rs[:, lo:14], rs[:, lo:14], ACT.Sqrt, scale=1.0 / 64, bias=core.eps[:, 0:1])
                lo = 22 if (last and t >= 2) else 14
                link(nc.scalar.activation(rs[:, lo:30], rs[:, lo:30], ACT.Sqrt, scale=1.0 / 32, bias=core.eps[:, 0:1]))
                act.sem_inc(*rt_r.one())

        @block.vector
        def _(dve):
            link = linker(dve, sig("dve_chain"))
            lp = pv(f"lam{i}", 4)
            for m in range(2):
                link(nc.vector.tensor_tensor(r2[:, 0:32], lp[:, 2 * m, :], lp[:, 2 * m + 1, :], ALU.mult))
                link(nc.vector.tensor_reduce(lamc[:, m:m + 1], r2[:, 0:32], AX.X, ALU.add))
            dve.sem_inc(*lam_s.one())
            dve.wait_ge(*lam_s.at(2))
            link(nc.vector.tensor_tensor(lamc[:, 2:3], lamc[:, 1:2], lamc[:, 0:1], ALU.subtract))
            link(nc.vector.tensor_scalar(lamc[:, 2:3], lamc[:, 2:3], -lam_init, None, ALU.add))

            def short(t):
                return last and t >= 2

            def sums(t):
                rs, sq = rss[t % 2], sqs[t % 2]
                b0, c0 = (12, 8) if short(t) else (0, 0)
                dve.wait_ge(*sq_r.at(t + 1))
                nc.vector.tensor_reduce(rs[:, b0:14], sq[:, b0 * 64:896].rearrange("p (g c) -> p g c", c=64), AX.X, ALU.add)
                link(nc.vector.tensor_reduce(rs[:, 14 + c0:30], sq[:, 896 + c0 * 32:1408].rearrange("p (g c) -> p g c", c=32),
                                             AX.X, ALU.add))
                dve.sem_inc(*ss_r.one())

            def scaled(t):
                rs = rss[t % 2]
                b0, c0 = (12, 8) if short(t) else (0, 0)
                dve.wait_ge(*rt_r.at(t + 1))
                nc.vector.reciprocal(rs[:, b0:14], rs[:, b0:14])
                link(nc.vector.reciprocal(rs[:, 14 + c0:30], rs[:, 14 + c0:30]))
                zb = z[:, t, 256 + b0 * 64:1152].rearrange("p (g c) -> p g c", c=64)
                zc = z[:, t, 1280 + c0 * 32:1792].rearrange("p (g c) -> p g c", c=32)
                nc.vector.tensor_tensor(zb, zb, rs[:, b0:14].unsqueeze(2).broadcast_to([P, 14 - b0, 64]), ALU.mult)
                link(nc.vector.tensor_tensor(zc, zc, rs[:, 14 + c0:30].unsqueeze(2).broadcast_to([P, 16 - c0, 32]), ALU.mult))
                for o, n, w, gname, go in ((512, 8, 64, "gain_b", 0), (1280, 8, 32, "gain_c", 0),
                                           (1024, 2, 64, "gain_b", 64), (1536, 8, 32, "gain_c", 32)):
                    if not short(t) or o in (1024, 1536):
                        zg = z[:, t, o:o + n * w].rearrange("p (n w) -> p n w", n=n)
                        gv = pr(f"{gname}{i}", go, w).unsqueeze(1).broadcast_to([P, n, w])
                        ins = nc.vector.tensor_tensor(zg, zg, gv, ALU.mult)
                link(ins)

            def rotate(t):
                for o, n, w, cname, sname, b in ((512, 10, 64, "cos_b", "sin_b", 0), (1280, 16, 32, "cos_c", "sin_c", 1024)):
                    f = w // 4
                    zz = z[:, t, o:o + n * w]
                    cosv = cn(cname, t * w, w).unsqueeze(1).broadcast_to([P, n, w])
                    sinv = cn(sname, t * w, w).rearrange("p (x e f) -> p x e f", x=2, e=2)
                    m1, m2 = r2[:, 0:n * w], r2[:, 640:640 + n * w]
                    z5 = zz.rearrange("p (n x e f) -> p n x e f", n=n, x=2, e=2)
                    m5 = m2.rearrange("p (n x e f) -> p n x e f", n=n, x=2, e=2)
                    nc.vector.tensor_tensor(m1.rearrange("p (n w) -> p n w", n=n), zz.rearrange("p (n w) -> p n w", n=n), cosv, ALU.mult)
                    for e in range(2):
                        ins = nc.vector.tensor_tensor(m5[:, :, :, e, :], z5[:, :, :, 1 - e, :],
                                                      sinv[:, :, e, :].unsqueeze(1).broadcast_to([P, n, 2, f]), ALU.mult)
                    link(ins)
                    link(nc.vector.tensor_tensor(zz, m1, m2, ALU.add))

            sums(0)
            for t in range(NT):
                if t + 1 < NT:
                    sums(t + 1)
                scaled(t)
                if t < 2:
                    rotate(t)

    turns = [(512 + j * P, j) for j in range(4)] + [(1280, 6), (1408, 7)] + [(1024, None), (1536, None), (1664, None)]
    tu, tur = sig("turned"), sig("turned_read")
    cat = H.rearrange("p k t -> p (k t)").rearrange("p (t c) -> p t c", t=4)
    NQ = 2 if last else 4
    wsT = pv(f"a_ws{i}", 4)
    gm = sig("gmlp_ready")
    with core.phase() as block:

        @block.tensor
        def _(pe):
            for j, (o, dst) in enumerate(turns):
                if j >= 4:
                    pe.wait_ge(*tur.at(j - 3))
                for t in range(4 if dst is None else NQ):
                    mm = nc.tensor.transpose(psum[:, j % 4, t * P:(t + 1) * P], z[:, t, o:o + P], ident)
                mm.then_inc(*tu.one())
            for t in range(NQ):
                for g_ in range(4):
                    v0 = 256 + (g_ // 2) * P
                    mm = nc.tensor.matmul(psum[:, 4 + t, g_ * P:(g_ + 1) * P], wsT[:, g_, :], z[:, t, v0:v0 + P],
                                          start=True, stop=True, skip_group_check=True)
                mm.then_inc(*gm.one())

        @block.scalar
        def _(act):
            for j, (o, dst) in enumerate(turns):
                act.wait_ge(*tu.at(j + 1))
                ps = psum[:, j % 4, :]
                if dst is not None:
                    ins = nc.scalar.activation(TT[:, dst, 0:NQ * P], ps[:, 0:NQ * P], ACT.Copy)
                elif o == 1024:
                    for g_ in range(2):
                        ins = nc.scalar.activation(TT[64 * g_:64 * g_ + 64, 4 + g_, :], ps[64 * g_:64 * g_ + 64, :], ACT.Copy)
                else:
                    for g_ in range(4):
                        ins = nc.scalar.activation(TT[32 * g_:32 * g_ + 32, 8 + 4 * (j - 7) + g_, :],
                                                   ps[32 * g_:32 * g_ + 32, :], ACT.Copy)
                ins.then_inc(*tur.one())

        @block.vector
        def _(dve):
            for t in range(NQ):
                dve.wait_ge(*gm.at(t + 1))
                for g_ in range(4):
                    o = g_ * P + 64 * (g_ % 2)
                    nc.vector.scalar_tensor_tensor(cat[:, t, g_ * 64:(g_ + 1) * 64], psum[:, 4 + t, o:o + 64],
                                                   pr(f"a_bs{i}", g_), z[:, t, g_ * 64:(g_ + 1) * 64], ALU.add, ALU.mult)

    units = [("B", t, h) for t in range(NQ) for h in range(8)] + [("C", t, h) for t in range(NQ) for h in range(4)]
    U = len(units)
    Eb = [core.norm_rt[:, 0:1024], core.norm_rt[:, 1024:2048], r2[:, 0:1024]]
    Eb = [e.rearrange("p (m k) -> p m k", m=2) for e in Eb]
    ETb = [r2[:, 1024:1536], r2[:, 1536:2048]]
    scr, mxr, exr, pdr, tp, tpr, ov, ovr = (sig(n) for n in (
        "at_scores_ready", "at_max_ready", "at_exp_ready", "at_probs_ready", "at_turned", "at_turned_read",
        "at_out_ready", "at_out_read"))

    def span(u):
        return (0, 512) if units[u][1] < 2 else (S, S)

    def scalars(u):
        return small[:, 10 * (u % 6):10 * (u % 6) + 10]

    with core.phase() as block:

        @block.tensor
        def _(pe):
            def scores(u):
                kind, t, h = units[u]
                k0, nk = span(u)
                if u >= 2:
                    pe.wait_ge(*exr.at(u - 1))
                for m in range(1 if kind == "B" else 2):
                    jq, jk = (h % 4, 4 + h // 4) if kind == "B" else (6 + h // 2, 8 + 2 * h + m)
                    mm = nc.tensor.matmul(psum[:, 2 * (u % 2) + m, 0:nk], TT[:, jq, t * P:(t + 1) * P],
                                          TT[:, jk, k0:k0 + nk], start=True, stop=True)
                mm.then_inc(*scr.one())

            def turn(u):
                k0, nk = span(u)
                pe.wait_ge(*pdr.at(u + 1))
                if u >= 2:
                    pe.wait_ge(*tpr.at(u - 1))
                for kt in range(nk // P):
                    mm = nc.tensor.transpose(psum[:, 4 + u % 2, kt * P:(kt + 1) * P], Eb[u % 3][:, 0, kt * P:(kt + 1) * P], ident)
                mm.then_inc(*tp.one())

            def values(u):
                kind, t, h = units[u]
                k0, nk = span(u)
                o = 1152 if kind == "B" else 1792 + P * (h // 2)
                pe.wait_ge(*tpr.at(u + 1))
                if u >= 2:
                    pe.wait_ge(*ovr.at(u - 1))
                for kt in range(nk // P):
                    mm = nc.tensor.matmul(psum[:, 6 + u % 2, 0:P], ETb[u % 2][:, kt * P:(kt + 1) * P],
                                          z[:, k0 // P + kt, o:o + P], start=(kt == 0), stop=(kt == nk // P - 1))
                mm.then_inc(*ov.one())

            for u in range(U + 4):
                if u < U:
                    scores(u)
                if 2 <= u < U + 2:
                    turn(u - 2)
                if u >= 4:
                    values(u - 4)

        @block.scalar
        def _(act):
            link = linker(act, sig("act_chain"))

            def exps(u):
                kind, t, h = units[u]
                _, nk = span(u)
                c, e = scalars(u), Eb[u % 3]
                act.wait_ge(*mxr.at(u + 1))
                if u >= 3:
                    act.wait_ge(*tp.at(u - 2))
                if kind == "B":
                    nc.scalar.activation(c[:, 3:4], pr(f"sink{i}", h), ACT.Exp, bias=c[:, 2:3])
                    link(nc.scalar.activation(e[:, 0, 0:nk], e[:, 1, 0:nk], ACT.Exp, bias=c[:, 2:3], accum_out=c[:, 4:5]))
                else:
                    for m in range(2):
                        ins = nc.scalar.activation(e[:, m, 0:nk], psum[:, 2 * (u % 2) + m, 0:nk], ACT.Exp,
                                                   bias=c[:, 2 + m:3 + m], scale=32 ** -0.5, accum_out=c[:, 4 + m:5 + m])
                    link(ins)
                act.sem_inc(*exr.one())

            def read_turned(u):
                _, nk = span(u)
                act.wait_ge(*tp.at(u + 1))
                if u >= 2:
                    act.wait_ge(*ov.at(u - 1))
                nc.scalar.activation(ETb[u % 2][:, 0:nk], psum[:, 4 + u % 2, 0:nk], ACT.Copy).then_inc(*tpr.one())

            for u in range(U + 3):
                if u < U:
                    exps(u)
                if u >= 3:
                    read_turned(u - 3)

        @block.vector
        def _(dve):
            link = linker(dve, sig("dve_chain"))

            def maxima(u):
                kind, t, h = units[u]
                _, nk = span(u)
                c = scalars(u)
                dve.wait_ge(*scr.at(u + 1))
                if kind == "B":
                    if u >= 3:
                        dve.wait_ge(*tp.at(u - 2))
                    so, ps = Eb[u % 3][:, 1, 0:nk], psum[:, 2 * (u % 2), 0:nk]
                    if t < 2:
                        link(nc.vector.scalar_tensor_tensor(so, ps, 0.125, cn("window", t * BANK, BANK), ALU.mult, ALU.add))
                    else:
                        link(nc.vector.tensor_scalar(so, ps, 0.125, None, ALU.mult))
                    link(nc.vector.tensor_reduce(c[:, 0:1], so, AX.X, ALU.max))
                    link(nc.vector.tensor_scalar(c[:, 2:3], c[:, 0:1], pr(f"sink{i}", h), -1.0, ALU.max, ALU.mult))
                else:
                    link(nc.vector.tensor_reduce(c[:, 0:2], psum[:, 2 * (u % 2):2 * (u % 2) + 2, 0:nk], AX.X, ALU.max))
                    link(nc.vector.tensor_scalar(c[:, 2:4], c[:, 0:2], -(32 ** -0.5), None, ALU.mult))
                dve.sem_inc(*mxr.one())

            def weigh(u):
                kind, t, h = units[u]
                _, nk = span(u)
                c, e = scalars(u), Eb[u % 3]
                dve.wait_ge(*exr.at(u + 1))
                if kind == "B":
                    link(nc.vector.tensor_tensor(c[:, 6:7], c[:, 3:4], c[:, 4:5], ALU.add))
                    link(nc.vector.reciprocal(c[:, 7:8], c[:, 6:7]))
                else:
                    link(nc.vector.reciprocal(c[:, 6:8], c[:, 4:6]))
                    nc.vector.tensor_scalar(e[:, 0, 0:nk], e[:, 0, 0:nk], c[:, 6:7], None, ALU.mult)
                    link(nc.vector.tensor_scalar(c[:, 8:9], c[:, 7:8], lamc[:, 2:3], None, ALU.mult))
                    link(nc.vector.scalar_tensor_tensor(e[:, 0, 0:nk], e[:, 1, 0:nk], c[:, 8:9], e[:, 0, 0:nk],
                                                        ALU.mult, ALU.add))
                dve.sem_inc(*pdr.one())

            def result(u):
                kind, t, h = units[u]
                c = scalars(u)
                dve.wait_ge(*ov.at(u + 1))
                if kind == "B":
                    ps = psum[:, 6 + u % 2, 64 * (h // 4):64 * (h // 4) + 64]
                    link(nc.vector.tensor_scalar(cat[:, t, 256 + 64 * h:320 + 64 * h], ps, c[:, 7:8], None, ALU.mult))
                else:
                    ps = psum[:, 6 + u % 2, 64 * (h % 2):64 * (h % 2) + 64]
                    link(nc.vector.tensor_copy(cat[:, t, 768 + 64 * h:832 + 64 * h], ps))
                dve.sem_inc(*ovr.one())

            for u in range(U + 4):
                if u < U:
                    maxima(u)
                if 1 <= u <= U:
                    weigh(u - 1)
                if u >= 4:
                    result(u - 4)

    ns = sig("subln_steps")
    with core.phase() as block:

        @block.scalar
        def _(act):
            act.wait_ge(*ns.at(1))
            nc.scalar.activation(small[:, 0:4 * NQ], small[:, 0:4 * NQ], ACT.Sqrt, scale=1.0 / 64, bias=core.eps[:, 0:1])\
                .then_inc(*ns.one())

        @block.vector
        def _(dve):
            link = linker(dve, sig("dve_chain"))
            cc = cat[:, 0:NQ, 768:1024]
            s3 = core.norm_rt[:, 0:NQ * 256].rearrange("p (t c) -> p t c", t=NQ)
            link(nc.vector.tensor_tensor(s3, cc, cc, ALU.mult))
            link(nc.vector.tensor_reduce(small[:, 0:4 * NQ], core.norm_rt[:, 0:NQ * 256].rearrange("p (g c) -> p g c", c=64),
                                         AX.X, ALU.add))
            dve.sem_inc(*ns.one())
            dve.wait_ge(*ns.at(2))
            link(nc.vector.reciprocal(small[:, 0:4 * NQ], small[:, 0:4 * NQ]))
            link(nc.vector.tensor_scalar(small[:, 0:4 * NQ], small[:, 0:4 * NQ], 1.0 - lam_init, None, ALU.mult))
            for t in range(NQ):
                c3 = cat[:, t, 768:1024].rearrange("p (h c) -> p h c", h=4)
                link(nc.vector.tensor_tensor(c3, c3, small[:, 4 * t:4 * t + 4].unsqueeze(2).broadcast_to([P, 4, 64]), ALU.mult))
                link(nc.vector.tensor_tensor(c3, c3, pr(f"subln{i}", 0, 64).unsqueeze(1).broadcast_to([P, 4, 64]), ALU.mult))

    catT = view(0, DT, 512)
    ct, ctr = sig("cat_turned"), sig("cat_read")
    T = NQ * P
    with core.phase() as block:

        @block.tensor
        def _(pe):
            for j in range(DT):
                for t in range(NQ):
                    mm = nc.tensor.transpose(psum[:, j, t * P:(t + 1) * P], cat[:, t, j * P:(j + 1) * P], ident)
                mm.then_inc(*ct.one())

        @block.scalar
        def _(act):
            for j in range(DT):
                act.wait_ge(*ct.at(j + 1))
                nc.scalar.activation(catT[:, j, 0:T], psum[:, j, 0:T], ACT.Copy)

    def residual(part):
        def f(dve, link, n_, ps):
            for s_ in range(T // S):
                ins = nc.vector.scalar_tensor_tensor(X[:, n_, s_ * S:(s_ + 1) * S], ps[:, s_ * S:(s_ + 1) * S],
                                                     adaM[:, part * DT + n_, s_:s_ + 1], X[:, n_, s_ * S:(s_ + 1) * S],
                                                     ALU.mult, ALU.add)
                if s_ < T // S - 1:
                    link(ins)
            return ins
        return f

    project(core, catT, T, [512] * 2, DT, on_dve=residual(2))
    feed_forward(core, X, H, view, T, None, None, lambda k, t: pr(f"cw{i}", k * 44 + t), lambda t: pr(f"cb{i}", t), 1,
                 residual(5), ctx_pars=lambda: modulated(1, T))


def constants():
    con = {}
    con["ident"] = np.eye(P, dtype=np.float32)
    s, t = np.meshgrid(np.arange(P), np.arange(P), indexing="ij")
    con["causal"] = (s <= t).astype(np.float32)
    win = np.zeros((P, 2, BANK), np.float32)
    for qt in range(2):
        qpos, kpos = qt * P + np.arange(P)[:, None], np.arange(S)[None, :]
        win[:, qt, 0:S] = np.where(np.abs(qpos - kpos) <= P, 0.0, -1e30)
    con["window"] = win.reshape(P, -1)
    for name, w in (("b", 64), ("c", 32)):
        nf = w // 4
        row, col = np.repeat(np.arange(S // 64), 64), np.tile(np.arange(64), S // 64)
        inv = (np.float32(10000.0) ** (-np.arange(nf, dtype=np.float32) / np.float32(nf))).astype(np.float32)
        ang = np.stack([row[:, None].astype(np.float32) * inv, col[:, None].astype(np.float32) * inv], axis=1)
        cos, sin = np.cos(ang).astype(np.float32), np.sin(ang).astype(np.float32)
        cos2 = np.stack([cos, cos], axis=2).reshape(2, P, w)
        sin2 = np.stack([-sin, sin], axis=2).reshape(2, P, w)
        con["cos_" + name] = cos2.transpose(1, 0, 2).reshape(P, -1)
        con["sin_" + name] = sin2.transpose(1, 0, 2).reshape(P, -1)
    lev = np.zeros((P, len(LEVELS) + 1, P), np.uint32)
    for n, L in enumerate(LEVELS):
        lev[:, n] = ((s // L) % 2 == 0) & (t // L == s // L + 1)
    lev[:, -1] = s == t
    return np.concatenate([con[n] for n, _ in CONS], axis=1), lev.reshape(P, -1)


def columns(v):
    v = np.asarray(v)
    return v.reshape(-1, P).T


def chunked(w, cols=512):
    w = np.asarray(w)
    w = w.reshape(-1, w.shape[-2], w.shape[-1])
    L, K, N = w.shape
    w = w.reshape(L, K // P, P, N // cols, cols).transpose(0, 3, 2, 1, 4)
    return np.ascontiguousarray(w).reshape(L * (N // cols), P, -1)


def paired(w):
    w = np.asarray(w)
    w = w.reshape(-1, D, 2, FFT // 2, 256).transpose(0, 1, 3, 2, 4)
    return chunked(np.ascontiguousarray(w).reshape(-1, D, 2 * FF))


def lay_out(i):
    w_in = np.asarray(i["w_in"])[0]
    big = np.concatenate([w_in[:, 0:6144], w_in[:, 6152:7176], w_in[:, 7176:10248], w_in[:, 10264:]], axis=1)
    small_w = np.concatenate([w_in[:, 6144:6152], w_in[:, 10248:10264]], axis=1)
    pad = lambda v: np.concatenate([np.asarray(v).reshape(-1), np.zeros(P - np.asarray(v).size, np.float32)])[:, None]
    rows = lambda v: np.broadcast_to(np.asarray(v).reshape(1, -1), (P, np.asarray(v).size))
    taps = lambda w: np.concatenate([columns(r) for r in np.asarray(w)], axis=1)
    gb = np.asarray(i["ml_gate_b"])[0]
    p = {
        "norm1": columns(i["norm1_g"][0]), "hg_norm": columns(i["hg_norm_g"][0]), "ml_w": taps(i["ml_conv_w"][0]),
        "ml_b": columns(i["ml_conv_b"][0]), "ml_norm": columns(i["ml_norm_g"][0]), "mb_w": taps(i["mb_conv_w"][0]),
        "mb_b": columns(i["mb_conv_b"][0]), "mb_norm": columns(i["mb_norm_g"][0]), "norm2": columns(i["norm2_g"][0]),
        "ff_w": taps(i["ffn_conv_w"][0]), "ff_b": columns(i["ffn_conv_b"][0]), "final": columns(i["final_g"]),
        "mb_d": columns(np.repeat(np.asarray(i["mb_d"])[0], MB_P)),
        "gate_i": pad(gb[:ML_H]), "gate_f": pad(gb[ML_H:]), "dt_bias": pad(i["mb_dt_bias"]), "a_log": pad(i["mb_a_log"]),
        "w_gates": small_w.reshape(DT, P, 24).transpose(1, 0, 2).reshape(P, -1),
        "cond": np.stack([columns(i["c_2"][0]), columns(i["c_ctx_2"])], axis=2).reshape(P, -1),
    }
    for n in range(LAYERS):
        bq, bk = np.asarray(i["b_qnorm_2"])[n], np.asarray(i["b_knorm_2"])[n]
        cq, ck = np.asarray(i["c_qnorm_2"])[n], np.asarray(i["c_knorm_2"])[n]
        p |= {
            f"norm1_{n}": columns(i["norm1_g_2"][n]), f"norm2_{n}": columns(i["norm2_g_2"][n]),
            f"b_ada{n}": columns(i["b_ada_2"][n]), f"cw{n}": taps(i["conv_w_2"][n][:, 0]), f"cb{n}": columns(i["conv_b_2"][n]),
            f"a_bs{n}": np.asarray(i["a_bs_2"])[n].T,
            f"a_ws{n}": np.asarray(i["a_ws_2"])[n].transpose(2, 0, 1).reshape(P, -1),
            f"gain_b{n}": rows(np.concatenate([bq, bk])),
            f"gain_c{n}": rows(np.concatenate([cq, ck])),
            f"subln{n}": rows(i["c_subln_2"][n]), f"sink{n}": rows(i["b_sink_2"][n]), f"lam{n}": rows(i["c_lam_2"][n]),
        }
    con, lev = constants()
    return {
        "x": np.asarray(i["x"])[0].T, "ctx": np.asarray(i["ctx_2"])[0].T,
        "par": np.concatenate([p[n] for n, _ in PARS], axis=1), "con": con, "levels": lev,
        "w_in": chunked(big), "w_br_hg": chunked(i["w_br_hg"]), "w_br_ml": chunked(i["w_br_ml"]),
        "w_br_mb": chunked(i["w_br_mb"]), "w_out": chunked(i["w_out"]), "w_up": paired(i["w_up"]),
        "w_down": chunked(i["w_down"], P), "w_ada_2": chunked(i["w_ada_2"]), "w_in_2": chunked(i["w_in_2"]),
        "w_out_2": chunked(i["w_out_2"]), "w_up_2": paired(i["w_up_2"]), "w_down_2": chunked(i["w_down_2"], P),
    }


def kernel(**inputs):
    import concourse.bacc as bacc
    from concourse.bass_utils import run_bass_kernel_spmd

    nc = bacc.Bacc("TRN2", target_bir_lowering=False, num_devices=1)
    arrays, aps = {}, {}
    for name, v in lay_out(inputs).items():
        v = np.ascontiguousarray(v)
        arrays[f"in_{name}"] = v
        aps[name] = nc.dram_tensor(f"in_{name}", v.shape, mybir.dt.from_np(v.dtype), kind="ExternalInput").ap()
    out = nc.dram_tensor("out", (D, S), F32, kind="ExternalOutput").ap()
    build(nc, aps, out)
    r = run_bass_kernel_spmd(nc, [arrays], core_ids=[0])
    return np.ascontiguousarray(r.results[0]["out"].T).reshape(1, S, D)
```

```python
from contextlib import ExitStack, contextmanager

import numpy as np

import concourse.bass as bass
from concourse import mybir

F32 = mybir.dt.float32
F32R = mybir.dt.float32r
U8 = mybir.dt.uint8
ALU = mybir.AluOpType
ACT = mybir.ActivationFunctionType
AX = mybir.AxisListType

P = 128
D = 1024
DT = D // P
S = 256
ST = S // P
EPS = 1e-6

HG_H = 8
ML_H, ML_DV = 4, 256
MB_H, MB_P, MB_G = 16, 64, 4
FF = 2816
FFT = FF // P
N_ADA = 6 * DT
RING = 3
UNIT = 256
SLOT = DT * UNIT
FFH = FFT // 2
BANK = 512
LEVELS = [64, 32, 16, 8, 4, 2, 1]
LAYERS = 2
ARENA = 16896


class Signal:

    def __init__(self, handle):
        self.handle, self.base, self.total = handle, 0, 0

    def one(self):
        self.total += 1
        return self.handle, 1

    def dma(self):
        self.total += 16
        return self.handle, 16

    def at(self, n):
        return self.handle, self.base + n


class Core:

    def __init__(self, nc, ctx):
        self.nc, self.ctx, self.signals = nc, ctx, {}
        self.psum = ctx.enter_context(nc.psum_tensor("acc_psum", [P, 8, BANK], F32))
        self.ring = self.sbuf("ring", [P, RING, SLOT])
        self.loaded = [self.sig(f"weights_loaded_{i}") for i in range(RING)]
        self.high, self.low = (self.sbuf(n, [P, 2, SLOT], F32R) for n in ("w_high", "w_low"))
        self.high_ready, self.low_ready = self.sig("weights_high_ready"), self.sig("weights_low_ready")
        self.stream = []
        self.released = 0
        self.taken = 0

    def sbuf(self, name, shape, dt=F32):
        return self.ctx.enter_context(self.nc.sbuf_tensor(name + "_sb", shape, dt))

    def sig(self, name):
        if name not in self.signals:
            self.signals[name] = Signal(self.ctx.enter_context(self.nc.semaphore(name)))
        return self.signals[name]

    @contextmanager
    def phase(self):
        with self.nc.Block() as block:
            yield block
        for s in self.signals.values():
            s.base = s.total

    def load(self, sp, c):
        if c < len(self.stream):
            src = self.stream[c][0]
            sp.dma_start(self.ring[:, c % RING, 0:src.shape[1]], src).then_inc(*self.loaded[c % RING].dma())

    def wait_loaded(self, eng, c):
        eng.wait_ge(self.loaded[c % RING].handle, 16 * (c // RING + 1))

    def place(self, g):
        split = [c for c, (_, y) in enumerate(self.stream) if y]
        return split[g] if g < len(split) else None

    def pieces(self, c):
        n = self.stream[c][0].shape[1]
        m = n // 2 if n == SLOT else (FFH + 1) // 2 * P
        return slice(0, m), slice(m, n)

    def split_high(self, act, g):
        c = self.place(g)
        if c is None:
            return
        self.wait_loaded(act, c)
        for piece in self.pieces(c):
            self.nc.scalar.activation(self.high[:, g % 2, piece], self.ring[:, c % RING, piece], ACT.Copy)\
                .then_inc(*self.high_ready.one())

    def split_low(self, eng, g):
        c = self.place(g)
        if c is None:
            return
        for i, piece in enumerate(self.pieces(c)):
            eng.wait_ge(self.high_ready.handle, 2 * g + i + 1)
            eng.tensor_tensor(self.low[:, g % 2, piece], self.ring[:, c % RING, piece],
                              self.high[:, g % 2, piece].bitcast(F32), ALU.subtract).then_inc(*self.low_ready.one())

    def wait_parts(self, pe, g, k, kt):
        if k in (0, (kt + 1) // 2):
            pe.wait_ge(self.low_ready.handle, 2 * g + (1 if k == 0 else 2))

    def release(self, sp, g, side=None):
        c1 = self.place(g)
        c1 = len(self.stream) - 1 if c1 is None else c1
        n = 0
        for c in range(self.released, c1 + 1):
            if self.stream[c][1]:
                sp.wait_ge(self.low_ready.handle, 2 * sum(y for _, y in self.stream[:c + 1]))
            else:
                n += 1
                sp.wait_ge(*side.scaled.at(n))
            self.load(sp, c + RING)
        self.released = c1 + 1

    def parts(self, g, kt, n):
        v = lambda t: t[:, g % 2, 0:kt * n].rearrange("p (k n) -> p k n", k=kt)
        return v(self.high), v(self.low)


def product(nc, out, stationary, moving, start, stop):
    (sh, sl), (mh, ml) = stationary, moving
    nc.tensor.matmul(out, sh, mh, start=start, stop=False)
    nc.tensor.matmul(out, sh, ml, start=False, stop=False)
    return nc.tensor.matmul(out, sl, mh, start=False, stop=stop)


def linker(eng, signal):
    start = signal.total

    def link(ins):
        ins.then_inc(*signal.one())
        eng.wait_ge(*signal.at(signal.total - signal.base))
        return ins

    return link


class Modulation:

    def __init__(self, core, cond, bias, result, sums):
        self.core, self.cond, self.bias, self.result, self.sums = core, cond, bias, result, sums
        self.taken = 0
        self.scaled, self.summed = core.sig("mod_scaled"), core.sig("mod_summed")

    def scale(self, dve, link, n, slot):
        nc = self.core.nc
        if n >= 2:
            dve.wait_ge(*self.summed.at(n - 1))
        for k in range(DT):
            for s in range(2):
                dst, c = self.sums[:, n % 2, s, :], self.cond[:, k, s:s + 1]
                if k == 0:
                    ins = nc.vector.tensor_scalar(dst, slot[:, k, :], c, None, ALU.mult)
                else:
                    ins = nc.vector.scalar_tensor_tensor(dst, slot[:, k, :], c, dst, ALU.mult, ALU.add)
            link(ins)
        dve.sem_inc(*self.scaled.one())

    def reduce(self, pe, n, m):
        nc = self.core.nc
        pe.wait_ge(*self.scaled.at(n + 1))
        for j in range(UNIT // P):
            for s in range(2):
                o = 2 * (UNIT // P * m + j) + s
                mm = nc.tensor.matmul(self.core.psum[:, 7, o:o + 1], self.sums[:, n % 2, s, j * P:(j + 1) * P],
                                      self.core.ones[:, 0:1], start=True, stop=True)
        mm.then_inc(*self.summed.one())

    def read(self, dve, n, m0):
        nc = self.core.nc
        dve.wait_ge(*self.summed.at(n))
        t0, t1 = UNIT // P * m0, UNIT // P * (m0 + n)
        ps = self.core.psum[:, 7, 2 * t0:2 * t1].rearrange("p (t s) -> p t s", s=2)
        nc.vector.tensor_tensor(self.result[:, t0:t1, :], ps, self.bias[:, t0:t1, :].broadcast_to([P, t1 - t0, 2]), ALU.add)


class Norm:
    SQUARES = 4
    BUFFERS = 4

    def __init__(self, core, src, ntile, m, W, gain, out, shift=None, gate=None, parts=None):
        self.core, self.src, self.ntile, self.m, self.W = core, src, ntile, m, W
        self.gain, self.out, self.shift, self.gate, self.parts = gain, out, shift, gate, parts
        self.groups = ntile // m
        self.sq_ready, self.sq_used, self.root, self.value, self.high, self.low = (core.sig(n) for n in (
            "norm_sq_ready", "norm_sq_used", "norm_root_ready", "norm_value_ready", "norm_high_ready", "norm_low_ready"))
        self.rt = core.norm_rt[:, 0:self.groups * W].rearrange("p (g w) -> p g w", g=self.groups)
        self.reciprocals = 0

    def roots(self, act):
        core, sq, W = self.core, self.core.norm_sq, self.W
        for t in range(self.ntile):
            if t >= self.SQUARES:
                act.wait_ge(*self.sq_used.at(t - self.SQUARES + 1))
            core.nc.scalar.activation(sq[:, t % self.SQUARES, 0:W], self.src(t), ACT.Square).then_inc(*self.sq_ready.one())
        for g in range(self.groups):
            act.wait_ge(*self.sq_used.at((g + 1) * self.m))
            core.nc.scalar.activation(self.rt[:, g, :], core.psum[:, g, 0:W], ACT.Sqrt, scale=1.0 / (P * self.m),
                                      bias=core.eps[:, 0:1]).then_inc(*self.root.one())

    def sums(self, pe):
        core, m, W = self.core, self.m, self.W
        for t in range(self.ntile):
            pe.wait_ge(*self.sq_ready.at(t + 1))
            core.nc.tensor.matmul(core.psum[:, t // m, 0:W], core.ones[:, :], core.norm_sq[:, t % self.SQUARES, 0:W],
                                  start=(t % m == 0), stop=(t % m == m - 1)).then_inc(*self.sq_used.one())

    def highs(self, act, tiles):
        for t in tiles:
            act.wait_ge(*self.value.at(t + 1))
            self.core.nc.scalar.activation(self.parts[0](t), self.out(t), ACT.Copy).then_inc(*self.high.one())

    def values(self, dve, link, tiles):
        nc, m = self.core.nc, self.m
        for t in tiles:
            g = t // m
            if self.reciprocals == g:
                dve.wait_ge(*self.root.at(g + 1))
                link(nc.vector.reciprocal(self.rt[:, g, :], self.rt[:, g, :]))
                self.reciprocals += 1
            if self.parts and t >= self.BUFFERS:
                dve.wait_ge(*self.low.at(t - self.BUFFERS + 1))
            out = self.out(t)
            ins = nc.vector.scalar_tensor_tensor(out, self.src(t), self.gain(t), self.rt[:, g, :], ALU.mult, ALU.mult)
            if self.gate:
                link(ins)
                ins = nc.vector.tensor_tensor(out, out, self.gate(t), ALU.mult)
            if self.shift:
                link(ins)
                ins = nc.vector.tensor_scalar(out, out, self.shift(t), None, ALU.add)
            if self.parts:
                ins.then_inc(*self.value.one())

    def lows(self, eng, tiles):
        for t in tiles:
            eng.wait_ge(*self.high.at(t + 1))
            eng.tensor_tensor(self.parts[1](t), self.out(t), self.parts[0](t).bitcast(F32), ALU.subtract)\
                .then_inc(*self.low.one())


def norm_fm(core, *args, **kw):
    norm = Norm(core, *args, **kw)
    with core.phase() as block:

        @block.scalar
        def _(act):
            norm.roots(act)

        @block.tensor
        def _(pe):
            norm.sums(pe)

        @block.vector
        def _(dve):
            norm.values(dve, linker(dve, core.sig("dve_chain")), range(norm.ntile))


def project(core, x, T, units, fm=True, kt=DT, on_act=None, on_dve=None, then_act=None, tok_tiles=None, side=None,
            every=1, halves=None, low="pool",
            norm=None, needed=True):
    nc = core.nc
    acc, free = core.sig("proj_acc_ready"), core.sig("proj_bank_free")
    mid, midfree = core.sig("proj_mid_ready"), core.sig("proj_mid_free")
    past = core.sig("proj_first_half_done")
    g0 = core.taken
    core.taken += units
    cols = P if halves else UNIT
    kt = FFH if halves else kt
    each = norm.ntile // units if norm and not needed else 0
    m0 = 0
    if side:
        m0 = side.taken
        side.taken += units // every
    rides = list(range(every - 1, units, every)) if side else []
    steps = []
    for n in range(units):
        if halves == "both":
            steps.append((n, 0, FFH * (n % 2), n % 2 == 0, n % 2 == 1))
        else:
            for j in (range(cols // P) if fm else tok_tiles(n) if tok_tiles else range(ST)):
                steps.append((n, j, 0, True, True))
    tiles = [(n, j) for n, j, _, _, closes in steps if closes]
    done_by = [sum(1 for n, *_, closes in steps if closes and n <= u) for u in range(units)]
    BANKS = 7 if side else 8

    def bank(i):
        return core.psum[:, i % BANKS, :]

    with core.phase() as block:

        @block.sync
        def _(sp):
            core.release(sp, g0 + units, side)

        @block.tensor
        def _(pe):
            i, seen = 0, set()
            if norm:
                norm.sums(pe)
            if norm and not needed:
                pe.wait_ge(*norm.root.at(norm.groups))
            for s_, (n, j, k0, opens, closes) in enumerate(steps):
                w = core.parts(g0 + n, kt, cols)
                fresh = s_ == 0 or steps[s_ - 1][0] != n
                if opens and i >= BANKS:
                    pe.wait_ge(*free.at(i - BANKS + 1))
                first_use = norm and needed and (0 if fm else j // ST) not in seen
                seen.add(0 if fm else j // ST)
                for k in range(kt):
                    if fresh:
                        core.wait_parts(pe, g0 + n, k, kt)
                    if first_use:
                        pe.wait_ge(*norm.low.at((j // ST * DT if not fm else norm.ntile - DT) + k + 1))
                    if fm:
                        mm = product(nc, bank(i)[:, 0:T], [p[:, k, j * P:(j + 1) * P] for p in w],
                                     [p[:, k0 + k, 0:T] for p in x], opens and k == 0, closes and k == kt - 1)
                    else:
                        mm = product(nc, bank(i)[:, 0:cols], [p[:, k, j * P:(j + 1) * P] for p in x],
                                     [p[:, k, :] for p in w], k == 0, k == kt - 1)
                if closes:
                    mm.then_inc(*acc.one())
                    i += 1
                else:
                    mm.then_inc(*past.one())
                if n - 1 in rides and (s_ + 1 == len(steps) or steps[s_ + 1][0] != n):
                    side.reduce(pe, rides.index(n - 1), m0 + rides.index(n - 1))
            if units - 1 in rides:
                side.reduce(pe, len(rides) - 1, m0 + len(rides) - 1)

        @block.scalar
        def _(act):
            i = 0
            if norm:
                norm.roots(act)
            if norm and needed:
                norm.highs(act, range(norm.ntile))
            for n in range(units):
                if n + 1 >= 2:
                    if halves == "both":
                        if n % 2 == 0:
                            act.wait_ge(*acc.at(n // 2))
                        else:
                            act.wait_ge(*past.at(n // 2 + 1))
                    elif done_by[n - 1]:
                        act.wait_ge(*acc.at(done_by[n - 1]))
                core.split_high(act, g0 + n + 1)
                while i < len(tiles) and (tiles[i][0] < n or n == units - 1):
                    if on_act:
                        act.wait_ge(*acc.at(i + 1))
                        on_act(act, i, tiles[i][0], tiles[i][1], bank(i)).then_inc(*free.one())
                    elif then_act:
                        act.wait_ge(*mid.at(i + 1))
                        then_act(act, i).then_inc(*midfree.one())
                    i += 1
                if each:
                    norm.highs(act, range(each * n, each * (n + 1)))

        @block.gpsimd
        def _(pool):
            if norm and needed:
                norm.lows(pool, range(norm.ntile))
            for n in range(units):
                if low == "pool":
                    core.split_low(pool, g0 + n + 1)
                if each:
                    norm.lows(pool, range(each * n, each * (n + 1)))

        @block.vector
        def _(dve):
            link = linker(dve, core.sig("dve_chain"))
            i = 0
            if norm and needed:
                norm.values(dve, link, range(norm.ntile))
            for n in range(units):
                if low == "dve":
                    core.split_low(dve, g0 + n + 1)
                if n + every - 1 in rides:
                    c = core.place(g0 + n + every - 1) + 1
                    core.wait_loaded(dve, c)
                    side.scale(dve, link, n // every, core.ring[:, c % RING, :].rearrange("p (k n) -> p k n", k=DT))
                if each:
                    norm.values(dve, link, range(each * n, each * (n + 1)))
                while on_dve and i < len(tiles) and tiles[i][0] == n:
                    dve.wait_ge(*acc.at(i + 1))
                    if then_act and i >= 2:
                        dve.wait_ge(*midfree.at(i - 1))
                    link(on_dve(dve, link, i, bank(i)))
                    dve.sem_inc(*free.one())
                    if then_act:
                        dve.sem_inc(*mid.one())
                    i += 1
            if side:
                side.read(dve, len(rides), m0)


def split_fm(core, src, parts):
    nc = core.nc
    hi = core.sig("split_high_ready")
    with core.phase() as block:

        @block.scalar
        def _(act):
            for t in range(0, DT, 2):
                nc.scalar.activation(parts[0][:, t:t + 2, :], src[:, t:t + 2, :], ACT.Copy).then_inc(*hi.one())

        @block.vector
        def _(dve):
            for t in range(0, DT, 2):
                dve.wait_ge(*hi.at(t // 2 + 1))
                nc.vector.tensor_tensor(parts[1][:, t:t + 2, :], src[:, t:t + 2, :], parts[0][:, t:t + 2, :].bitcast(F32),
                                        ALU.subtract)


def pack_columns(items):
    at, n = {}, 0
    for name, w in items:
        at[name] = (n, w)
        n += w
    return at, n


PARS = [("norm1", DT), ("hg_norm", 1), ("ml_w", 4 * DT), ("ml_b", DT), ("ml_norm", 2), ("mb_w", 4 * 16),
        ("mb_b", 16), ("mb_norm", DT), ("norm2", DT), ("ff_w", 3 * 44), ("ff_b", 44), ("final", DT), ("mb_d", DT),
        ("gate_i", 1), ("gate_f", 1), ("dt_bias", 1), ("a_log", 1), ("w_gates", DT * 80), ("cond", 2 * DT)]
for _i in range(LAYERS):
    PARS += [(f"{n}{_i}", w) for n, w in (
        ("norm1_", DT), ("norm2_", DT), ("b_ada", N_ADA), ("cw", 132), ("cb", 44), ("a_bs", 4),
        ("gain_b", 128), ("gain_c", 64), ("subln", 64), ("sink", 8), ("lam", 128))]
PAR_AT, PAR_N = pack_columns(PARS)
CONS = [("ident", P), ("causal", P), ("window", 2 * BANK), ("cos_b", 2 * 64), ("sin_b", 2 * 64),
        ("cos_c", 2 * 32), ("sin_c", 2 * 32)]
CON_AT, CON_N = pack_columns(CONS)
LEV_N = (len(LEVELS) + 1) * P


def build(nc, a, out):
    with ExitStack() as ctx:
        core = Core(nc, ctx)
        sb, sig = core.sbuf, core.sig
        par = sb("par", [P, PAR_N])
        con = sb("con", [P, CON_N])
        X = sb("X", [P, DT, 2 * S])
        H = tuple(sb(n, [P, DT, 2 * S], F32R) for n in ("h_high", "h_low"))
        core.ones = sb("ones", [P, P])
        core.eps = sb("eps", [P, 1])
        core.norm_sq = sb("norm_sq", [P, 4, 512])
        core.norm_rt = sb("norm_rt", [P, 2048])
        adaM = [sb(f"modulation{i}", [P, N_ADA, 2]) for i in range(LAYERS)]
        cond = sb("cond", [P, DT, 2])
        mod_sums = core.mod_sums = sb("mod_sums", [P, 2, 2, UNIT])
        small = sb("small", [P, 64])
        core.gate_columns = sb("gate_columns", [P, ST, 3, MB_H])
        core.mod_gains = sb("mod_gains", [P, 2, DT, 2])
        core.lam = sb("lam", [P, 4])

        def pr(name, i=0, n=1):
            o = PAR_AT[name][0] + i
            return par[:, o:o + n]

        def pv(name, a_):
            o, w = PAR_AT[name]
            return par[:, o:o + w].rearrange("p (a b) -> p a b", a=a_)

        def cn(name, i=0, n=None):
            o, w = CON_AT[name]
            return con[:, o + i:o + i + (w if n is None else n)]

        def view(o, a_, b_):
            assert o + a_ * b_ <= ARENA, (o, a_, b_)
            return core.arena[:, o:o + a_ * b_].rearrange("p (a b) -> p a b", a=a_)

        ident = cn("ident")
        causal = cn("causal")

        stream, counts = core.stream, [0, 0]
        NM = N_ADA * P // UNIT

        def add(name, idx, layer=None, every=1):
            for i, n in enumerate(idx):
                stream.append((a[name][n], True))
                if layer is not None and i % every == every - 1:
                    stream.append((a["w_ada_2"][NM * layer + counts[layer]], False))
                    counts[layer] += 1

        add("w_in", range(0, 16), 0, 2)
        add_gate = lambda b: add("w_in", range(40 + 4 * b, 44 + 4 * b), 0, 2)
        add_gate(0)
        add("w_br_hg", range(4), 0, 2)
        add("w_in", range(16, 20))
        add("w_in", range(20, 28), 0, 2)
        add_gate(1)
        add("w_br_ml", range(4), 0, 2)
        add("w_in", range(28, 32), 0, 2)
        add("w_in", range(32, 40))
        add_gate(2)
        add("w_br_mb", range(4), 1, 2)
        add("w_out", range(4), 1, 2)
        add("w_up", range(FFT))
        add("w_down", range(2 * DT))
        for i in range(LAYERS):
            add("w_in_2", range(8 * i, 8 * i + 8))
            add("w_out_2", range(4 * i, 4 * i + 4), 1 if i == 0 else None)
            up0, down0 = FFT * i, 2 * DT * i
            if i < LAYERS - 1:
                for half in range(2):
                    add("w_up_2", range(up0 + FFH * half, up0 + FFH * (half + 1)))
                    add("w_down_2", range(down0 + half, down0 + 2 * DT, 2), 1)
            else:
                add("w_up_2", range(up0, up0 + FFT))
                add("w_down_2", range(down0, down0 + 2 * DT))
        assert counts == [NM, NM]

        in_ready = sig("inputs_ready")
        with core.phase() as block:

            @block.sync
            def _(sp):
                sp.dma_start(X[:, :, 0:S], a["x"].rearrange("(k p) t -> p k t", p=P)).then_inc(*in_ready.dma())
                sp.dma_start(par[:, :], a["par"]).then_inc(*in_ready.dma())
                sp.dma_start(con[:, :], a["con"]).then_inc(*in_ready.dma())
                for c in range(RING):
                    core.load(sp, c)
                sp.wait_ge(*in_ready.at(48))
                core.release(sp, 0)

            @block.vector
            def _(dve):
                nc.vector.memset(core.ones[:, :], 1.0)
                nc.vector.memset(core.eps[:, :], EPS)

            @block.scalar
            def _(act):
                act.wait_ge(*in_ready.at(48))
                nc.scalar.activation(cond[:, :, :], pv("cond", DT), ACT.Silu)
                core.split_high(act, 0)

            @block.gpsimd
            def _(pool):
                core.split_low(pool, 0)

        mods = [Modulation(core, cond, pv(f"b_ada{i}", N_ADA), adaM[i], mod_sums) for i in range(LAYERS)]
        @contextmanager
        def arena(name):
            with nc.sbuf_tensor(name, [P, ARENA], F32) as core.arena:
                yield
            core.arena = None

        with arena("arena_hybrid"):
            hybrid_block(core, a, X, H, pr, pv, cn, view, ident, causal, small, mods)
        feed_forward(core, "1", stream_norm(core, X, H, S, lambda t: pr("norm2", t)), X, H, S, lambda k, t: pr("ff_w", k * 44 + t), lambda t: pr("ff_b", t), 2,
                     lambda dve, link, i, ps: nc.vector.tensor_tensor(X[:, i, 0:S], ps[:, 0:S], X[:, i, 0:S], ALU.add))
        load_context(core, a, X)
        for i in range(LAYERS):
            attention_layer(core, a, i, X, H, pr, pv, cn, view, arena, ident, small, adaM[i], mods[1] if i == 0 else None)
        stored = sig("output_stored")
        with core.phase() as block:

            @block.sync
            def _(sp):
                sp.dma_start(out.rearrange("(k p) t -> p k t", p=P), X[:, :, 0:S]).then_inc(*stored.dma())
                sp.wait_ge(*stored.at(16))


def hybrid_block(core, a, X, H, pr, pv, cn, view, ident, causal, small, mods):
    nc, sig, psum = core.nc, core.sig, core.psum
    W8 = DT * S
    Y = tuple(p[:, :, S:2 * S] for p in H)
    Yt = tuple(lambda t, p=p: p[:, t, S:2 * S] for p in H)
    spare = X[:, :, S:2 * S]
    gate, mixed = view(0, DT, S), view(W8, DT, S)
    tmpm = core.norm_rt[:, 0:S]

    def merge(bi, norm=None):
        project(core, H, S, 4, on_act=lambda act, i, n, j, ps: nc.scalar.activation(gate[:, i, :], ps[:, 0:S], ACT.Sigmoid),
                side=mods[0], every=2, norm=norm, needed=False)

        def gated(dve, link, i, ps):
            if bi == 0:
                return nc.vector.tensor_tensor(mixed[:, i, :], ps[:, 0:S], gate[:, i, :], ALU.mult)
            link(nc.vector.tensor_tensor(tmpm, ps[:, 0:S], gate[:, i, :], ALU.mult))
            return nc.vector.tensor_tensor(mixed[:, i, :], mixed[:, i, :], tmpm, ALU.add)

        project(core, Y, S, 4, on_dve=gated, side=mods[0 if bi < 2 else 1], every=2)

    norm1 = stream_norm(core, X, H, S, lambda t: pr("norm1", t))

    q, k, b = view(0, HG_H, S), view(W8, HG_H, S), view(2 * W8, HG_H, S)
    v = view(3 * W8, ST, D)
    g = view(4 * W8, HG_H, S)
    dec = view(5 * W8, HG_H, S)
    qe, ke = view(6 * W8, HG_H, S), view(7 * W8, HG_H, S)

    def silu_to(dst):
        return lambda act, i, n, j, ps: nc.scalar.activation(dst[:, i, :], ps[:, 0:S], ACT.Silu)

    def copy_to(dst):
        return lambda act, i, n, j, ps: nc.scalar.activation(dst[:, i, :], ps[:, 0:S], ACT.Copy)

    def tm_to(dst):
        return lambda act, i, n, j, ps: nc.scalar.activation(dst[:, j, n * UNIT:(n + 1) * UNIT], ps[:, 0:UNIT], ACT.Copy)

    project(core, H, S, 4, on_act=silu_to(q), side=mods[0], every=2, norm=norm1)
    project(core, H, S, 4, on_act=copy_to(k), side=mods[0], every=2)
    project(core, H, S, 4, fm=False, on_act=tm_to(v), side=mods[0], every=2)
    project(core, H, S, 4, on_act=silu_to(g), side=mods[0], every=2)

    steps, mk_ready = sig("hg_gate_steps"), sig("level_masks_ready")
    lv, lv_in = view(8 * W8, 1, LEV_N // 4)[:, 0].bitcast(U8), core.norm_rt[:, 0:LEV_N]
    flat = lambda t: t.rearrange("p a b -> p (a b)")
    with core.phase() as block:

        @block.sync
        def _(sp):
            sp.dma_start(lv_in, a["levels"]).then_inc(*mk_ready.dma())

        @block.scalar
        def _(act):
            link = linker(act, sig("act_chain"))
            link(nc.scalar.activation(flat(dec), flat(k), ACT.Abs))
            link(nc.scalar.activation(flat(dec), flat(dec), ACT.Exp, scale=-1.0))
            nc.scalar.activation(flat(qe), flat(dec), ACT.Ln, bias=1.0).then_inc(*steps.one())
            act.wait_ge(*steps.at(2))
            nc.scalar.activation(flat(k), flat(k), ACT.Sigmoid, scale=-1.0)

        @block.vector
        def _(dve):
            link = linker(dve, sig("dve_chain"))
            nc.vector.memset(flat(ke), 1.0)
            dve.wait_ge(*mk_ready.at(16))
            nc.vector.tensor_copy(lv, lv_in)
            dve.wait_ge(*steps.at(1))
            link(nc.vector.scalar_tensor_tensor(flat(dec), flat(k), 0.0, flat(qe), ALU.min, ALU.subtract))
            dve.sem_inc(*steps.one())
            for h in range(HG_H):
                nc.vector.tensor_tensor_scan(b[:, h, :], ke[:, h, :], dec[:, h, :], 0.0, ALU.mult, ALU.add)

    attn, attn1 = spare, core.mod_sums[:, :, :, :].rearrange("p a b c -> p (a b c)").rearrange("p (h c) -> p h c", h=HG_H)
    diff, expd, qd, qd_last, kd, prod, put = (sig(n) for n in (
        "hg_diff_ready", "hg_decay_ready", "hg_q_ready", "hg_q_last_ready", "hg_k_ready", "hg_scores_ready",
        "hg_scores_read"))
    levels = [P] + LEVELS + [0]
    decs = (flat(dec), core.norm_rt[:, :])
    qes = (flat(qe), core.norm_sq[:, :, :].rearrange("p a b -> p (a b)"))
    NL = len(levels)
    with core.phase() as block:

        @block.vector
        def _(dve):
            link = linker(dve, sig("dve_chain"))
            nc.vector.memset(attn, 0.0)
            link(nc.vector.memset(attn1, 0.0))

            def take(n):
                L = levels[n]
                for h4 in range(4):
                    dve.wait_ge(*prod.at(4 * n + h4 + 1))
                    ps = psum[:, (4 * n + h4) % 8, :]
                    pair = attn[:, 2 * h4:2 * h4 + 2, :]
                    if L == P:
                        ins = nc.vector.tensor_copy(
                            pair[:, :, P:2 * P], ps[:, 0:2 * P].rearrange("p (h t) -> p h t", h=2))
                        link(ins)
                    else:
                        o = P * (levels.index(L) - 1)
                        m = lv[:, o:o + P].unsqueeze(1).broadcast_to([P, 2, P])
                        for t in range(2):
                            ins = nc.vector.copy_predicated(
                                (attn if t == 0 else attn1)[:, 2 * h4:2 * h4 + 2, 0:P], m, ps.rearrange("p (t h c) -> p t h c", t=2, h=2)[:, t])
                            link(ins)
                    dve.sem_inc(*put.one())

            def difference(n):
                L = levels[n]
                if n >= 2:
                    dve.wait_ge(*kd.at(4 * (n - 1)))
                    dve.wait_ge(*qd.at(3 * (n - 1)))
                nb = W8 // (2 * L)
                bv = flat(b).rearrange("p (n e l) -> p n e l", e=2, l=L)
                dv = decs[n % 2].rearrange("p (n e l) -> p n e l", e=2, l=L)
                r = bv[:, :, 0, L - 1:L].broadcast_to([P, nb, L])
                nc.vector.tensor_tensor(dv[:, :, 1, :], bv[:, :, 1, :], r, ALU.subtract)
                link(nc.vector.tensor_tensor(dv[:, :, 0, :], r, bv[:, :, 0, :], ALU.subtract))
                dve.sem_inc(*diff.one())

            difference(0)
            for n in range(NL - 1):
                if n + 1 < NL - 1:
                    difference(n + 1)
                dve.wait_ge(*expd.at(n + 1))
                if n >= 2:
                    dve.wait_ge(*prod.at(4 * (n - 1)))
                for h4 in range(3):
                    w = slice(2 * h4 * S, 2 * (h4 + 1) * S)
                    nc.vector.tensor_tensor(qes[n % 2][:, w], flat(q)[:, w], decs[n % 2][:, w], ALU.mult)\
                        .then_inc(*qd.one())
                if n:
                    take(n - 1)
            take(NL - 2)
            take(NL - 1)

        @block.scalar
        def _(act):
            for n in range(NL - 1):
                act.wait_ge(*diff.at(n + 1))
                nc.scalar.activation(decs[n % 2], decs[n % 2], ACT.Exp).then_inc(*expd.one())

        @block.gpsimd
        def _(pool):
            for n in range(NL - 1):
                pool.wait_ge(*expd.at(n + 1))
                w = slice(6 * S, 8 * S)
                if n >= 2:
                    pool.wait_ge(*prod.at(4 * (n - 1)))
                nc.gpsimd.tensor_tensor(qes[n % 2][:, w], flat(q)[:, w], decs[n % 2][:, w], ALU.mult)\
                    .then_inc(*qd_last.one())
                for h4 in range(4):
                    w = slice(2 * h4 * S, 2 * (h4 + 1) * S)
                    if n:
                        pool.wait_ge(*prod.at(4 * (n - 1) + h4 + 1))
                    nc.gpsimd.tensor_tensor(flat(ke)[:, w], flat(k)[:, w], decs[n % 2][:, w], ALU.mult)\
                        .then_inc(*kd.one())

        @block.tensor
        def _(pe):
            for n, L in enumerate(levels):
                ko = ke if L else k
                qo = qes[n % 2].rearrange("p (h t) -> p h t", h=HG_H) if L else q
                for h4 in range(4):
                    i = 4 * n + h4
                    if L:
                        if h4 < 3:
                            pe.wait_ge(*qd.at(3 * n + h4 + 1))
                        else:
                            pe.wait_ge(*qd_last.at(n + 1))
                        pe.wait_ge(*kd.at(4 * n + h4 + 1))
                    if i >= 8:
                        pe.wait_ge(*put.at(i - 7))
                    for t in range(1 if L == P else 2):
                        for e in range(2):
                            h = 2 * h4 + e
                            o = psum[:, i % 8, (2 * t + e) * P:(2 * t + e + 1) * P]
                            ks = ko[:, h, t * P:(t + 1) * P]
                            qs = qo[:, h, P:2 * P] if L == P else qo[:, h, t * P:(t + 1) * P]
                            mm = nc.tensor.matmul(o, ks, qs, start=True, stop=True)
                    mm.then_inc(*prod.one())

    o = dec
    oacc = sig("hg_out_ready")
    with core.phase() as block:

        @block.tensor
        def _(pe):
            for h in range(HG_H):
                ps = psum[:, h, 0:S]
                nc.tensor.matmul(ps[:, P:S], v[:, 1, h * P:(h + 1) * P], attn1[:, h, :], start=True, stop=False,
                                 skip_group_check=True)
                nc.tensor.matmul(ps, v[:, 0, h * P:(h + 1) * P], attn[:, h, :], start=False, stop=True,
                                 skip_group_check=True).then_inc(*oacc.one())

        @block.scalar
        def _(act):
            for h in range(HG_H):
                act.wait_ge(*oacc.at(h + 1))
                nc.scalar.activation(o[:, h, :], psum[:, h, 0:S], ACT.Copy)

    merge(0, Norm(core, lambda t: o[:, t, :], HG_H, 1, S, lambda t: pr("hg_norm"), lambda t: o[:, t, :],
                  gate=lambda t: g[:, t, :], parts=Yt))

    mq = view(2 * W8, 2 * ML_H, S)
    vml = view(3 * W8, ST, D)
    go = view(4 * W8, DT, S)
    tmp = core.norm_rt[:, 0:2 * S].rearrange("p (a b) -> p a b", a=2)

    def conv4(w, bias, tmpb):
        def f(dve, link, i, ps):
            t = tmpb[:, i % 2, :]
            link(nc.vector.tensor_scalar(t, ps[:, 0:S], w(3, i), bias(i), ALU.mult, ALU.add))
            for d in (1, 2, 3):
                ins = nc.vector.scalar_tensor_tensor(t[:, d:S], ps[:, 0:S - d], w(3 - d, i), t[:, d:S],
                                                     ALU.mult, ALU.add)
                if d < 3:
                    link(ins)
            return ins
        return f

    project(core, H, S, 4, on_dve=conv4(lambda kk, i: pr("ml_w", kk * DT + i), lambda i: pr("ml_b", i), tmp),
            then_act=lambda act, i: nc.scalar.activation(mq[:, i, :], tmp[:, i % 2, :], ACT.Silu))
    project(core, H, S, 4, fm=False, on_act=tm_to(vml), side=mods[0], every=2)
    project(core, H, S, 4,
            on_act=lambda act, i, n, j, ps: nc.scalar.activation(go[:, i, :], ps[:, 0:S], ACT.Sigmoid), side=mods[0], every=2)

    WK = 5 * W8
    gt = view(WK, 12, S)
    gs = sig("gates_steps")
    wg = pv("w_gates", DT)
    with core.phase() as block:

        @block.tensor
        def _(pe):
            for kk in range(DT):
                for half in range(2):
                    mm = nc.tensor.matmul(psum[0:80, 0, 0:S], wg[:, kk, :], H[half][:, kk, 0:S].bitcast(F32),
                                          start=(kk == 0 and half == 0), stop=(kk == DT - 1 and half == 1))
            mm.then_inc(*gs.one())

        @block.scalar
        def _(act):
            link = linker(act, sig("act_chain"))
            act.wait_ge(*gs.at(1))
            link(nc.scalar.activation(gt[0:4, 0, :], psum[0:4, 0, 0:S], ACT.Identity, bias=pr("gate_i")[0:4]))
            link(nc.scalar.activation(gt[0:4, 1, :], psum[32:36, 0, 0:S], ACT.Identity, bias=pr("gate_f")[0:4]))
            link(nc.scalar.activation(gt[0:16, 2, :], psum[64:80, 0, 0:S], ACT.Identity, bias=pr("dt_bias")[0:16]))
            link(nc.scalar.activation(gt[0:4, 3, :], gt[0:4, 1, :], ACT.Abs))
            link(nc.scalar.activation(gt[0:16, 4, :], gt[0:16, 2, :], ACT.Abs))
            link(nc.scalar.activation(gt[0:4, 3, :], gt[0:4, 3, :], ACT.Exp, scale=-1.0))
            link(nc.scalar.activation(gt[0:16, 4, :], gt[0:16, 4, :], ACT.Exp, scale=-1.0))
            link(nc.scalar.activation(small[0:16, 0:1], pr("a_log")[0:16], ACT.Exp))
            link(nc.scalar.activation(gt[0:4, 3, :], gt[0:4, 3, :], ACT.Ln, bias=1.0))
            link(nc.scalar.activation(gt[0:16, 4, :], gt[0:16, 4, :], ACT.Ln, bias=1.0))
            act.sem_inc(*gs.one())

        @block.vector
        def _(dve):
            link = linker(dve, sig("dve_chain"))
            link(nc.vector.memset(gt[0:16, 5, :], 1.0))
            dve.wait_ge(*gs.at(2))
            link(nc.vector.scalar_tensor_tensor(gt[0:4, 1, :], gt[0:4, 1, :], 0.0, gt[0:4, 3, :], ALU.min, ALU.subtract))
            link(nc.vector.tensor_tensor_scan(gt[0:4, 6, :], gt[0:4, 5, :], gt[0:4, 1, :], 0.0, ALU.mult, ALU.add))
            link(nc.vector.tensor_tensor(gt[0:4, 7, :], gt[0:4, 0, :], gt[0:4, 6, :], ALU.subtract))
            link(nc.vector.tensor_tensor_scan(gt[0:4, 8, :], gt[0:4, 7, :], gt[0:4, 7, :], 0.0, ALU.max, ALU.max))
            link(nc.vector.tensor_tensor(gt[0:4, 9, :], gt[0:4, 6, :], gt[0:4, 8, :], ALU.add))
            link(nc.vector.scalar_tensor_tensor(gt[0:16, 2, :], gt[0:16, 2, :], 0.0, gt[0:16, 4, :], ALU.max, ALU.add))
            link(nc.vector.tensor_scalar(gt[0:16, 10, :], gt[0:16, 2, :], small[0:16, 0:1], -1.0, ALU.mult, ALU.mult))
            nc.vector.tensor_tensor_scan(gt[0:16, 11, :], gt[0:16, 5, :], gt[0:16, 10, :], 0.0, ALU.mult, ALU.add)

    cols = core.gate_columns
    cs = sig("columns_ready")
    with core.phase() as block:

        @block.tensor
        def _(pe):
            for t in range(ST):
                for i, (r, n) in enumerate(((7, 4), (11, 16), (2, 16))):
                    mm = nc.tensor.transpose(psum[:, 3 * t + i, 0:n], gt[0:n, r, t * P:(t + 1) * P], ident[0:n, 0:n])
                    mm.then_inc(*cs.one())

        @block.vector
        def _(dve):
            dve.wait_ge(*cs.at(6))
            for t in range(ST):
                nc.vector.tensor_copy(cols[:, t, 0, 0:4], psum[:, 3 * t, 0:4])
                nc.vector.tensor_scalar(cols[:, t, 1, :], psum[:, 3 * t + 1, 0:16], -1.0, None, ALU.mult)
                nc.vector.tensor_copy(cols[:, t, 2, :], psum[:, 3 * t + 2, 0:16])

    arg = view(WK + 12 * S, 2, 3 * P)
    wts = view(WK + 12 * S + 6 * P, 2, 3 * P)
    num = spare

    def pick(h, n):
        return ident[0:n, h:h + 1].broadcast_to([n, P])

    big = [sig(n) for n in ("ml_scores_ready", "ml_arg_ready", "ml_exp_ready", "ml_weights_ready", "ml_sums_ready",
                            "ml_abs_ready", "ml_head_done")]
    sc, ag, ex, wt, sm, ab, hd = big
    scale = float(P) ** -0.5
    with core.phase() as block:

        @block.tensor
        def _(pe):
            def scores(h):
                if h >= 2:
                    pe.wait_ge(*wt.at(h - 1))
                b0 = 2 * (h % 2)
                nc.tensor.matmul(psum[:, b0, 0:S], mq[:, ML_H + h, 0:P], mq[:, h, :], start=True, stop=True)
                nc.tensor.matmul(psum[:, b0, S:3 * P], mq[:, ML_H + h, P:S], mq[:, h, P:S], start=True, stop=True,
                                 skip_group_check=True)
                nc.tensor.matmul(psum[:, b0 + 1, 0:S], pick(h, 4), gt[0:4, 8, :], start=True, stop=True)\
                    .then_inc(*sc.one())

            scores(0)
            for h in range(ML_H):
                if h + 1 < ML_H:
                    scores(h + 1)
                pe.wait_ge(*wt.at(h + 1))
                if h >= 1:
                    pe.wait_ge(*hd.at(h))
                w = wts[:, h % 2, :]
                for j in range(3):
                    v0 = vml[:, 0, h * 256 + j * P:h * 256 + (j + 1) * P] if j < 2 else core.ones[:, :]
                    v1 = vml[:, 1, h * 256 + j * P:h * 256 + (j + 1) * P] if j < 2 else core.ones[:, :]
                    nc.tensor.matmul(psum[:, 4 + j, P:S], v1, w[:, S:3 * P], start=True, stop=False,
                                     skip_group_check=True)
                    nc.tensor.matmul(psum[:, 4 + j, 0:S], v0, w[:, 0:S], start=False, stop=True,
                                     skip_group_check=True)
                nc.tensor.matmul(psum[:, 7, 0:S], pick(h, 4), gt[0:4, 9, :], start=True, stop=True)\
                    .then_inc(*sm.one())

        @block.scalar
        def _(act):
            link = linker(act, sig("act_chain"))

            def bounds(h):
                act.wait_ge(*sm.at(h + 1))
                if h:
                    act.wait_ge(*hd.at(h))
                nc.scalar.activation(core.norm_rt[:, 0:S], psum[:, 6, 0:S], ACT.Abs)
                link(nc.scalar.activation(core.norm_rt[:, S:2 * S], psum[:, 7, 0:S], ACT.Exp, scale=-1.0))
                act.sem_inc(*ab.one())

            for h in range(ML_H):
                act.wait_ge(*ag.at(h + 1))
                nc.scalar.activation(arg[:, h % 2, :], arg[:, h % 2, :], ACT.Exp).then_inc(*ex.one())
                if h:
                    bounds(h - 1)
            bounds(ML_H - 1)

        @block.vector
        def _(dve):
            link = linker(dve, sig("dve_chain"))

            def exponents(h):
                dve.wait_ge(*sc.at(h + 1))
                ar = arg[:, h % 2, :]
                mt = psum[:, 2 * (h % 2) + 1, 0:S]
                nc.vector.tensor_scalar(ar[:, 0:S], mt, -1.0, cols[:, 0, 0, h:h + 1], ALU.mult, ALU.add)
                link(nc.vector.tensor_scalar(ar[:, S:3 * P], mt[:, P:S], -1.0, cols[:, 1, 0, h:h + 1], ALU.mult, ALU.add))
                link(nc.vector.tensor_scalar(ar[:, :], ar[:, :], 0.0, None, ALU.min))
                dve.sem_inc(*ag.one())

            def weights(h):
                dve.wait_ge(*ex.at(h + 1))
                ar = arg[:, h % 2, :]
                dg = ar.rearrange("p (b c) -> p b c", b=3)[:, 0:3:2, :]
                link(nc.vector.tensor_tensor(dg, dg, causal.unsqueeze(1).broadcast_to([P, 2, P]), ALU.mult))
                if h >= 2:
                    dve.wait_ge(*sm.at(h - 1))
                link(nc.vector.scalar_tensor_tensor(wts[:, h % 2, :], psum[:, 2 * (h % 2), 0:3 * P], scale, ar,
                                                    ALU.mult, ALU.mult))
                dve.sem_inc(*wt.one())

            def divide(h):
                dve.wait_ge(*ab.at(h + 1))
                rt = core.norm_rt
                link(nc.vector.tensor_tensor(rt[:, 2 * S:3 * S], rt[:, 0:S], rt[:, S:2 * S], ALU.max))
                link(nc.vector.reciprocal(rt[:, 2 * S:3 * S], rt[:, 2 * S:3 * S]))
                for j in range(2):
                    ins = nc.vector.tensor_tensor(num[:, 2 * h + j, :], psum[:, 4 + j, 0:S], rt[:, 2 * S:3 * S], ALU.mult)
                link(ins)
                dve.sem_inc(*hd.one())

            exponents(0)
            for h in range(ML_H):
                if h + 1 < ML_H:
                    exponents(h + 1)
                weights(h)
                if h:
                    divide(h - 1)
            divide(ML_H - 1)

    merge(1, Norm(core, lambda t: num[:, t, :], DT, 2, S, lambda t: pr("ml_norm", t % 2), lambda t: num[:, t, :],
            gate=lambda t: go[:, t, :], parts=Yt))

    z = view(2 * W8, DT, S)
    xbc = view(3 * W8, 2 * DT, S)
    XS, BM, CM = 0, DT, DT + MB_G
    tmp2 = core.norm_rt[:, 0:2 * S].rearrange("p (a b) -> p a b", a=2)
    project(core, H, S, 4, on_act=silu_to(z), side=mods[0], every=2)
    project(core, H, S, 8, on_dve=conv4(lambda kk, i: pr("mb_w", kk * 16 + i), lambda i: pr("mb_b", i), tmp2),
            then_act=lambda act, i: nc.scalar.activation(xbc[:, i, :], tmp2[:, i % 2, :], ACT.Silu))

    cbs = view(WK + 12 * S + 12 * P, MB_G, 3 * P)
    tr, trr, cb, cbr = sig("mb_x_turned"), sig("mb_x_read"), sig("mb_cb_ready"), sig("mb_cb_read")
    halves = (spare, gate)

    def xh(t, h):
        return halves[t][:, h // 2, (h % 2) * P:(h % 2 + 1) * P]

    with core.phase() as block:

        @block.tensor
        def _(pe):
            for i in range(2 * DT):
                t, j = i // DT, i % DT
                if i >= 4:
                    pe.wait_ge(*trr.at(i - 3))
                nc.tensor.transpose(psum[:, i % 4, 0:P], xbc[:, XS + j, t * P:(t + 1) * P], ident).then_inc(*tr.one())
            for gq in range(MB_G):
                ps = psum[:, 4 + gq, :]
                nc.tensor.matmul(ps[:, 0:S], xbc[:, BM + gq, 0:P], xbc[:, CM + gq, :], start=True, stop=True)
                nc.tensor.matmul(ps[:, S:3 * P], xbc[:, BM + gq, P:S], xbc[:, CM + gq, P:S], start=True, stop=True,
                                 skip_group_check=True).then_inc(*cb.one())

        @block.scalar
        def _(act):
            for gq in range(MB_G):
                act.wait_ge(*cb.at(gq + 1))
                nc.scalar.activation(cbs[:, gq, :], psum[:, 4 + gq, 0:3 * P], ACT.Copy)

        @block.vector
        def _(dve):
            link = linker(dve, sig("dve_chain"))
            for t in range(ST):
                link(nc.vector.memset(halves[t], 0.0))
            for i in range(2 * DT):
                t, j = i // DT, i % DT
                dve.wait_ge(*tr.at(i + 1))
                for e in range(2):
                    ins = nc.vector.tensor_scalar(xh(t, 2 * j + e)[:, e * 64:(e + 1) * 64], psum[:, i % 4, e * 64:(e + 1) * 64],
                                                  cols[:, t, 2, 2 * j + e:2 * j + e + 1], None, ALU.mult)
                link(ins)
                dve.sem_inc(*trr.one())

    yz, ytmp = z, core.norm_rt[:, 0:S]
    bc, ag2, ex2, wt2, ou, our = (sig(n) for n in ("mb_cum_ready", "mb_arg_ready", "mb_exp_ready", "mb_weights_ready",
                                                   "mb_pair_ready", "mb_pair_read"))
    with core.phase() as block:

        @block.tensor
        def _(pe):
            def cum(h):
                if h >= 4:
                    pe.wait_ge(*ag2.at(h - 3))
                nc.tensor.matmul(psum[:, h % 4, 0:S], pick(h, 16), gt[0:16, 11, :], start=True, stop=True)\
                    .then_inc(*bc.one())

            cum(0)
            cum(1)
            for h in range(MB_H):
                if h + 2 < MB_H:
                    cum(h + 2)
                pe.wait_ge(*wt2.at(h + 1))
                j, e = h // 2, h % 2
                if e == 0 and j >= 2:
                    pe.wait_ge(*our.at(j - 1))
                ps = psum[:, 4 + j % 2, 0:S]
                w = wts[:, h % 2, :]
                if e == 0:
                    nc.tensor.matmul(ps, xh(0, h), w[:, 0:S], start=True, stop=False, skip_group_check=True)
                mm = nc.tensor.matmul(ps[:, P:S], xh(1, h), w[:, S:3 * P], start=False, stop=False, skip_group_check=True)
                if e == 1:
                    mm = nc.tensor.matmul(ps, xh(0, h), w[:, 0:S], start=False, stop=True, skip_group_check=True)
                mm.then_inc(*ou.one())

        @block.scalar
        def _(act):
            for h in range(MB_H):
                act.wait_ge(*ag2.at(h + 1))
                nc.scalar.activation(arg[:, h % 2, :], arg[:, h % 2, :], ACT.Exp).then_inc(*ex2.one())

        @block.vector
        def _(dve):
            link = linker(dve, sig("dve_chain"))

            def exponents(h):
                dve.wait_ge(*bc.at(h + 1))
                ar, ps = arg[:, h % 2, :], psum[:, h % 4, 0:S]
                nc.vector.tensor_scalar(ar[:, 0:S], ps, cols[:, 0, 1, h:h + 1], 0.0, ALU.add, ALU.min)
                link(nc.vector.tensor_scalar(ar[:, S:3 * P], ps[:, P:S], cols[:, 1, 1, h:h + 1], 0.0, ALU.add, ALU.min))
                dve.sem_inc(*ag2.one())

            def pair(j):
                dve.wait_ge(*ou.at(2 * j + 2))
                link(nc.vector.scalar_tensor_tensor(ytmp, xbc[:, XS + j, :], pr("mb_d", j), psum[:, 4 + j % 2, 0:S],
                                                    ALU.mult, ALU.add))
                dve.sem_inc(*our.one())
                link(nc.vector.tensor_tensor(yz[:, j, :], ytmp, z[:, j, :], ALU.mult))

            exponents(0)
            for h in range(MB_H):
                if h + 1 < MB_H:
                    exponents(h + 1)
                dve.wait_ge(*ex2.at(h + 1))
                ar = arg[:, h % 2, :]
                dg = ar.rearrange("p (b c) -> p b c", b=3)[:, 0:3:2, :]
                link(nc.vector.tensor_tensor(dg, dg, causal.unsqueeze(1).broadcast_to([P, 2, P]), ALU.mult))
                if h >= 2:
                    dve.wait_ge(*ou.at(h - 1))
                link(nc.vector.tensor_tensor(wts[:, h % 2, :], cbs[:, h // 4, :], ar, ALU.mult))
                dve.sem_inc(*wt2.one())
                if h >= 3 and h % 2 == 1:
                    pair(h // 2 - 1)
            pair(MB_H // 2 - 1)

    merge(2, Norm(core, lambda t: yz[:, t, :], DT, 2, S, lambda t: pr("mb_norm", t), lambda t: yz[:, t, :], parts=Yt))

    split_fm(core, mixed, Y)
    project(core, Y, S, 4,
            on_dve=lambda dve, link, i, ps: nc.vector.tensor_tensor(X[:, i, 0:S], ps[:, 0:S], X[:, i, 0:S], ALU.add),
            side=mods[1], every=2)


def stream_norm(core, X, H, T, gain, shift=None):
    at = lambda v, t: v[:, t % DT, (t // DT) * S:(t // DT + 1) * S]
    per = lambda f: (lambda t: f(t % DT, t // DT)) if T > S or shift else f
    return Norm(core, lambda t: at(X, t), DT * T // S, DT, S, per(gain), lambda t: core.norm_sq[:, t % 4, S:2 * S],
                shift=per(shift) if shift else None, parts=tuple(lambda t, p=p: at(p, t) for p in H))


def feed_forward(core, tag, norm, X, H, T, cw, cb, lead, residual, side=None):
    nc = core.nc
    seg = T // S
    n = FFT if seg == 1 else FFH
    low = "pool" if seg == 1 else "dve"
    with (nc.sbuf_tensor(f"u_high{tag}", [P, n, T], F32R) as uh, nc.sbuf_tensor(f"u_low{tag}", [P, n, T], F32R) as ul,
          nc.sbuf_tensor(f"u_filtered{tag}", [P, 4, T], F32) as tmp):

        def conv3(link, ch, o, ps):
            t = o.rearrange("p (s t) -> p s t", s=seg)
            pp = ps[:, 0:T].rearrange("p (s t) -> p s t", s=seg)
            link(nc.vector.tensor_scalar(o, ps[:, 0:T], cw(lead, ch), cb(ch), ALU.mult, ALU.add))
            for k in [k for k in range(3) if k != lead]:
                d = lead - k
                a, b = (t[:, :, d:S], pp[:, :, 0:S - d]) if d > 0 else (t[:, :, 0:S + d], pp[:, :, -d:S])
                link(nc.vector.scalar_tensor_tensor(a, b, cw(k, ch), a, ALU.mult, ALU.add))

        for first in range(0, FFT, n):
            up(core, H, T, first, n, conv3, tmp, uh, ul, low, None if first else norm)
            project(core, (uh, ul), T, 2 * DT * n // FFT, halves="both" if seg == 1 else "one", on_dve=residual, side=side)


def up(core, H, T, first, n_units, conv3, tmp, uh, ul, low, norm):
    nc = core.nc
    acc, free = core.sig("up_acc_ready"), core.sig("up_bank_free")
    filt, sil, prod, hi = (core.sig(n) for n in ("up_filtered", "up_silu_ready", "up_product_ready", "up_high_ready"))
    g0 = core.taken
    core.taken += n_units
    with core.phase() as block:

        @block.sync
        def _(sp):
            core.release(sp, g0 + n_units)

        @block.tensor
        def _(pe):
            if norm:
                norm.sums(pe)
            for n in range(n_units):
                w = core.parts(g0 + n, DT, UNIT)
                for j in range(2):
                    i = 2 * n + j
                    if i >= 8:
                        pe.wait_ge(*free.at(i - 7))
                    for k in range(DT):
                        if j == 0:
                            core.wait_parts(pe, g0 + n, k, DT)
                        if norm and n == 0 and j == 0:
                            pe.wait_ge(*norm.low.at(norm.ntile - DT + k + 1))
                        mm = product(nc, core.psum[:, i % 8, 0:T], [p[:, k, j * P:(j + 1) * P] for p in w],
                                     [p[:, k, 0:T] for p in H], k == 0, k == DT - 1)
                    mm.then_inc(*acc.one())

        @block.vector
        def _(dve):
            link = linker(dve, core.sig("dve_chain"))

            def low_part(n):
                dve.wait_ge(*hi.at(n + 1))
                link(nc.vector.tensor_tensor(ul[:, n, :], tmp[:, 2 * (n % 2), :], uh[:, n, :].bitcast(F32), ALU.subtract))

            def multiply(n):
                dve.wait_ge(*sil.at(n + 1))
                g = tmp[:, 2 * (n % 2), :]
                link(nc.vector.tensor_tensor(g, g, tmp[:, 2 * (n % 2) + 1, :], ALU.mult))
                dve.sem_inc(*prod.one())

            if norm:
                norm.values(dve, link, range(norm.ntile))
            for n in range(n_units):
                if n:
                    multiply(n - 1)
                if low == "dve":
                    core.split_low(dve, g0 + n + 1)
                if n:
                    low_part(n - 1)
                for j in range(2):
                    i = 2 * n + j
                    dve.wait_ge(*acc.at(i + 1))
                    conv3(link, first + n + FFT * j, tmp[:, 2 * (n % 2) + j, :], core.psum[:, i % 8, :])
                    dve.sem_inc(*free.one())
                    if j == 0:
                        dve.sem_inc(*filt.one())
            multiply(n_units - 1)
            low_part(n_units - 1)

        @block.scalar
        def _(act):
            def high_part(n):
                act.wait_ge(*prod.at(n + 1))
                nc.scalar.activation(uh[:, n, :], tmp[:, 2 * (n % 2), :], ACT.Copy).then_inc(*hi.one())

            if norm:
                norm.roots(act)
                norm.highs(act, range(norm.ntile))
            for n in range(n_units):
                if n:
                    act.wait_ge(*acc.at(2 * n))
                core.split_high(act, g0 + n + 1)
                if n:
                    high_part(n - 1)
                act.wait_ge(*filt.at(n + 1))
                g = tmp[:, 2 * (n % 2), :]
                nc.scalar.activation(g, g, ACT.Silu).then_inc(*sil.one())
            high_part(n_units - 1)

        @block.gpsimd
        def _(pool):
            if norm:
                norm.lows(pool, range(norm.ntile))
            for n in range(n_units if low == "pool" else 0):
                core.split_low(pool, g0 + n + 1)


def load_context(core, a, X):
    ctx_ready = core.sig("context_ready")
    with core.phase() as block:

        @block.sync
        def _(sp):
            sp.dma_start(X[:, :, S:2 * S], a["ctx"].rearrange("(k p) t -> p k t", p=P)).then_inc(*ctx_ready.dma())
            sp.wait_ge(*ctx_ready.at(16))


def attention_layer(core, a, i, X, H, pr, pv, cn, view, arena, ident, small, adaM, side):
    nc, sig, psum = core.nc, core.sig, core.psum
    last = i == LAYERS - 1
    lam_init = 0.8 - 0.6 * float(np.exp(-0.3 * i))
    if i == 0:
        norm_fm(core, lambda t: X[:, t, 0:S], DT, DT, S, lambda t: pr("final", t), lambda t: X[:, t, 0:S])

    gains = core.mod_gains
    with core.phase() as block:

        @block.vector
        def _(dve):
            link = linker(dve, sig("dve_chain"))
            for half, (name, part) in enumerate(((f"norm1_{i}", 1), (f"norm2_{i}", 4))):
                gcol = pv(name, DT).broadcast_to([P, DT, 2])
                sc_ = adaM[:, part * DT:(part + 1) * DT, :]
                link(nc.vector.tensor_scalar(gains[:, half], sc_, 1.0, None, ALU.add))
                link(nc.vector.tensor_tensor(gains[:, half], gains[:, half], gcol, ALU.mult))

    def modulated(half, T):
        return stream_norm(core, X, H, T, lambda t, s_: gains[:, half, t, s_:s_ + 1],
                      lambda t, s_: adaM[:, 3 * half * DT + t, s_:s_ + 1])

    with arena(f"arena_attention{i}"):
        z = view(0, 4, 2048)
        NT = 4

        def toks(n):
            return range(NT if not last or n in (4, 6, 7) else ST)

        def zout(act, i_, n, j, ps):
            if n in (2, 3):
                dst = z[:, j, 512:1024].rearrange("p (h g c) -> p g h c", g=2, h=4)[:, n - 2]
                return nc.scalar.activation(dst, ps[:, 0:UNIT].rearrange("p (h c) -> p h c", h=4), ACT.Copy)
            return nc.scalar.activation(z[:, j, n * UNIT:(n + 1) * UNIT], ps[:, 0:UNIT], ACT.Gelu_apprx_tanh if n < 2 else ACT.Copy)

        project(core, H, 2 * S, 8, fm=False, on_act=zout, tok_tiles=toks, low="dve",
                norm=modulated(0, 2 * S))

        TT = view(4 * 2048, 16, 512)
        ws_t, ws_in = view(4 * 2048 + 16 * 512, 1, 512)[:, 0], sig("spatial_weights_ready")
        sqs = (core.norm_rt[:, 0:1408], view(4 * 2048, 1, 1408)[:, 0])
        rss = (small[:, 0:30], small[:, 32:62])
        r2 = core.norm_sq[:, :, :].rearrange("p a b -> p (a b)")
        lam_s, sq_r, ss_r, rt_r = (sig(n) for n in ("lambda_steps", "qk_squares_ready", "qk_sums_ready", "qk_roots_ready"))
        lamc = core.lam
        with core.phase() as block:

            @block.sync
            def _(sp):
                sp.dma_start(ws_t, a["a_ws"][i]).then_inc(*ws_in.dma())
                sp.wait_ge(*ws_in.at(16))

            @block.gpsimd
            def _(pool):
                nc.gpsimd.memset(TT[:, 4:6, :], 0.0)
                nc.gpsimd.memset(TT[:, 8:16, :], 0.0)

            @block.scalar
            def _(act):
                link = linker(act, sig("act_chain"))
                act.wait_ge(*lam_s.at(1))
                nc.scalar.activation(lamc[:, 0:2], lamc[:, 0:2], ACT.Exp).then_inc(*lam_s.one())

                def squares(t):
                    sq = sqs[t % 2]
                    if t >= 2:
                        act.wait_ge(*ss_r.at(t - 1))
                    if last and t >= 2:
                        nc.scalar.activation(sq[:, 768:896], z[:, t, 1024:1152], ACT.Square)
                        link(nc.scalar.activation(sq[:, 1152:1408], z[:, t, 1536:1792], ACT.Square))
                    else:
                        nc.scalar.activation(sq[:, 0:896], z[:, t, 256:1152], ACT.Square)
                        link(nc.scalar.activation(sq[:, 896:1408], z[:, t, 1280:1792], ACT.Square))
                    act.sem_inc(*sq_r.one())

                squares(0)
                for t in range(NT):
                    if t + 1 < NT:
                        squares(t + 1)
                    act.wait_ge(*ss_r.at(t + 1))
                    rs = rss[t % 2]
                    lo = 12 if (last and t >= 2) else 0
                    nc.scalar.activation(rs[:, lo:14], rs[:, lo:14], ACT.Sqrt, scale=1.0 / 64, bias=core.eps[:, 0:1])
                    lo = 22 if (last and t >= 2) else 14
                    link(nc.scalar.activation(rs[:, lo:30], rs[:, lo:30], ACT.Sqrt, scale=1.0 / 32, bias=core.eps[:, 0:1]))
                    act.sem_inc(*rt_r.one())

            @block.vector
            def _(dve):
                link = linker(dve, sig("dve_chain"))
                lp = pv(f"lam{i}", 4)
                for m in range(2):
                    link(nc.vector.tensor_tensor(r2[:, 0:32], lp[:, 2 * m, :], lp[:, 2 * m + 1, :], ALU.mult))
                    link(nc.vector.tensor_reduce(lamc[:, m:m + 1], r2[:, 0:32], AX.X, ALU.add))
                dve.sem_inc(*lam_s.one())
                dve.wait_ge(*lam_s.at(2))
                link(nc.vector.tensor_tensor(lamc[:, 2:3], lamc[:, 1:2], lamc[:, 0:1], ALU.subtract))
                link(nc.vector.tensor_scalar(lamc[:, 2:3], lamc[:, 2:3], -lam_init, None, ALU.add))

                def short(t):
                    return last and t >= 2

                def sums(t):
                    rs, sq = rss[t % 2], sqs[t % 2]
                    b0, c0 = (12, 8) if short(t) else (0, 0)
                    dve.wait_ge(*sq_r.at(t + 1))
                    nc.vector.tensor_reduce(rs[:, b0:14], sq[:, b0 * 64:896].rearrange("p (g c) -> p g c", c=64), AX.X, ALU.add)
                    link(nc.vector.tensor_reduce(rs[:, 14 + c0:30], sq[:, 896 + c0 * 32:1408].rearrange("p (g c) -> p g c", c=32),
                                                 AX.X, ALU.add))
                    dve.sem_inc(*ss_r.one())

                def scaled(t):
                    rs = rss[t % 2]
                    b0, c0 = (12, 8) if short(t) else (0, 0)
                    dve.wait_ge(*rt_r.at(t + 1))
                    nc.vector.reciprocal(rs[:, b0:14], rs[:, b0:14])
                    link(nc.vector.reciprocal(rs[:, 14 + c0:30], rs[:, 14 + c0:30]))
                    zb = z[:, t, 256 + b0 * 64:1152].rearrange("p (g c) -> p g c", c=64)
                    zc = z[:, t, 1280 + c0 * 32:1792].rearrange("p (g c) -> p g c", c=32)
                    nc.vector.tensor_tensor(zb, zb, rs[:, b0:14].unsqueeze(2).broadcast_to([P, 14 - b0, 64]), ALU.mult)
                    link(nc.vector.tensor_tensor(zc, zc, rs[:, 14 + c0:30].unsqueeze(2).broadcast_to([P, 16 - c0, 32]), ALU.mult))
                    for o, n, w, gname, go in ((512, 8, 64, "gain_b", 0), (1280, 8, 32, "gain_c", 0),
                                               (1024, 2, 64, "gain_b", 64), (1536, 8, 32, "gain_c", 32)):
                        if not short(t) or o in (1024, 1536):
                            zg = z[:, t, o:o + n * w].rearrange("p (n w) -> p n w", n=n)
                            gv = pr(f"{gname}{i}", go, w).unsqueeze(1).broadcast_to([P, n, w])
                            ins = nc.vector.tensor_tensor(zg, zg, gv, ALU.mult)
                    link(ins)

                def rotate(t):
                    for o, n, w, cname, sname, b in ((512, 10, 64, "cos_b", "sin_b", 0), (1280, 16, 32, "cos_c", "sin_c", 1024)):
                        f = w // 4
                        zz = z[:, t, o:o + n * w]
                        cosv = cn(cname, t * w, w).unsqueeze(1).broadcast_to([P, n, w])
                        sinv = cn(sname, t * w, w).rearrange("p (x e f) -> p x e f", x=2, e=2)
                        m1, m2 = r2[:, 0:n * w], r2[:, 640:640 + n * w]
                        z5 = zz.rearrange("p (n x e f) -> p n x e f", n=n, x=2, e=2)
                        m5 = m2.rearrange("p (n x e f) -> p n x e f", n=n, x=2, e=2)
                        nc.vector.tensor_tensor(m1.rearrange("p (n w) -> p n w", n=n), zz.rearrange("p (n w) -> p n w", n=n), cosv, ALU.mult)
                        for e in range(2):
                            ins = nc.vector.tensor_tensor(m5[:, :, :, e, :], z5[:, :, :, 1 - e, :],
                                                          sinv[:, :, e, :].unsqueeze(1).broadcast_to([P, n, 2, f]), ALU.mult)
                        link(ins)
                        link(nc.vector.tensor_tensor(zz, m1, m2, ALU.add))

                sums(0)
                for t in range(NT):
                    if t + 1 < NT:
                        sums(t + 1)
                    scaled(t)
                    if t < 2:
                        rotate(t)

        turns = [(512 + j * P, j) for j in range(4)] + [(1280, 6), (1408, 7)] + [(1024, None), (1536, None), (1664, None)]
        tu, tur = sig("turned"), sig("turned_read")
        cat_at = [0, P] + [512 + P * n for n in range(4)] + [1280, 1280 + P]
        NQ = 2 if last else 4
        wsT = ws_t.rearrange("p (g q) -> p g q", g=4)
        gm = sig("gmlp_ready")
        with core.phase() as block:

            @block.tensor
            def _(pe):
                for j, (o, dst) in enumerate(turns):
                    if j >= 4:
                        pe.wait_ge(*tur.at(j - 3))
                    for t in range(4 if dst is None else NQ):
                        mm = nc.tensor.transpose(psum[:, j % 4, t * P:(t + 1) * P], z[:, t, o:o + P], ident)
                    mm.then_inc(*tu.one())
                for t in range(NQ):
                    for g_ in range(4):
                        v0 = 256 + (g_ // 2) * P
                        mm = nc.tensor.matmul(psum[:, 4 + t, g_ * P:(g_ + 1) * P], wsT[:, g_, :], z[:, t, v0:v0 + P],
                                              start=True, stop=True, skip_group_check=True)
                    mm.then_inc(*gm.one())

            @block.scalar
            def _(act):
                for j, (o, dst) in enumerate(turns):
                    act.wait_ge(*tu.at(j + 1))
                    ps = psum[:, j % 4, :]
                    if dst is not None:
                        ins = nc.scalar.activation(TT[:, dst, 0:NQ * P], ps[:, 0:NQ * P], ACT.Copy)
                    elif o == 1024:
                        for g_ in range(2):
                            ins = nc.scalar.activation(TT[64 * g_:64 * g_ + 64, 4 + g_, :], ps[64 * g_:64 * g_ + 64, :], ACT.Copy)
                    else:
                        for g_ in range(4):
                            ins = nc.scalar.activation(TT[32 * g_:32 * g_ + 32, 8 + 4 * (j - 7) + g_, :],
                                                       ps[32 * g_:32 * g_ + 32, :], ACT.Copy)
                    ins.then_inc(*tur.one())

            @block.vector
            def _(dve):
                for t in range(NQ):
                    dve.wait_ge(*gm.at(t + 1))
                    for g_ in range(4):
                        o = g_ * P + 64 * (g_ % 2)
                        nc.vector.scalar_tensor_tensor(z[:, t, g_ * 64:(g_ + 1) * 64], psum[:, 4 + t, o:o + 64],
                                                       pr(f"a_bs{i}", g_), z[:, t, g_ * 64:(g_ + 1) * 64], ALU.add, ALU.mult)

        units = [("B", t, h) for t in range(NQ) for h in range(8)] + [("C", t, h) for t in range(NQ) for h in range(4)]
        U = len(units)
        Eb = [core.norm_rt[:, 0:1024], core.norm_rt[:, 1024:2048], r2[:, 0:1024]]
        Eb = [e.rearrange("p (m k) -> p m k", m=2) for e in Eb]
        ETb = [r2[:, 1024:1536], r2[:, 1536:2048]]
        scr, mxr, exr, pdr, tp, tpr, ov, ovr = (sig(n) for n in (
            "at_scores_ready", "at_max_ready", "at_exp_ready", "at_probs_ready", "at_turned", "at_turned_read",
            "at_out_ready", "at_out_read"))

        def span(u):
            return (0, 512) if units[u][1] < 2 else (S, S)

        def scalars(u):
            return small[:, 10 * (u % 6):10 * (u % 6) + 10]

        with core.phase() as block:

            @block.tensor
            def _(pe):
                def scores(u):
                    kind, t, h = units[u]
                    k0, nk = span(u)
                    if u >= 2:
                        pe.wait_ge(*exr.at(u - 1))
                    for m in range(1 if kind == "B" else 2):
                        jq, jk = (h % 4, 4 + h // 4) if kind == "B" else (6 + h // 2, 8 + 2 * h + m)
                        mm = nc.tensor.matmul(psum[:, 2 * (u % 2) + m, 0:nk], TT[:, jq, t * P:(t + 1) * P],
                                              TT[:, jk, k0:k0 + nk], start=True, stop=True)
                    mm.then_inc(*scr.one())

                def turn(u):
                    k0, nk = span(u)
                    pe.wait_ge(*pdr.at(u + 1))
                    if u >= 2:
                        pe.wait_ge(*tpr.at(u - 1))
                    for kt in range(nk // P):
                        mm = nc.tensor.transpose(psum[:, 4 + u % 2, kt * P:(kt + 1) * P], Eb[u % 3][:, 0, kt * P:(kt + 1) * P], ident)
                    mm.then_inc(*tp.one())

                def values(u):
                    kind, t, h = units[u]
                    k0, nk = span(u)
                    o = 1152 if kind == "B" else 1792 + P * (h // 2)
                    pe.wait_ge(*tpr.at(u + 1))
                    if u >= 2:
                        pe.wait_ge(*ovr.at(u - 1))
                    for kt in range(nk // P):
                        mm = nc.tensor.matmul(psum[:, 6 + u % 2, 0:P], ETb[u % 2][:, kt * P:(kt + 1) * P],
                                              z[:, k0 // P + kt, o:o + P], start=(kt == 0), stop=(kt == nk // P - 1))
                    mm.then_inc(*ov.one())

                for u in range(U + 4):
                    if u < U:
                        scores(u)
                    if 2 <= u < U + 2:
                        turn(u - 2)
                    if u >= 4:
                        values(u - 4)

            @block.scalar
            def _(act):
                link = linker(act, sig("act_chain"))

                def exps(u):
                    kind, t, h = units[u]
                    _, nk = span(u)
                    c, e = scalars(u), Eb[u % 3]
                    act.wait_ge(*mxr.at(u + 1))
                    if u >= 3:
                        act.wait_ge(*tp.at(u - 2))
                    if kind == "B":
                        nc.scalar.activation(c[:, 3:4], pr(f"sink{i}", h), ACT.Exp, bias=c[:, 2:3])
                        link(nc.scalar.activation(e[:, 0, 0:nk], e[:, 1, 0:nk], ACT.Exp, bias=c[:, 2:3], accum_out=c[:, 4:5]))
                    else:
                        for m in range(2):
                            ins = nc.scalar.activation(e[:, m, 0:nk], psum[:, 2 * (u % 2) + m, 0:nk], ACT.Exp,
                                                       bias=c[:, 2 + m:3 + m], scale=32 ** -0.5, accum_out=c[:, 4 + m:5 + m])
                        link(ins)
                    act.sem_inc(*exr.one())

                def read_turned(u):
                    _, nk = span(u)
                    act.wait_ge(*tp.at(u + 1))
                    if u >= 2:
                        act.wait_ge(*ov.at(u - 1))
                    nc.scalar.activation(ETb[u % 2][:, 0:nk], psum[:, 4 + u % 2, 0:nk], ACT.Copy).then_inc(*tpr.one())

                for u in range(U + 3):
                    if u < U:
                        exps(u)
                    if u >= 3:
                        read_turned(u - 3)

            @block.vector
            def _(dve):
                link = linker(dve, sig("dve_chain"))

                def maxima(u):
                    kind, t, h = units[u]
                    _, nk = span(u)
                    c = scalars(u)
                    dve.wait_ge(*scr.at(u + 1))
                    if kind == "B":
                        if u >= 3:
                            dve.wait_ge(*tp.at(u - 2))
                        so, ps = Eb[u % 3][:, 1, 0:nk], psum[:, 2 * (u % 2), 0:nk]
                        if t < 2:
                            link(nc.vector.scalar_tensor_tensor(so, ps, 0.125, cn("window", t * BANK, BANK), ALU.mult, ALU.add))
                        else:
                            link(nc.vector.tensor_scalar(so, ps, 0.125, None, ALU.mult))
                        link(nc.vector.tensor_reduce(c[:, 0:1], so, AX.X, ALU.max))
                        link(nc.vector.tensor_scalar(c[:, 2:3], c[:, 0:1], pr(f"sink{i}", h), -1.0, ALU.max, ALU.mult))
                    else:
                        link(nc.vector.tensor_reduce(c[:, 0:2], psum[:, 2 * (u % 2):2 * (u % 2) + 2, 0:nk], AX.X, ALU.max))
                        link(nc.vector.tensor_scalar(c[:, 2:4], c[:, 0:2], -(32 ** -0.5), None, ALU.mult))
                    dve.sem_inc(*mxr.one())

                def weigh(u):
                    kind, t, h = units[u]
                    _, nk = span(u)
                    c, e = scalars(u), Eb[u % 3]
                    dve.wait_ge(*exr.at(u + 1))
                    if kind == "B":
                        link(nc.vector.tensor_tensor(c[:, 6:7], c[:, 3:4], c[:, 4:5], ALU.add))
                        link(nc.vector.reciprocal(c[:, 7:8], c[:, 6:7]))
                    else:
                        link(nc.vector.reciprocal(c[:, 6:8], c[:, 4:6]))
                        nc.vector.tensor_scalar(e[:, 0, 0:nk], e[:, 0, 0:nk], c[:, 6:7], None, ALU.mult)
                        link(nc.vector.tensor_scalar(c[:, 8:9], c[:, 7:8], lamc[:, 2:3], None, ALU.mult))
                        link(nc.vector.scalar_tensor_tensor(e[:, 0, 0:nk], e[:, 1, 0:nk], c[:, 8:9], e[:, 0, 0:nk],
                                                            ALU.mult, ALU.add))
                    dve.sem_inc(*pdr.one())

                def result(u):
                    kind, t, h = units[u]
                    c = scalars(u)
                    dve.wait_ge(*ov.at(u + 1))
                    if kind == "B":
                        ps = psum[:, 6 + u % 2, 64 * (h // 4):64 * (h // 4) + 64]
                        link(nc.vector.tensor_scalar(z[:, t, 512 + 64 * h:576 + 64 * h], ps, c[:, 7:8], None, ALU.mult))
                    else:
                        ps = psum[:, 6 + u % 2, 64 * (h % 2):64 * (h % 2) + 64]
                        link(nc.vector.tensor_copy(z[:, t, 1280 + 64 * h:1344 + 64 * h], ps))
                    dve.sem_inc(*ovr.one())

                for u in range(U + 4):
                    if u < U:
                        maxima(u)
                    if 1 <= u <= U:
                        weigh(u - 1)
                    if u >= 4:
                        result(u - 4)

        ns = sig("subln_steps")
        with core.phase() as block:

            @block.scalar
            def _(act):
                act.wait_ge(*ns.at(1))
                nc.scalar.activation(small[:, 0:4 * NQ], small[:, 0:4 * NQ], ACT.Sqrt, scale=1.0 / 64, bias=core.eps[:, 0:1])\
                    .then_inc(*ns.one())

            @block.vector
            def _(dve):
                link = linker(dve, sig("dve_chain"))
                cc = z[:, 0:NQ, 1280:1536]
                s3 = core.norm_rt[:, 0:NQ * 256].rearrange("p (t c) -> p t c", t=NQ)
                link(nc.vector.tensor_tensor(s3, cc, cc, ALU.mult))
                link(nc.vector.tensor_reduce(small[:, 0:4 * NQ], core.norm_rt[:, 0:NQ * 256].rearrange("p (g c) -> p g c", c=64),
                                             AX.X, ALU.add))
                dve.sem_inc(*ns.one())
                dve.wait_ge(*ns.at(2))
                link(nc.vector.reciprocal(small[:, 0:4 * NQ], small[:, 0:4 * NQ]))
                link(nc.vector.tensor_scalar(small[:, 0:4 * NQ], small[:, 0:4 * NQ], 1.0 - lam_init, None, ALU.mult))
                for t in range(NQ):
                    c3 = z[:, t, 1280:1536].rearrange("p (h c) -> p h c", h=4)
                    link(nc.vector.tensor_tensor(c3, c3, small[:, 4 * t:4 * t + 4].unsqueeze(2).broadcast_to([P, 4, 64]), ALU.mult))
                    link(nc.vector.tensor_tensor(c3, c3, pr(f"subln{i}", 0, 64).unsqueeze(1).broadcast_to([P, 4, 64]), ALU.mult))

        ct, ctr = sig("cat_turned"), sig("cat_read")
        T = NQ * P
        with core.phase() as block:

            @block.tensor
            def _(pe):
                for j in range(DT):
                    for t in range(NQ):
                        mm = nc.tensor.transpose(psum[:, j, t * P:(t + 1) * P], z[:, t, cat_at[j]:cat_at[j] + P], ident)
                    mm.then_inc(*ct.one())

            @block.scalar
            def _(act):
                for j in range(DT):
                    act.wait_ge(*ct.at(j + 1))
                    nc.scalar.activation(H[0][:, j, 0:T], psum[:, j, 0:T], ACT.Copy).then_inc(*ctr.one())

            @block.vector
            def _(dve):
                for j in range(DT):
                    dve.wait_ge(*ctr.at(j + 1))
                    nc.vector.tensor_tensor(H[1][:, j, 0:T], psum[:, j, 0:T], H[0][:, j, 0:T].bitcast(F32), ALU.subtract)

    def residual(part):
        def f(dve, link, n_, ps):
            for s_ in range(T // S):
                ins = nc.vector.scalar_tensor_tensor(X[:, n_, s_ * S:(s_ + 1) * S], ps[:, s_ * S:(s_ + 1) * S],
                                                     adaM[:, part * DT + n_, s_:s_ + 1], X[:, n_, s_ * S:(s_ + 1) * S],
                                                     ALU.mult, ALU.add)
                if s_ < T // S - 1:
                    link(ins)
            return ins
        return f

    project(core, H, T, 4, on_dve=residual(2), side=side)
    feed_forward(core, f"2_{i}", modulated(1, T), X, H, T, lambda k, t: pr(f"cw{i}", k * 44 + t), lambda t: pr(f"cb{i}", t), 1, residual(5), side)


def constants():
    con = {}
    con["ident"] = np.eye(P, dtype=np.float32)
    s, t = np.meshgrid(np.arange(P), np.arange(P), indexing="ij")
    con["causal"] = (s <= t).astype(np.float32)
    win = np.zeros((P, 2, BANK), np.float32)
    for qt in range(2):
        qpos, kpos = qt * P + np.arange(P)[:, None], np.arange(S)[None, :]
        win[:, qt, 0:S] = np.where(np.abs(qpos - kpos) <= P, 0.0, -1e30)
    con["window"] = win.reshape(P, -1)
    for name, w in (("b", 64), ("c", 32)):
        nf = w // 4
        row, col = np.repeat(np.arange(S // 64), 64), np.tile(np.arange(64), S // 64)
        inv = (np.float32(10000.0) ** (-np.arange(nf, dtype=np.float32) / np.float32(nf))).astype(np.float32)
        ang = np.stack([row[:, None].astype(np.float32) * inv, col[:, None].astype(np.float32) * inv], axis=1)
        cos, sin = np.cos(ang).astype(np.float32), np.sin(ang).astype(np.float32)
        cos2 = np.stack([cos, cos], axis=2).reshape(2, P, w)
        sin2 = np.stack([-sin, sin], axis=2).reshape(2, P, w)
        con["cos_" + name] = cos2.transpose(1, 0, 2).reshape(P, -1)
        con["sin_" + name] = sin2.transpose(1, 0, 2).reshape(P, -1)
    lev = np.zeros((P, len(LEVELS) + 1, P), np.float32)
    for n, L in enumerate(LEVELS):
        lev[:, n] = ((s // L) % 2 == 0) & (t // L == s // L + 1)
    lev[:, -1] = s == t
    return np.concatenate([con[n] for n, _ in CONS], axis=1), lev.reshape(P, -1)


def columns(v):
    v = np.asarray(v)
    return v.reshape(-1, P).T


def units_of(w, cols=UNIT):
    w = np.asarray(w)
    w = w.reshape(-1, w.shape[-2], w.shape[-1])
    L, K, N = w.shape
    w = w.reshape(L, K // P, P, N // cols, cols).transpose(0, 3, 2, 1, 4)
    return np.ascontiguousarray(w).reshape(L * (N // cols), P, -1)


def paired(w):
    w = np.asarray(w)
    w = w.reshape(-1, D, 2, FFT, P).transpose(0, 1, 3, 2, 4)
    return units_of(np.ascontiguousarray(w).reshape(-1, D, 2 * FF))


def halved(w):
    w = np.asarray(w).reshape(-1, 2, FFH, P, DT, P).transpose(0, 4, 1, 3, 2, 5)
    return np.ascontiguousarray(w).reshape(-1, P, FFH * P)


def lay_out(i):
    w_in = np.asarray(i["w_in"])[0]
    big = np.concatenate([w_in[:, 0:6144], w_in[:, 6152:7176], w_in[:, 7176:10248], w_in[:, 10264:]], axis=1)
    gap = np.zeros((D, 28), np.float32)
    small_w = np.concatenate([w_in[:, 6144:6148], gap, w_in[:, 6148:6152], gap, w_in[:, 10248:10264]], axis=1)
    pad = lambda v: np.concatenate([np.asarray(v).reshape(-1), np.zeros(P - np.asarray(v).size, np.float32)])[:, None]
    rows = lambda v: np.broadcast_to(np.asarray(v).reshape(1, -1), (P, np.asarray(v).size))
    taps = lambda w: np.concatenate([columns(r) for r in np.asarray(w)], axis=1)
    gb = np.asarray(i["ml_gate_b"])[0]
    p = {
        "norm1": columns(i["norm1_g"][0]), "hg_norm": columns(i["hg_norm_g"][0]), "ml_w": taps(i["ml_conv_w"][0]),
        "ml_b": columns(i["ml_conv_b"][0]), "ml_norm": columns(i["ml_norm_g"][0]), "mb_w": taps(i["mb_conv_w"][0]),
        "mb_b": columns(i["mb_conv_b"][0]), "mb_norm": columns(i["mb_norm_g"][0]), "norm2": columns(i["norm2_g"][0]),
        "ff_w": taps(i["ffn_conv_w"][0]), "ff_b": columns(i["ffn_conv_b"][0]), "final": columns(i["final_g"]),
        "mb_d": columns(np.repeat(np.asarray(i["mb_d"])[0], MB_P)),
        "gate_i": pad(gb[:ML_H]), "gate_f": pad(gb[ML_H:]), "dt_bias": pad(i["mb_dt_bias"]), "a_log": pad(i["mb_a_log"]),
        "w_gates": small_w.reshape(DT, P, 80).transpose(1, 0, 2).reshape(P, -1),
        "cond": np.stack([columns(i["c_2"][0]), columns(i["c_ctx_2"])], axis=2).reshape(P, -1),
    }
    for n in range(LAYERS):
        bq, bk = np.asarray(i["b_qnorm_2"])[n], np.asarray(i["b_knorm_2"])[n]
        cq, ck = np.asarray(i["c_qnorm_2"])[n], np.asarray(i["c_knorm_2"])[n]
        p |= {
            f"norm1_{n}": columns(i["norm1_g_2"][n]), f"norm2_{n}": columns(i["norm2_g_2"][n]),
            f"b_ada{n}": columns(i["b_ada_2"][n]), f"cw{n}": taps(i["conv_w_2"][n][:, 0]), f"cb{n}": columns(i["conv_b_2"][n]),
            f"a_bs{n}": np.asarray(i["a_bs_2"])[n].T,
            f"gain_b{n}": rows(np.concatenate([bq, bk])),
            f"gain_c{n}": rows(np.concatenate([cq, ck])),
            f"subln{n}": rows(i["c_subln_2"][n]), f"sink{n}": rows(i["b_sink_2"][n]), f"lam{n}": rows(i["c_lam_2"][n]),
        }
    con, lev = constants()
    return {
        "x": np.asarray(i["x"])[0].T, "ctx": np.asarray(i["ctx_2"])[0].T,
        "par": np.concatenate([p[n] for n, _ in PARS], axis=1), "con": con, "levels": lev,
        "a_ws": np.asarray(i["a_ws_2"]).transpose(0, 3, 1, 2).reshape(LAYERS, P, -1),
        "w_in": units_of(big), "w_br_hg": units_of(i["w_br_hg"]), "w_br_ml": units_of(i["w_br_ml"]),
        "w_br_mb": units_of(i["w_br_mb"]), "w_out": units_of(i["w_out"]), "w_up": paired(i["w_up"]),
        "w_down": halved(i["w_down"]), "w_ada_2": units_of(i["w_ada_2"]), "w_in_2": units_of(i["w_in_2"]),
        "w_out_2": units_of(i["w_out_2"]), "w_up_2": paired(i["w_up_2"]), "w_down_2": halved(i["w_down_2"]),
    }


def kernel(**inputs):
    import concourse.bacc as bacc
    from concourse.bass_utils import run_bass_kernel_spmd

    nc = bacc.Bacc("TRN2", target_bir_lowering=False, num_devices=1)
    arrays, aps = {}, {}
    for name, v in lay_out(inputs).items():
        v = np.ascontiguousarray(v)
        arrays[f"in_{name}"] = v
        aps[name] = nc.dram_tensor(f"in_{name}", v.shape, mybir.dt.from_np(v.dtype), kind="ExternalInput").ap()
    out = nc.dram_tensor("out", (D, S), F32, kind="ExternalOutput").ap()
    build(nc, aps, out)
    r = run_bass_kernel_spmd(nc, [arrays], core_ids=[0])
    return np.ascontiguousarray(r.results[0]["out"].T).reshape(1, S, D)
```
